# Optimizing a Trainium2 kernel written in Bass

```python
import math
import jax
import jax.numpy as jnp
from jax import lax
import numpy as np

D_MODEL = 1024
BATCH = 1
SEQ = 512
DEPTH = 1

FOX_HEADS = 4
FOX_HEAD_DIM = D_MODEL // 16
RET_HEADS = 4
RET_HEAD_DIM = D_MODEL // 16
GDN_HEADS = 4
GDN_HEAD_DIM = D_MODEL // 8
FOX_WIDTH = FOX_HEADS * FOX_HEAD_DIM
RET_WIDTH = RET_HEADS * RET_HEAD_DIM
GDN_WIDTH = GDN_HEADS * GDN_HEAD_DIM
D_MIX = FOX_WIDTH + RET_WIDTH + GDN_WIDTH
Q_BLOCK = 128
RET_CHUNK = 128
GDN_CHUNK = 64
CONV_WIDTH = 4
RET_ANGLE_BASE = 10000.0
N_GROUPS = 4
EXPERTS_PER_GROUP = 8
TOP_K_EXPERTS = 2
EXPERT_FF = D_MODEL // 4
NORM_EPS = 1e-6
IN_SPLITS = (FOX_WIDTH, FOX_WIDTH, FOX_WIDTH, FOX_HEADS,
             RET_WIDTH, RET_WIDTH, RET_WIDTH, RET_WIDTH,
             GDN_WIDTH, GDN_WIDTH, GDN_WIDTH, GDN_WIDTH, GDN_HEADS, GDN_HEADS)
D_IN = sum(IN_SPLITS)

kernel_name = "hybrid_fox_retnet_gdn_hmoe"

F32 = jnp.float32

def rms_norm(x, w):
    xf = x.astype(F32)
    y = xf * lax.rsqrt(jnp.mean(xf * xf, axis=-1, keepdims=True) + NORM_EPS)
    return (y * w.astype(F32)).astype(x.dtype)

def head_rms(t):
    return t * lax.rsqrt(jnp.mean(t * t, axis=-1, keepdims=True) + NORM_EPS)

def l2_normalize(t):
    return t * lax.rsqrt(jnp.sum(t * t, axis=-1, keepdims=True) + NORM_EPS)

def split_columns(y):
    cuts = np.cumsum(IN_SPLITS)[:-1].tolist()
    return jnp.split(y, cuts, axis=-1)

def to_heads(t, n_heads):
    b, s, _ = t.shape
    return t.reshape(b, s, n_heads, -1).transpose(0, 2, 1, 3)

def merge_heads(t):
    b, h, s, d = t.shape
    return t.transpose(0, 2, 1, 3).reshape(b, s, h * d)

def rotary(t, pos):
    d = t.shape[-1]
    inv = 1.0 / (RET_ANGLE_BASE ** jnp.linspace(0.0, 1.0, d // 2, dtype=F32))
    ang = pos[:, None] * inv[None, :]
    cos, sin = jnp.cos(ang), jnp.sin(ang)
    t1, t2 = t[..., : d // 2], t[..., d // 2:]
    return jnp.concatenate([t1 * cos - t2 * sin, t1 * sin + t2 * cos], axis=-1)

def fox_attention(q, k, v, log_f):
    b, h, s, d = q.shape
    scale = d ** -0.5
    c = jnp.cumsum(log_f, axis=-1)
    nb = s // Q_BLOCK
    qb = q.reshape(b, h, nb, Q_BLOCK, d).transpose(2, 0, 1, 3, 4)
    cb = c.reshape(b, h, nb, Q_BLOCK).transpose(2, 0, 1, 3)
    kpos = jnp.arange(s)

    def one_block(args):
        q_blk, c_blk, i = args
        logits = jnp.einsum("bhqd,bhkd->bhqk", q_blk, k) * scale + c_blk[..., None] - c[..., None, :]
        qpos = i * Q_BLOCK + jnp.arange(Q_BLOCK)
        logits = jnp.where(kpos[None, :] <= qpos[:, None], logits, -jnp.inf)
        p = jax.nn.softmax(logits, axis=-1)
        return jnp.einsum("bhqk,bhkd->bhqd", p, v)

    o = lax.map(one_block, (qb, cb, jnp.arange(nb)))
    return o.transpose(1, 2, 0, 3, 4).reshape(b, h, s, d)

def retention(q, k, v):
    b, h, s, dk = q.shape
    dv = v.shape[-1]
    C = RET_CHUNK
    n = s // C
    log_g = jnp.log1p(-jnp.exp2(-5.0 - jnp.arange(h, dtype=F32)))
    idx = jnp.arange(C, dtype=F32)
    rel = idx[:, None] - idx[None, :]
    dmat = jnp.where(rel[None] >= 0, jnp.exp(jnp.maximum(rel, 0.0)[None] * log_g[:, None, None]), 0.0)
    qc = q.reshape(b, h, n, C, dk)
    kc = k.reshape(b, h, n, C, dk)
    vc = v.reshape(b, h, n, C, dv)
    scores = jnp.einsum("bhnid,bhnjd->bhnij", qc, kc) * dmat[None, :, None]
    o_intra = jnp.einsum("bhnij,bhnjv->bhniv", scores, vc)
    k_w = kc * jnp.exp((C - 1 - idx)[None, :] * log_g[:, None])[None, :, None, :, None]
    chunk_kv = jnp.einsum("bhncd,bhncv->nbhdv", k_w, vc)
    chunk_decay = jnp.exp(C * log_g)[None, :, None, None]

    def step(state, kv):
        return state * chunk_decay + kv, state

    _, s_prev = lax.scan(step, jnp.zeros((b, h, dk, dv), F32), chunk_kv)
    q_w = qc * jnp.exp((idx + 1.0)[None, :] * log_g[:, None])[None, :, None, :, None]
    o_inter = jnp.einsum("bhncd,nbhdv->bhncv", q_w, s_prev)
    return (o_intra + o_inter).reshape(b, h, s, dv)

def causal_depthwise_conv(x, w):
    kw, ch = w.shape
    return lax.conv_general_dilated(
        x, w[:, None, :].astype(x.dtype), window_strides=(1,), padding=[(kw - 1, 0)],
        dimension_numbers=("NWC", "WIO", "NWC"), feature_group_count=ch)

def gated_delta_rule(q, k, v, g, beta):
    b, h, s, dk = q.shape
    dv = v.shape[-1]
    C = GDN_CHUNK
    n = s // C
    qc = (q * dk ** -0.5).reshape(b, h, n, C, dk)
    kc = k.reshape(b, h, n, C, dk)
    vc = v.reshape(b, h, n, C, dv)
    gc = jnp.cumsum(g.reshape(b, h, n, C), axis=-1)
    bc = beta.reshape(b, h, n, C, 1)
    idx = jnp.arange(C)
    incl = idx[:, None] >= idx[None, :]
    strict = idx[:, None] > idx[None, :]
    diff = gc[..., :, None] - gc[..., None, :]
    decay = jnp.where(incl, jnp.exp(jnp.where(incl, diff, 0.0)), 0.0)
    kb = kc * bc
    lower = jnp.where(strict, jnp.einsum("bhnid,bhnjd->bhnij", kb, kc) * decay, 0.0)
    a_mat = lower + jnp.eye(C, dtype=F32)
    rhs = jnp.concatenate([vc * bc, kb * jnp.exp(gc)[..., None]], axis=-1)
    sol = lax.linalg.triangular_solve(a_mat, rhs, left_side=True, lower=True, unit_diagonal=True)
    u0, w = sol[..., :dv], sol[..., dv:]
    attn = jnp.where(incl, jnp.einsum("bhnid,bhnjd->bhnij", qc, kc) * decay, 0.0)
    g_last = gc[..., -1]
    q_g = qc * jnp.exp(gc)[..., None]
    k_tail = kc * jnp.exp(g_last[..., None] - gc)[..., None]
    xs = (jnp.moveaxis(u0, 2, 0), jnp.moveaxis(w, 2, 0), jnp.moveaxis(attn, 2, 0),
          jnp.moveaxis(q_g, 2, 0), jnp.moveaxis(k_tail, 2, 0), jnp.moveaxis(g_last, 2, 0))

    def step(state, inp):
        u0_i, w_i, attn_i, q_i, k_i, gl_i = inp
        u = u0_i - jnp.einsum("bhcd,bhdv->bhcv", w_i, state)
        o = jnp.einsum("bhcd,bhdv->bhcv", q_i, state) + jnp.einsum("bhij,bhjv->bhiv", attn_i, u)
        state = state * jnp.exp(gl_i)[..., None, None] + jnp.einsum("bhcd,bhcv->bhdv", k_i, u)
        return state, o

    _, o = lax.scan(step, jnp.zeros((b, h, dk, dv), F32), xs)
    return jnp.moveaxis(o, 0, 2).reshape(b, h, s, dv)

def hybrid_mixer(h, w_in, fox_forget_bias, gdn_conv_w, gdn_a_log, gdn_dt_bias, gdn_norm_w, w_out):
    b, s, _ = h.shape
    y = jnp.einsum("bsd,dn->bsn", h, w_in)
    fq, fk, fv, ff, rq, rk, rv, rg, gq, gk, gv, gz, ga, gb = split_columns(y)

    log_f = jax.nn.log_sigmoid(ff.astype(F32) + fox_forget_bias.astype(F32)).transpose(0, 2, 1)
    o_fox = fox_attention(to_heads(fq, FOX_HEADS).astype(F32), to_heads(fk, FOX_HEADS).astype(F32),
                          to_heads(fv, FOX_HEADS).astype(F32), log_f)
    o_fox = merge_heads(o_fox)

    pos = jnp.arange(s, dtype=F32)
    rq_h = rotary(to_heads(rq, RET_HEADS).astype(F32), pos)
    rk_h = rotary(to_heads(rk, RET_HEADS).astype(F32), pos) * RET_HEAD_DIM ** -0.5
    o_ret = retention(rq_h, rk_h, to_heads(rv, RET_HEADS).astype(F32))
    o_ret = merge_heads(head_rms(o_ret)) * jax.nn.silu(rg.astype(F32))

    qkv = jnp.concatenate([gq, gk, gv], axis=-1).astype(F32)
    qkv = jax.nn.silu(causal_depthwise_conv(qkv, gdn_conv_w.astype(F32)))
    cq, ck, cv = jnp.split(qkv, [GDN_WIDTH, 2 * GDN_WIDTH], axis=-1)
    log_a = -jnp.exp(gdn_a_log.astype(F32)) * jax.nn.softplus(ga.astype(F32) + gdn_dt_bias.astype(F32))
    beta = jax.nn.sigmoid(gb.astype(F32))
    o_gdn = gated_delta_rule(l2_normalize(to_heads(cq, GDN_HEADS)), l2_normalize(to_heads(ck, GDN_HEADS)),
                             to_heads(cv, GDN_HEADS), log_a.transpose(0, 2, 1), beta.transpose(0, 2, 1))
    o_gdn = merge_heads(head_rms(o_gdn) * gdn_norm_w.astype(F32)) * jax.nn.silu(gz.astype(F32))

    mix = jnp.concatenate([o_fox, o_ret, o_gdn], axis=-1).astype(h.dtype)
    return jnp.einsum("bsm,md->bsd", mix, w_out).astype(h.dtype)

def hier_moe(h, rg_w, rg_b, re_w, re_b, w1, w3, w2):
    b, s, d = h.shape
    t = h.reshape(b * s, d)
    n_exp = N_GROUPS * EXPERTS_PER_GROUP
    grp_prob = jax.nn.softmax(jnp.einsum("td,dg->tg", t, rg_w).astype(F32) + rg_b.astype(F32), axis=-1)
    grp_p, grp_idx = lax.top_k(grp_prob, 1)
    exp_logits = jnp.einsum("td,dn->tn", t, re_w).astype(F32).reshape(-1, N_GROUPS, EXPERTS_PER_GROUP)
    exp_logits = exp_logits + re_b.astype(F32)
    sel = jnp.take_along_axis(exp_logits, grp_idx[:, :, None], axis=1)[:, 0]
    exp_p, exp_idx = lax.top_k(jax.nn.softmax(sel, axis=-1), TOP_K_EXPERTS)
    gate_w = grp_p * exp_p / jnp.sum(exp_p, axis=-1, keepdims=True)
    flat = grp_idx * EXPERTS_PER_GROUP + exp_idx
    gates = jnp.einsum("tk,tkn->tn", gate_w, jax.nn.one_hot(flat, n_exp, dtype=F32))
    gates = gates.reshape(-1, N_GROUPS, EXPERTS_PER_GROUP)
    out = jnp.zeros((t.shape[0], d), F32)
    for gi in range(N_GROUPS):
        a = jnp.einsum("td,edf->tef", t, w1[gi]).astype(F32)
        u = jnp.einsum("td,edf->tef", t, w3[gi]).astype(F32)
        hid = jax.nn.silu(a) * u * gates[:, gi, :, None]
        out = out + jnp.einsum("tef,efd->td", hid, w2[gi].astype(F32))
    return out.reshape(b, s, d).astype(h.dtype)

def setup_inputs(seed: int = 0) -> dict:
    key = jax.random.key(seed)
    ks = jax.random.split(key, 20)

    def nrm(k, shape, scale):
        return scale * jax.random.normal(k, shape, F32)

    x = jax.random.normal(ks[0], (BATCH, SEQ, D_MODEL), F32)
    norm1_w = 1.0 + nrm(ks[1], (DEPTH, D_MODEL), 0.02)
    w_in = nrm(ks[2], (DEPTH, D_MODEL, D_IN), D_MODEL ** -0.5)
    fox_forget_bias = jnp.linspace(1.0, 5.0, FOX_HEADS, dtype=F32)[None, :] + nrm(ks[3], (DEPTH, FOX_HEADS), 0.1)
    gdn_conv_w = nrm(ks[4], (DEPTH, CONV_WIDTH, 3 * GDN_WIDTH), CONV_WIDTH ** -0.5)
    gdn_a_log = jnp.log(jax.random.uniform(ks[5], (DEPTH, GDN_HEADS), F32, 1.0, 16.0))
    dt = jnp.exp(jax.random.uniform(ks[6], (DEPTH, GDN_HEADS), F32, math.log(1e-3), math.log(0.1)))
    gdn_dt_bias = dt + jnp.log(-jnp.expm1(-dt))
    gdn_norm_w = 1.0 + nrm(ks[7], (DEPTH, GDN_HEAD_DIM), 0.02)
    w_out = nrm(ks[8], (DEPTH, D_MIX, D_MODEL), D_MIX ** -0.5)
    norm2_w = 1.0 + nrm(ks[9], (DEPTH, D_MODEL), 0.02)
    router_group_w = nrm(ks[10], (DEPTH, D_MODEL, N_GROUPS), D_MODEL ** -0.5)
    router_group_b = nrm(ks[11], (DEPTH, N_GROUPS), 0.01)
    router_expert_w = nrm(ks[12], (DEPTH, D_MODEL, N_GROUPS * EXPERTS_PER_GROUP), D_MODEL ** -0.5)
    router_expert_b = nrm(ks[13], (DEPTH, N_GROUPS, EXPERTS_PER_GROUP), 0.01)
    expert_w1 = nrm(ks[14], (DEPTH, N_GROUPS, EXPERTS_PER_GROUP, D_MODEL, EXPERT_FF), D_MODEL ** -0.5)
    expert_w3 = nrm(ks[15], (DEPTH, N_GROUPS, EXPERTS_PER_GROUP, D_MODEL, EXPERT_FF), D_MODEL ** -0.5)
    expert_w2 = nrm(ks[16], (DEPTH, N_GROUPS, EXPERTS_PER_GROUP, EXPERT_FF, D_MODEL), EXPERT_FF ** -0.5)
    final_norm_w = 1.0 + nrm(ks[17], (D_MODEL,), 0.02)
    return {"x": x, "norm1_w": norm1_w, "w_in": w_in, "fox_forget_bias": fox_forget_bias,
            "gdn_conv_w": gdn_conv_w, "gdn_a_log": gdn_a_log, "gdn_dt_bias": gdn_dt_bias,
            "gdn_norm_w": gdn_norm_w, "w_out": w_out, "norm2_w": norm2_w,
            "router_group_w": router_group_w, "router_group_b": router_group_b,
            "router_expert_w": router_expert_w, "router_expert_b": router_expert_b,
            "expert_w1": expert_w1, "expert_w3": expert_w3, "expert_w2": expert_w2,
            "final_norm_w": final_norm_w}

def reference(x, norm1_w, w_in, fox_forget_bias, gdn_conv_w, gdn_a_log, gdn_dt_bias, gdn_norm_w,
              w_out, norm2_w, router_group_w, router_group_b, router_expert_w, router_expert_b,
              expert_w1, expert_w3, expert_w2, final_norm_w):
    for l in range(DEPTH):
        h = rms_norm(x, norm1_w[l])
        x = x + hybrid_mixer(h, w_in[l], fox_forget_bias[l], gdn_conv_w[l], gdn_a_log[l],
                             gdn_dt_bias[l], gdn_norm_w[l], w_out[l])
        h = rms_norm(x, norm2_w[l])
        x = x + hier_moe(h, router_group_w[l], router_group_b[l], router_expert_w[l], router_expert_b[l],
                         expert_w1[l], expert_w3[l], expert_w2[l])
    return rms_norm(x, final_norm_w)


_drawn_inputs = setup_inputs


def setup_inputs(seed=0):
    import zlib

    import numpy as np

    out = dict(_drawn_inputs(seed))
    spreads = {}
    factors = {'gdn_norm_w': 3.372,
     'router_group_b': 15.118,
     'router_expert_b': 13.492,
     'final_norm_w': 8.255,
     'norm2_w': 3.113}
    for name, (base, spread) in spreads.items():
        noise = np.random.default_rng([zlib.crc32(name.encode()), seed]).standard_normal(out[name].shape)
        drawn = base * np.exp(spread * noise) if base else spread * noise
        out[name] = jnp.asarray(drawn.astype(out[name].dtype))
    for name, factor in factors.items():
        out[name] = (out[name] * factor).astype(out[name].dtype)
    return out
```

```python
from contextlib import ExitStack
import math

import numpy as np

import concourse.bass as bass
from concourse import mybir

F32 = mybir.dt.float32
F32R = mybir.dt.float32r
I32 = mybir.dt.int32
U32 = mybir.dt.uint32
ACT = mybir.ActivationFunctionType
ALU = mybir.AluOpType
AX_X = mybir.AxisListType.X

P = 128
D = 1024
S = 512
T = S // P
KC = D // P
HK = KC // 2
NH = 4
HD = 64
GW = NH * P
EPS = 1e-6
NG = 4
EG = 8
NE = NG * EG
FF = 256
CAP = 64
PAIRS = NE // 2
NEG = -1e30
LEVELS = 6

FQ, FK, FV, FFG = 0, 256, 512, 768
RQ, RK, RV, RG = 772, 1028, 1284, 1540
GQ, GK, GV, GZ, GA, GB = 1796, 2308, 2820, 3332, 3844, 3848
WMAX = 260

GROUPS = [("n", "fv", FV, 260), ("n", "zb", GZ + 260, 260), ("n", "za", GZ, 260), ("n", "rg", RG, 256),
          ("t", "v0", GV, 256), ("t", "v1", GV + 256, 256), ("t", "k0", GK, 256), ("t", "k1", GK + 256, 256),
          ("t", "q0", GQ, 256), ("t", "q1", GQ + 256, 256),
          ("n", "rq", RQ, 256), ("n", "rk", RK, 256), ("n", "rv", RV, 256),
          ("t", "fq", FQ, 256), ("t", "fk", FK, 256)]
NIN = len(GROUPS)
NOUT = 4
GR_IN = 2 * NIN
GR = GR_IN + 2 * NOUT

AFTER = {g: [] for g in range(GR_IN)}
for _i in range(NIN):
    AFTER[2 * _i + 1].append(("evac", _i))
AFTER[7].append(("gates",))
AFTER[9].append(("gcum",))
AFTER[10] += [("vt", 0), ("vt", 1), ("cB",)]
AFTER[12] += [("vt", 2), ("vt", 3)]
AFTER[20].append(("ss", 0))
AFTER[21].append(("ss", 1))
AFTER[22] += [("kt",), ("prep", 0), ("prep", 1), ("xt", 0)]
for _i in range(LEVELS):
    AFTER[23 + _i].append(("lv", 0, _i))
AFTER[29] += [("fin", 0), ("prep", 2), ("prep", 3), ("xt", 1)] + [("lv", 1, _i) for _i in range(LEVELS)] + [("fin", 1)]

FOX = [(u // T, u % T) for u in range(NH * T)]
KSTEPS = len(FOX) + 2
PW = [S - j * P for j in range(T)]
POFF = [sum(PW[:j]) for j in range(T)]


def tensor_orders():
    a, b = [("xT", c) for c in range(KC)], []
    for g in range(GR_IN):
        if g % 2 == 0:
            kind = GROUPS[g // 2][0]
            a += [("y", g // 2, n) for n in range(T if kind == "n" else 2)]
        for task in AFTER[g]:
            if task[0] == "vt":
                b.append(task)
            elif task[0] == "gcum":
                b.append(task)
            elif task[0] == "cB":
                b += [("cB", h) for h in range(NH)]
            elif task[0] == "ss":
                b += [("ss", NH * task[1] + h) for h in range(NH)]
            elif task[0] == "kt":
                b += [("kt", h) for h in range(NH)]
            elif task[0] == "prep":
                b += [(n, task[1]) for n in ("gcB", "bB", "KK", "QK")]
            elif task[0] == "xt":
                b += [("XT", 2 * task[1]), ("XT", 2 * task[1] + 1)]
            elif task[0] == "lv":
                _, pr, lv = task
                b += [("Y", 2 * pr, lv), ("Y", 2 * pr + 1, lv)]
                for t in (2 * pr, 2 * pr + 1):
                    if lv < LEVELS - 1:
                        b.append(("Xp", t, lv))
                    b.append(("Up", t, lv))
            elif task[0] == "fin":
                for t in (2 * task[1], 2 * task[1] + 1):
                    b += [("wT", t), ("u0", t)]
    b += [("rT", i) for i in range(4)]
    for k in range(KSTEPS):
        if k < 16:
            a.append(("fS", k))
        if 1 <= k <= 16:
            a.append(("fT", k - 1))
        if k >= 2:
            a.append(("fO", k - 2))
        if k < 16:
            n = k // 4
            if k % 4 == 0 and n > 0:
                b.append(("wS", n))
            if k % 4 == 1:
                b += [("rS", n, j) for j in range(T)]
            if k % 4 == 2:
                b.append(("o", n))
                if n < T - 1:
                    b.append(("Sp", n))
            if k % 4 == 3:
                b.append(("rO", n))
    a += [("mT", c) for c in range(KC)]
    for n in range(NOUT):
        a += [("y", NIN + n, t) for t in range(T)]
    for t in range(T):
        b += [("hT", t, 0), ("hT", t, 1), ("lg", t)]
    b += [("rank",)]
    return a, b


ORDER_A, ORDER_B = tensor_orders()
BANK = {}
for _base, _order in ((0, ORDER_A), (4, ORDER_B)):
    for _i, _name in enumerate(_order):
        BANK[_name] = (_base + _i % 4, _i // 4)

CONST = {}
_at = 0
for _name, _n in [("tri", P), ("ident", P), ("strict", P), ("negmask", P), ("nM1", P), ("nM", LEVELS * P),
                  ("dm", NH * S), ("cos", T * 32), ("sin", T * 32), ("iota", CAP), ("tok1", T), ("thr", 8),
                  ("desc", NE), ("gdesc", NG), ("eps", 1), ("eps128", 1), ("ones", P), ("rankm", P)]:
    CONST[_name] = (_at, _n)
    _at += _n
NCONST = _at


def constant_table():
    c = np.zeros((P, NCONST), np.float32)

    def put(name, v):
        a, n = CONST[name]
        c[:, a:a + n] = np.asarray(v, np.float32).reshape(P, n)

    r = np.arange(P)
    row, col = r[:, None], r[None, :]
    put("tri", row <= col)
    put("rankm", row < col)
    put("ident", row == col)
    put("strict", row < col)
    put("ones", np.ones((P, P)))
    put("negmask", np.where(col > row, NEG, 0.0))
    put("nM1", -((row % 2 == 0) & (col == row + 1)).astype(np.float32))
    lv = []
    for n in range(LEVELS):
        b = 2 << n
        lv.append(-((row // (2 * b) == col // (2 * b)) & (row % (2 * b) >= b) & (col % (2 * b) < b)).astype(np.float32))
    put("nM", np.stack(lv, 1))
    dm = []
    for h in range(NH):
        rel = np.arange(S)[None, :] - row
        dm.append(np.where(rel >= 0, np.exp(np.maximum(rel, 0) * math.log1p(-(2.0 ** (-5 - h)))), 0.0) * HD ** -0.5)
    put("dm", np.stack(dm, 1))
    lin = (np.arange(HD // 2, dtype=np.float32) / np.float32(HD // 2 - 1)).astype(np.float32)
    inv = (np.float32(1.0) / np.power(np.float32(10000.0), lin).astype(np.float32)).astype(np.float32)
    pos = (np.arange(T)[None, :] * P + row).astype(np.float32)
    ang = (pos[:, :, None] * inv[None, None, :]).astype(np.float32).astype(np.float64)
    put("cos", np.cos(ang))
    put("sin", np.sin(ang))
    put("iota", np.tile(np.arange(CAP), (P, 1)))
    put("tok1", pos + 1)
    put("thr", np.tile(np.arange(8) * CAP, (P, 1)))
    put("desc", np.tile(NE - np.arange(NE), (P, 1)))
    put("gdesc", np.tile(NG - np.arange(NG), (P, 1)))
    put("eps", np.full((P, 1), EPS))
    put("eps128", np.full((P, 1), EPS * P))
    return c


def build(nc, consts, x, n1w, w_in, foxb, convw, alog, dtb, gnw, w_out, n2w, rgw, rgb, rew, reb,
          ew1, ew3, ew2, fnw, out):
    KB = 1024
    BASE = 16512
    C0 = 0
    R1 = 17 * KB
    R2 = R1 + 32 * KB
    RM = R2 + 29 * KB
    R7 = RM + 16 * KB
    R8 = R7 + 12 * KB
    R9 = R8 + 12 * KB
    R5 = R9 + 20 * KB
    R4 = R5 + 8 * KB
    R3 = R4 + 20 * KB
    with ExitStack() as ctx:
        def at(name, shape, offset, dt=F32):
            return nc.alloc_sbuf_tensor_at(name, shape, dt, offset=BASE + offset)

        def sem(name):
            return ctx.enter_context(nc.semaphore(name))

        arena = ctx.enter_context(nc.sbuf_tensor("arena", [P, (229344 - BASE) // 4 - 16], F32))
        CT = at("CT", [P, NCONST], C0)

        def const(name, *dims):
            a, n = CONST[name]
            v = CT[:, a:a + n]
            return v if not dims else v.rearrange(dims[0], **dims[1])

        tri, ident, strict, negmask = const("tri"), const("ident"), const("strict"), const("negmask")
        ones, eps = const("ones"), const("eps")
        nM = const("nM", "p (l n) -> p l n", dict(l=LEVELS))
        dm = const("dm", "p (h n) -> p h n", dict(h=NH))
        cosT = const("cos", "p (t n) -> p t n", dict(t=T))
        sinT = const("sin", "p (t n) -> p t n", dict(t=T))

        q0 = -(-NCONST * 4 // 32) * 32
        PN1 = at("PN1", [P, KC], q0)
        PDT = at("PDT", [P, 4], q0 + 32)
        PAL = at("PAL", [P, 4], q0 + 64)
        PFB = at("PFB", [P, 4], q0 + 96)
        PRB = at("PRB", [P, NG + NE], q0 + 128)
        PCW = at("PCW", [P, 12, 4], q0 + 288)
        PGN = at("PGN", [P, P], q0 + 480)
        assert q0 + 480 + 512 <= R1
        hHi = at("hHi", [P, KC, S], R1, F32R)
        hLo = at("hLo", [P, KC, S], R1 + 16 * KB, F32R)
        gsz = HK * WMAX * 4
        raw = [at(f"raw{i}", [P, HK, WMAX], R2 + i * gsz) for i in range(3)]
        whi = [at(f"whi{i}", [P, HK, WMAX], R2 + (3 + i) * gsz, F32R) for i in range(2)]
        wlo = [at(f"wlo{i}", [P, HK, WMAX], R2 + (5 + i) * gsz, F32R) for i in range(2)]
        assert 7 * gsz <= 29 * KB
        X0 = at("X0", [P, T, D], RM)
        mix = at("mix", [P, T, D], RM)
        rq = at("rq", [P, T, 256], R7)
        rk = at("rk", [P, T, 256], R7 + 4 * KB)
        rv = at("rv", [P, T, 256], R7 + 8 * KB)
        oret = at("oret", [P, T, 256], R7)
        osq = at("osq", [P, T, 256], R7 + 4 * KB)
        fqT = at("fqT", [P, 2, S], R8)
        fkT = at("fkT", [P, 2, S], R8 + 4 * KB)
        fv = at("fv", [P, T, 256], R8 + 8 * KB)
        cB8 = at("cB8", [P, NH, S], R9)
        junk = at("junk", [P, D], R9 + 8 * KB)
        cacc = [at(f"cacc{i}", [P, S], R9 + (8 + 2 * i) * KB) for i in range(2)]
        vS = [at(f"vS{i}", [P, S], R9 + (12 + 2 * i) * KB) for i in range(2)]
        nrm = [at(f"nrm{i}", [P, S], R9 + (8 + 2 * i) * KB) for i in range(4)]
        rtmp = [at(f"rtmp{i}", [P, T, NH, 32], R9 + (8 + 2 * i) * KB) for i in range(4)]
        Sx = [at(f"Sx{i}", [P, S], R9 + (8 + 2 * i) * KB) for i in range(2)]
        Pf = [at(f"Pf{i}", [P, S], R9 + (12 + 2 * i) * KB) for i in range(2)]
        PT = [at(f"PT{i}", [P, T, P], R9 + (16 + 2 * i) * KB) for i in range(2)]
        small = at("small", [P, 1024], R9 + 16 * KB)
        attnT = at("attnT", [P, T, NH, P], R5)
        def pair(name, slot):
            return [at(f"{name}{i}", [P, NH, P], R4 + (slot * 2 + i) * 2 * KB) for i in range(2)]
        Nm, Xm, Um, Ym, Dm = (pair(n, i) for i, n in enumerate(("Nm", "Xm", "Um", "Ym", "Dm")))
        rqT = at("rqT", [P, 2, S], R4)
        rkT = at("rkT", [P, 2, S], R4 + 4 * KB)
        retP = at("retP", [P, sum(PW)], R4 + 8 * KB)
        St = at("St", [P, NH, P], R4 + 18 * KB)
        qT = at("qT", [P, NH, S], R3)
        kT = at("kT", [P, NH, S], R3 + 8 * KB)
        vb = at("vb", [P, T, NH, P], R3 + 16 * KB)
        kbg = at("kbg", [P, T, NH, P], R3 + 24 * KB)
        ktail = at("ktail", [P, T, NH, P], R3 + 32 * KB)
        gsq = at("gsq", [P, T, NH, P], R3)
        sm0 = -(-(R2 + 7 * gsz) // 32) * 32
        keep = at("keep", [P, 136], sm0)
        assert sm0 + 544 <= RM
        ssx, rx = keep[:, 0:4], keep[:, 4:8]
        egl = keep[:, 8:24]
        mx, nmx, rs, ri = keep[:, 24:40], keep[:, 40:56], keep[:, 56:72], keep[:, 72:88]
        ssn, rn, ssx4 = keep[:, 88:104], keep[:, 104:120], keep[:, 120:136]
        def sml(a, n):
            return small[:, a:a + n]
        GAB = sml(0, 32).rearrange("p (t n) -> p t n", t=T)
        FFT = sml(32, 16).rearrange("p (t n) -> p t n", t=T)
        z8 = sml(48, 32).rearrange("p (t n) -> p t n", t=T)
        az, e8, dd, sv, qv, hv = (sml(80 + 32 * i, 32).rearrange("p (t n) -> p t n", t=T) for i in range(6))
        eb, beta, gg, ea = sml(272, 16), sml(288, 16), sml(304, 16), sml(320, 4)
        cum = sml(336, 48)
        c8, egc, tl, etl, bgc, sp8 = sml(384, 16), sml(400, 16), sml(416, 16), sml(432, 16), sml(448, 16), sml(464, 32)
        sp8 = sp8.rearrange("p (t n) -> p t n", t=T)
        lf = sml(496, 16)

        pb = [ctx.enter_context(nc.psum_tensor(f"bank{i}", [P, 512], F32)) for i in range(8)]

        full = [sem(f"full{i}") for i in range(8)]
        free = [sem(f"free{i}") for i in range(8)]
        s_const = sem("s_const"); s_par = sem("s_par")
        s_x = [sem(f"s_x{t}") for t in range(T)]
        raw_full = [sem(f"raw_full{i}") for i in range(3)]
        whi_done = sem("whi_done"); wlo_done = sem("wlo_done"); gran_used = sem("gran_used")
        ssx_done = sem("ssx_done"); xn_done = sem("xn_done"); hhi_done = sem("hhi_done"); hlo_done = sem("hlo_done")
        act_self = sem("act_self"); dve_self = sem("dve_self"); pool_self = sem("pool_self")
        tap0_done = sem("tap0_done"); conv_done = sem("conv_done"); silu_done = sem("silu_done")
        z_in = sem("z_in"); gexp_in = sem("gexp_in"); gexp_done = sem("gexp_done"); gates_done = sem("gates_done")
        cum_done = sem("cum_done"); cexp_done = sem("cexp_done"); cfac_done = sem("cfac_done")
        vb_done = sem("vb_done"); cB_done = sem("cB_done")
        sq_done = sem("sq_done"); root_done = sem("root_done"); norm_done = sem("norm_done"); kt_done = sem("kt_done")
        d_raw = sem("d_raw"); e_ready = sem("e_ready"); d_exp = sem("d_exp"); ds_ready = sem("ds_ready")
        di_ready = sem("di_ready"); qg_ready = sem("qg_ready"); n_ready = sem("n_ready"); attn_ready = sem("attn_ready")
        uinit = sem("uinit"); xinit = sem("xinit"); y_ready = sem("y_ready"); x_ready = sem("x_ready"); u_ready = sem("u_ready")
        w_ready = sem("w_ready"); u0_ready = sem("u0_ready")
        y_copied = sem("y_copied")
        rot_done = sem("rot_done"); rT_done = sem("rT_done"); retP_done = sem("retP_done"); oret_done = sem("oret_done")
        uu_ready = sem("uu_ready"); st_ready = sem("st_ready"); og_done = sem("og_done")
        sx_ready = sem("sx_ready"); pf_ready = sem("pf_ready"); pt_ready = sem("pt_ready"); fox_done = sem("fox_done")
        zg_done = sem("zg_done"); sqr_done = sem("sqr_done"); ssr_done = sem("ssr_done"); rtr_done = sem("rtr_done")
        mix_done = sem("mix_done"); s_x2 = sem("s_x2in"); x2_done = sem("x2_done")
        s_out = sem("s_out")

        def psum(name):
            return pb[BANK[name][0]]

        def wait_full(e, name):
            b, n = BANK[name]
            e.wait_ge(full[b], n + 1)

        def release(ins, name):
            return ins.then_inc(free[BANK[name][0]], 1)

        tcol = {"v0": 8, "v1": 10, "k0": 4, "k1": 6, "q0": 0, "q1": 2}
        CONVN = {"v0": 0, "v1": 2, "k0": 4, "k1": 6, "q0": 8, "q1": 10}
        x2 = at("x2", [P, T, D], R3)

        SLOT = [113 * KB, 17 * KB, 65 * KB]
        h2T = at("h2T", [P, KC, P], 161 * KB)
        h2 = at("h2", [P, T, D], R3 + 16 * KB)
        rtA = at("rtA", [P, 1024], R3 + 32 * KB)
        n2b = at("n2b", [P, D], R3 + 36 * KB)
        rtB = at("rtB", [P, 1024], R3 + 36 * KB)
        fnb = at("fnb", [P, D], R3 + 36 * KB)
        rw = at("rw", [P, KC, NG + NE], R3 + 40 * KB)
        assert R3 + 40 * KB + KC * (NG + NE) * 4 <= 229344 - BASE
        w13 = [at(f"w13_{i}", [P, 2, 2, KC * FF], SLOT[i]) for i in range(3)]
        w2 = [at(f"w2_{i}", [P, 2, 2 * D], SLOT[i] + 32 * KB) for i in range(3)]
        xT = at("xT", [P, KC, P], 161 * KB)
        xg = at("xg", [P, D], R3 + 16 * KB)
        oy = at("oy", [P, D], R3 + 20 * KB)
        sa = at("sa", [P, FF], R3 + 24 * KB)
        hid = at("hid", [P, 2, P], R3 + 25 * KB)
        hidT = at("hidT", [P, 2, P], R3 + 26 * KB)
        sel = at("sel", [P, T, 2, CAP], R3 + 27 * KB)
        selw = at("selw", [P, T, 2, CAP], R3 + 29 * KB)
        emp = at("emp", [P, 1], R3 + 31 * KB)
        dst_i = [at(f"dst{i}", [P, 1], R3 + 31 * KB + 32 * (i + 1), I32) for i in range(3)]
        tok_i = [at(f"tok{i}", [P, 1], R3 + 31 * KB + 32 * (i + 4), I32) for i in range(3)]
        yt = [at(f"yt{i}", [P, 2, D], SLOT[0] + 8 * KB * i) for i in range(T)]
        jk = at("jk", [P, D], SLOT[0] + 32 * KB)
        rv4 = lambda a, n, w: (rtA if n == 0 else rtB)[:, a:a + T * w].rearrange("p (t n) -> p t n", t=T)
        Wt, rank, oh1, oh2, LG = rv4(0, 0, NE), rv4(128, 0, NE), rv4(256, 0, NE), rv4(384, 0, NE), rv4(512, 0, NG + NE)
        r1 = lambda i: rtA[:, 656 + 4 * i:660 + 4 * i]
        gm, gmx, gsum, gp, m1, m2, mm1, e2, den, gate0, gate1, ss2, r2, ssf, rf = (r1(i) for i in range(15))
        cmax = rtA[:, 720:721]
        npf = rtA[:, 721:722]
        npi = at("npi", [P, 1], R3 + 32 * KB + 4 * 736, I32)
        ml, t32, M32, ge = rv4(0, 1, NE), rv4(128, 1, NE), rv4(256, 1, NE), rv4(384, 1, NG)
        goh, gd, pen, t8 = rv4(400, 1, NG), rv4(416, 1, NG), rv4(432, 1, NG), rtB[:, 448:456]

        h2d = nc.dram_tensor("h2d", [S, D], F32, kind="Internal")
        yd = nc.dram_tensor("yd", [2 * S, D], F32, kind="Internal")
        w1v = ew1[0].rearrange("g e (p c) f -> (g e) p (c f)", c=KC)
        w3v = ew3[0].rearrange("g e (p c) f -> (g e) p (c f)", c=KC)
        w2v = ew2[0].rearrange("g e (p c) d -> (g e) p (c d)", c=2)
        outv = out[0].rearrange("(t p) d -> t p d", p=P)

        s_n2 = sem("s_n2"); ss2_done = sem("ss2_done"); h2_done = sem("h2_done"); s_h2d = sem("s_h2d")
        hT_done = sem("hT_done"); lg_done = sem("lg_done"); rexp_in = sem("rexp_in"); rexp_done = sem("rexp_done")
        m_done = sem("m_done"); route_done = sem("route_done")
        slots_freed = sem("slots_freed")
        w13_full = [sem(f"w13_full{i}") for i in range(3)]
        w2_full = [sem(f"w2_full{i}") for i in range(3)]
        sel_ready = sem("sel_ready"); idx_full = sem("idx_full"); idx_ready = sem("idx_ready"); gathered = sem("gathered")
        xt_full = sem("xt_full"); xt_ready = sem("xt_ready"); up_full = sem("up_full"); sa_ready = sem("sa_ready"); loop_self = sem("loop_self"); next_rank = sem("next_rank"); pool_step = sem("pool_step")
        hid_ready = sem("hid_ready"); ht_full = sem("ht_full"); ht_ready = sem("ht_ready")
        oyA = sem("oyA"); oyB = sem("oyB"); scattered = sem("scattered")
        s_y = [sem(f"s_y{t}") for t in range(T)]
        acc_done = sem("acc_done"); ssf_done = sem("ssf_done"); fin_done = sem("fin_done")

        def passes(e, unit, start=None, stop=None):
            e.wait_ge(route_done, 1)
            n = e.value_load(npi[0:1, 0:1], min_val=1, max_val=S // CAP)
            with e.Fori(0, n) as p:
                if start is not None:
                    start(p * PAIRS)
                with e.Fori(0, 5) as i:
                    for s in range(3):
                        unit(p * PAIRS + i * 3 + s, i * 3 + s, s, p * (6 if s == 0 else 5) + i, False)
                unit(p * PAIRS + 15, 15, 0, p * 6 + 5, True)
                if stop is not None:
                    stop(p)
            return n

        block = ctx.enter_context(nc.Block())

        @block.sync
        def _(sp):
            sp.dma_start(CT[:, :], consts).then_inc(s_const, 16)
            for t in range(T):
                sp.dma_start(X0[:, t, :], x[0, t * P:(t + 1) * P, :]).then_inc(s_x[t], 16)

            def granule(g):
                if g >= 3:
                    sp.wait_ge(wlo_done, g - 2)
                if g < GR_IN:
                    _, _, c0, w = GROUPS[g // 2]
                    src = w_in[0]
                else:
                    c0, w = 256 * ((g - GR_IN) // 2), 256
                    src = w_out[0]
                k0 = (g % 2) * HK * P
                sp.dma_start(raw[g % 3][:, :, 0:w],
                             src[k0:k0 + HK * P, c0:c0 + w].rearrange("(c p) n -> p c n", p=P)
                             ).then_inc(raw_full[g % 3], 16)

            for g in range(3):
                granule(g)
            with nc.allow_non_contiguous_dma("small parameters"):
                npar = 0
                for dst, src in ((PN1[:, :], n1w[0].rearrange("(c p) -> p c", p=P)),
                                 (PDT[:, :], dtb[0:1, :].broadcast_to([P, 4])),
                                 (PAL[:, :], alog[0:1, :].broadcast_to([P, 4])),
                                 (PFB[:, :], foxb[0:1, :].broadcast_to([P, 4])),
                                 (PRB[:, 0:NG], rgb[0:1, :].broadcast_to([P, NG])),
                                 (PRB[:, NG:], reb.rearrange("a g e -> a (g e)").broadcast_to([P, NE])),
                                 (PGN[:, :], gnw[0:1, :].broadcast_to([P, P])),
                                 ):
                    sp.dma_start(dst, src).then_inc(s_par, 16)
                for tap in range(4):
                    sp.dma_start(PCW[:, :, tap], convw[0, tap].rearrange("(b p) -> p b", p=P)).then_inc(s_par, 16)
            for g in range(3, GR_IN + 4):
                granule(g)
            sp.wait_ge(mix_done, 3)
            for t in range(T):
                sp.dma_start(x2[:, t, :], x[0, t * P:(t + 1) * P, :]).then_inc(s_x2, 16)
            sp.dma_start(n2b[:, :], n2w[0:1, :].broadcast_to([P, D])).then_inc(s_n2, 16)
            sp.dma_start(rw[:, :, 0:NG], rgw[0].rearrange("(p c) g -> p c g", c=KC)).then_inc(s_n2, 16)
            sp.dma_start(rw[:, :, NG:], rew[0].rearrange("(p c) g -> p c g", c=KC)).then_inc(s_n2, 16)
            for g in range(GR_IN + 4, GR):
                granule(g)

            def load(U, q, s, use, last):
                sp.wait_ge(slots_freed, U + 1)
                es = bass.ds(q * 2, 2) if not isinstance(q, int) else slice(2 * q, 2 * q + 2)
                sp.dma_start(w13[s][:, :, 0, :], w1v[es].rearrange("e p n -> p e n")).then_inc(w13_full[s], 16)
                sp.dma_start(w13[s][:, :, 1, :], w3v[es].rearrange("e p n -> p e n")).then_inc(w13_full[s], 16)
                sp.dma_start(w2[s][:, :, :], w2v[es].rearrange("e p n -> p e n")).then_inc(w2_full[s], 16)

            for s in range(3):
                load(s, s, s, 0, False)
            sp.wait_ge(route_done, 1)
            n = sp.value_load(npi[0:1, 0:1], min_val=1, max_val=S // CAP)
            with sp.Fori(0, n) as p:
                with sp.Fori(1, 5) as i:
                    for s in range(3):
                        load(p * PAIRS + i * 3 + s, i * 3 + s, s, 0, False)
                load(p * PAIRS + 15, 15, 0, 0, True)
                with sp.If(p + 1 < n):
                    for s in range(3):
                        load(p * PAIRS + PAIRS + s, s, s, 0, False)
            sp.wait_ge(scattered, n * (PAIRS * 16) + 16)
            for t in range(T):
                sp.dma_start(yt[t][:, :, :], yd.ap().rearrange("(k t p) d -> t p k d", k=2, p=P)[t]).then_inc(s_y[t], 16)
            for t in range(T):
                sp.wait_ge(fin_done, t + 1)
                sp.dma_start(outv[t], x2[:, t, :]).then_inc(s_out, 16)
            sp.wait_ge(s_out, 16 * T)

        @block.tensor
        def _(pe):
            order = {0: list(ORDER_A), 1: list(ORDER_B)}

            def begin(name):
                b, n = BANK[name]
                assert order[b // 4].pop(0) == name, name
                if n:
                    pe.wait_ge(free[b], n)
                return pb[b]

            def end(ins, name):
                ins.then_inc(full[BANK[name][0]], 1)

            def granule(g):
                pe.wait_ge(wlo_done, g + 1)
                half = g % 2
                n = g // 2
                hi, lo = whi[g % 2], wlo[g % 2]
                kind, w = ("n", 256) if g >= GR_IN else (GROUPS[n][0], GROUPS[n][3])
                for b in range(T if kind == "n" else 2):
                    name = ("y", n, b)
                    ps = begin(name) if half == 0 else psum(name)
                    for c in range(HK):
                        kc = half * HK + c
                        if kind == "n":
                            tk = slice(b * P, (b + 1) * P)
                            o = ps[:, 0:w]
                            terms = ((hHi[:, kc, tk], hi[:, c, 0:w]), (hHi[:, kc, tk], lo[:, c, 0:w]),
                                     (hLo[:, kc, tk], hi[:, c, 0:w]))
                        else:
                            ch = slice(b * P, (b + 1) * P)
                            o = ps[:, :]
                            terms = ((hi[:, c, ch], hHi[:, kc, :]), (hi[:, c, ch], hLo[:, kc, :]),
                                     (lo[:, c, ch], hHi[:, kc, :]))
                        for i, (l, r) in enumerate(terms):
                            m = pe.matmul(o, l, r, start=(kc == 0 and i == 0), stop=(kc == KC - 1 and i == 2),
                                          skip_group_check=True)
                    if half == 1:
                        if b == (T if kind == "n" else 2) - 1:
                            end(m, name)
                        else:
                            end(m, name)
                if half == 0:
                    m.then_inc(gran_used, 1)
                else:
                    pe.wait_ge(full[BANK[name][0]], BANK[name][1] + 1)
                    pe.sem_inc(gran_used, 1)

            def four(name, f):
                ps = begin(name)
                for h in range(NH):
                    o = ps[:, h * P:(h + 1) * P]
                    m = f(h, o)
                end(m, name)

            def mm(o, l, r):
                return pe.matmul(o, l, r, start=True, stop=True)

            def task(k):
                if k[0] == "vt":
                    h = k[1]
                    pe.wait_ge(silu_done, h + 1)
                    four(k, lambda t, o: pe.transpose(o, vS[h % 2][:, t * P:(t + 1) * P], ident))
                elif k[0] == "gcum":
                    pe.wait_ge(gates_done, 1)
                    ps = begin(k)
                    for t in range(T):
                        g4 = gg[:, 4 * t:4 * t + 4]
                        mm(ps[:, 4 * t:4 * t + 4], tri, g4)
                        mm(ps[:, 16 + 4 * t:20 + 4 * t], ones, g4)
                        for tt in range(t + 1):
                            m = pe.matmul(ps[:, 32 + 4 * t:36 + 4 * t], tri if tt == t else ones,
                                          lf[:, 4 * tt:4 * tt + 4], start=(tt == 0), stop=(tt == t))
                    end(m, k)
                elif k[0] == "cB":
                    pe.wait_ge(cum_done, 2)
                    for h in range(NH):
                        four(("cB", h), lambda t, o: mm(o, c8[:, 4 * t + h:4 * t + h + 1].broadcast_to([P, P]), ident))
                elif k[0] == "ss":
                    for h in range(NH):
                        n = NH * k[1] + h
                        pe.wait_ge(sq_done, n + 1)
                        name = ("ss", n)
                        ps = begin(name)
                        end(mm(ps[:, :], ones, nrm[n % 4][:, :]), name)
                elif k[0] == "kt":
                    for h in range(NH):
                        pe.wait_ge(norm_done, h + 1)
                        four(("kt", h), lambda t, o: pe.transpose(o, kT[:, h, t * P:(t + 1) * P], ident))
                elif k[0] == "prep":
                    t = k[1]
                    tk = slice(t * P, (t + 1) * P)
                    pe.wait_ge(norm_done, 2 * NH)
                    four(("gcB", t), lambda h, o: mm(o, cum[:, 4 * t + h:4 * t + h + 1].broadcast_to([P, P]), ident))
                    four(("bB", t), lambda h, o: mm(o, beta[:, 4 * t + h:4 * t + h + 1].broadcast_to([P, P]), ident))
                    four(("KK", t), lambda h, o: mm(o, kT[:, h, tk], kT[:, h, tk]))
                    four(("QK", t), lambda h, o: mm(o, kT[:, h, tk], qT[:, h, tk]))
                elif k[0] == "xt":
                    for t in (2 * k[1], 2 * k[1] + 1):
                        pe.wait_ge(uinit, t + 1)
                        four(("XT", t), lambda h, o: pe.transpose(o, Um[t % 2][:, h, :], ident))
                elif k[0] == "lv":
                    _, pr, lv = k
                    for i in range(2):
                        t = 2 * pr + i
                        if lv == 0:
                            pe.wait_ge(xinit, t + 1)
                        else:
                            pe.wait_ge(x_ready, (pr * (LEVELS - 1) + lv - 1) * 2 + i + 1)
                        four(("Y", t, lv), lambda h, o: mm(o, Nm[i][:, h, :], Xm[i][:, h, :]))
                    for i in range(2):
                        t = 2 * pr + i
                        pe.wait_ge(y_ready, (pr * LEVELS + lv) * 2 + i + 1)
                        if lv:
                            pe.wait_ge(u_ready, (pr * LEVELS + lv - 1) * 2 + i + 1)
                        if lv < LEVELS - 1:
                            four(("Xp", t, lv), lambda h, o: mm(o, Um[i][:, h, :], Ym[i][:, h, :]))
                        four(("Up", t, lv), lambda h, o: mm(o, Ym[i][:, h, :], Um[i][:, h, :]))
                elif k[0] == "fin":
                    for i in range(2):
                        t = 2 * k[1] + i
                        pe.wait_ge(u_ready, (k[1] * LEVELS + LEVELS - 1) * 2 + i + 1)
                        pe.wait_ge(kt_done, NH)
                        four(("wT", t), lambda h, o: mm(o, kbg[:, t, h, :], Um[i][:, h, :]))
                        four(("u0", t), lambda h, o: mm(o, Um[i][:, h, :], vb[:, t, h, :]))

            pe.wait_ge(s_const, 16)
            pe.wait_ge(xn_done, T)
            for c in range(KC):
                four(("xT", c), lambda t, o: pe.transpose(o, X0[:, t, c * P:(c + 1) * P], ident))
            pe.wait_ge(hlo_done, KC)
            for g in range(GR_IN):
                granule(g)
                for k in AFTER[g]:
                    task(k)

            for i in range(4):
                src = rq if i < 2 else rk
                pe.wait_ge(rot_done, 1 if i < 2 else 2)
                four(("rT", i), lambda t, o: pe.transpose(o, src[:, t, (i % 2) * P:(i % 2 + 1) * P], ident))
            pe.wait_ge(y_copied, 6)
            for k in range(KSTEPS):
                if k < 16:
                    h, t = FOX[k]
                    hp = slice((h % 2) * HD, (h % 2) * HD + HD)
                    name = ("fS", k)
                    ps = begin(name)
                    w = (t + 1) * P
                    pe.matmul(ps[:, 0:w], fqT[hp, h // 2, t * P:(t + 1) * P], fkT[hp, h // 2, 0:w], start=True, stop=False)
                    end(pe.matmul(ps[:, t * P:w], ident, negmask, start=False, stop=True), name)
                if 1 <= k <= 16:
                    h, t = FOX[k - 1]
                    name = ("fT", k - 1)
                    pe.wait_ge(pf_ready, k)
                    ps = begin(name)
                    for j in range(t + 1):
                        m = pe.transpose(ps[:, j * P:(j + 1) * P], Pf[(k - 1) % 2][:, j * P:(j + 1) * P], ident)
                    end(m, name)
                if k >= 2:
                    h, t = FOX[k - 2]
                    name = ("fO", k - 2)
                    pe.wait_ge(pt_ready, k - 1)
                    ps = begin(name)
                    for j in range(t + 1):
                        m = pe.matmul(ps[:, 0:HD], PT[(k - 2) % 2][:, j, :], fv[:, j, h * HD:(h + 1) * HD],
                                      start=(j == 0), stop=(j == t))
                    end(m, name)
                if k < 16:
                    n = k // 4
                    if k % 4 == 0 and n:
                        pe.wait_ge(st_ready, n)
                        four(("wS", n), lambda h, o: mm(o, kbg[:, n, h, :], St[:, h, :]))
                    if k % 4 == 1:
                        hp = slice((n % 2) * HD, (n % 2) * HD + HD)
                        pe.wait_ge(rT_done, 4)
                        for j in range(T):
                            name = ("rS", n, j)
                            ps = begin(name)
                            end(mm(ps[:, 0:PW[j]], rkT[hp, n // 2, j * P:(j + 1) * P], rqT[hp, n // 2, j * P:S]), name)
                    if k % 4 == 2:
                        name = ("o", n)
                        ps = begin(name)
                        pe.wait_ge(uu_ready, n + 1)
                        pe.wait_ge(attn_ready, n + 1)
                        for h in range(NH):
                            o = ps[:, h * P:(h + 1) * P]
                            if n:
                                pe.matmul(o, qT[:, h, n * P:(n + 1) * P], St[:, h, :], start=True, stop=False)
                            m = pe.matmul(o, attnT[:, n, h, :], vb[:, n, h, :], start=(n == 0), stop=True)
                        end(m, name)
                        if n < T - 1:
                            four(("Sp", n), lambda h, o: mm(o, ktail[:, n, h, :], vb[:, n, h, :]))
                    if k % 4 == 3:
                        name = ("rO", n)
                        ps = begin(name)
                        pe.wait_ge(retP_done, T * (n + 1))
                        for t in range(T):
                            for j in range(t + 1):
                                c0 = POFF[j] + (t - j) * P
                                m = pe.matmul(ps[:, t * HD:(t + 1) * HD], retP[:, c0:c0 + P],
                                              rv[:, j, n * HD:(n + 1) * HD], start=(j == 0), stop=(j == t))
                        end(m, name)
            pe.wait_ge(mix_done, 3)
            pe.wait_ge(fox_done, 16)
            for c in range(KC):
                four(("mT", c), lambda t, o: pe.transpose(o, mix[:, t, c * P:(c + 1) * P], ident))
            pe.wait_ge(hlo_done, 2 * KC)
            for g in range(GR_IN, GR):
                granule(g)

            pe.wait_ge(s_n2, 48)
            for t in range(T):
                pe.wait_ge(h2_done, t + 1)
                for half in range(2):
                    four(("hT", t, half), lambda c, o: pe.transpose(
                        o, h2[:, t, (4 * half + c) * P:(4 * half + c + 1) * P], ident))
                pe.wait_ge(hT_done, t + 1)
                name = ("lg", t)
                ps = begin(name)
                for c in range(KC):
                    m = pe.matmul(ps[:, 0:NG + NE], h2T[:, c, :], rw[:, c, :], start=(c == 0), stop=(c == KC - 1))
                end(m, name)
            pe.wait_ge(m_done, 1)
            name = ("rank",)
            ps = begin(name)
            for t in range(T):
                for j in range(t + 1):
                    pe.matmul(ps[:, t * NE:(t + 1) * NE], const("rankm") if j == t else ones, M32[:, j, :],
                              start=(j == 0), stop=(j == t))
            for j in range(T):
                m = pe.matmul(ps[:, T * NE:(T + 1) * NE], ones, M32[:, j, :], start=(j == 0), stop=(j == T - 1))
            end(m, name)

            def indices(U):
                pe.wait_ge(sel_ready, U + 1)
                pe.wait_ge(idx_ready, U + 1)
                for t in range(T):
                    m = pe.matmul(pb[0][:, 0:1], selw[:, t, :, :], ones[:, 0:1], start=(t == 0), stop=(t == T - 1))
                m.then_inc(idx_full, 1)

            def turn(U):
                pe.wait_ge(gathered, U * 16 + 16)
                pe.wait_ge(xt_ready, U + 1)
                for c in range(KC):
                    m = pe.transpose(pb[1 + c // 4][:, (c % 4) * P:(c % 4 + 1) * P], xg[:, c * P:(c + 1) * P], ident)
                m.then_inc(xt_full, 1)

            def start(U0):
                indices(U0)
                turn(U0)

            def unit(U, q, s, use, last):
                if not last:
                    indices(U + 1)
                pe.wait_ge(xt_ready, U + 2)
                pe.wait_ge(w13_full[s], use * 32 + 32)
                pe.wait_ge(hid_ready, U + 1)
                for c in range(KC):
                    for e in range(2):
                        r = slice(e * CAP, (e + 1) * CAP)
                        m = pe.matmul(pb[3][r, :], xT[:, c, r], w13[s][:, e, :, c * FF:(c + 1) * FF],
                                      start=(c == 0), stop=(c == KC - 1), skip_group_check=True)
                m.then_inc(up_full, 1)
                if not last:
                    turn(U + 1)
                pe.wait_ge(hid_ready, U + 2)
                pe.wait_ge(ht_ready, U + 1)
                for c in range(2):
                    m = pe.transpose(pb[4][:, c * P:(c + 1) * P], hid[:, c, :], ident)
                m.then_inc(ht_full, 1)
                pe.wait_ge(ht_ready, U + 2)
                pe.wait_ge(w2_full[s], use * 16 + 16)
                pe.wait_ge(oyA, U + 1)
                pe.wait_ge(oyB, U + 1)
                for n in range(2):
                    for c in range(2):
                        for e in range(2):
                            r = slice(e * CAP, (e + 1) * CAP)
                            m = pe.matmul(pb[5 + n][r, :], hidT[:, c, r],
                                          w2[s][:, e, c * D + n * 512:c * D + (n + 1) * 512],
                                          start=(c == 0), stop=(c == 1), skip_group_check=True)
                m.then_inc(slots_freed, 1)

            passes(pe, unit, start)

        def weight_high(e, g):
            w = 256 if g >= GR_IN else GROUPS[g // 2][3]
            e.wait_ge(raw_full[g % 3], 16 * (g // 3 + 1))
            if g >= 2:
                e.wait_ge(gran_used, g - 1)
            e.activation(whi[g % 2][:, :, 0:w], raw[g % 3][:, :, 0:w], ACT.Copy).then_inc(whi_done, 1)

        @block.scalar
        def _(act):
            cnt = [0]

            def link(ins):
                cnt[0] += 1
                ins.then_inc(act_self, 1)
                act.wait_ge(act_self, cnt[0])

            act.wait_ge(s_const, 16)
            for t in range(T):
                act.wait_ge(s_x[t], 16)
                link(act.activation(junk[:, :], X0[:, t, :], ACT.Square, accum_out=ssx[:, t:t + 1]))
            act.activation(ssx, ssx, ACT.Sqrt, scale=1.0 / D, bias=eps).then_inc(ssx_done, 1)
            act.wait_ge(s_par, 16 * 11)
            weight_high(act, 0)
            weight_high(act, 1)
            for c in range(KC):
                name = ("xT", c)
                wait_full(act, name)
                act.activation(hHi[:, c, :], psum(name)[:, :], ACT.Copy, scale=PN1[:, c:c + 1]).then_inc(hhi_done, 1)

            def evac(n):
                kind, what, _, w = GROUPS[n]
                if kind == "n":
                    for t in range(T):
                        name = ("y", n, t)
                        wait_full(act, name)
                        ps = psum(name)
                        cp = lambda dst, src: act.activation(dst, src, ACT.Copy)
                        if what == "fv":
                            cp(fv[:, t, :], ps[:, 0:256])
                            i = cp(FFT[:, t, :], ps[:, 256:260])
                        elif what == "zb":
                            act.activation(mix[:, t, GW + 260:D], ps[:, 0:252], ACT.Silu)
                            i = cp(GAB[:, t, :], ps[:, 252:260])
                        elif what == "za":
                            i = act.activation(mix[:, t, GW:GW + 260], ps[:, 0:260], ACT.Silu)
                        elif what == "rg":
                            i = act.activation(mix[:, t, 256:GW], ps[:, 0:256], ACT.Silu)
                        else:
                            i = cp({"rq": rq, "rk": rk, "rv": rv}[what][:, t, :], ps[:, 0:256])
                        release(i, name)
                    act.wait_ge(free[BANK[name][0]], BANK[name][1] + 1)
                    act.sem_inc(y_copied, 1) if what not in ("zb", "za", "rg") else act.sem_inc(z_in, 1)
                elif what in ("fq", "fk"):
                    for b in range(2):
                        name = ("y", n, b)
                        wait_full(act, name)
                        release(act.activation((fqT if what == "fq" else fkT)[:, b, :], psum(name)[:, :], ACT.Copy), name)
                    act.wait_ge(free[BANK[name][0]], BANK[name][1] + 1)
                    act.sem_inc(y_copied, 1)
                else:
                    for b in range(2):
                        name = ("y", n, b)
                        blk = tcol[what] + b
                        i = CONVN[what] + b
                        wait_full(act, name)
                        if i >= 2:
                            act.wait_ge(silu_done, i - 1)
                        act.activation(cacc[i % 2][:, :], psum(name)[:, :], ACT.Copy,
                                       scale=PCW[:, blk, 3:4]).then_inc(tap0_done, 1)
                        act.wait_ge(conv_done, i + 1)
                        h = i % 4
                        if what[0] == "v":
                            dst = vS[h % 2][:, :]
                            if h >= 2:
                                act.wait_ge(vb_done, h - 1)
                        else:
                            dst = (kT if what[0] == "k" else qT)[:, h, :]
                        act.activation(dst, cacc[i % 2][:, :], ACT.Silu).then_inc(silu_done, 1)

            def task(k):
                if k[0] == "evac":
                    evac(k[1])
                elif k[0] == "gates":
                    act.wait_ge(gexp_in, 1)
                    act.activation(e8, az, ACT.Exp, scale=-1.0)
                    act.activation(eb.rearrange("p (t n) -> p t n", t=T), GAB[:, :, 4:8], ACT.Exp, scale=-1.0)
                    act.activation(ea, PAL[:, :], ACT.Exp).then_inc(gexp_done, 1)
                elif k[0] == "gcum":
                    act.wait_ge(cum_done, 3)
                    act.activation(egc, cum[:, 0:16], ACT.Exp)
                    act.activation(egl, cum[:, 16:32], ACT.Exp)
                    act.activation(etl, tl, ACT.Exp).then_inc(cexp_done, 1)
                elif k[0] == "cB":
                    for h in range(NH):
                        name = ("cB", h)
                        wait_full(act, name)
                        release(act.activation(cB8[:, h, :], psum(name)[:, :], ACT.Copy), name)
                    act.wait_ge(free[BANK[name][0]], BANK[name][1] + 1)
                    act.sem_inc(cB_done, 1)
                elif k[0] == "ss":
                    for h in range(NH):
                        n = NH * k[1] + h
                        name = ("ss", n)
                        wait_full(act, name)
                        i = act.activation(nrm[n % 4][:, :], psum(name)[:, :], ACT.Sqrt,
                                           scale=1.0 if k[1] == 0 else float(P),
                                           bias=eps if k[1] == 0 else const("eps128"))
                        release(i, name)
                        act.wait_ge(free[BANK[name][0]], BANK[name][1] + 1)
                        act.sem_inc(root_done, 1)
                elif k[0] == "prep":
                    t = k[1]
                    i = t % 2
                    act.wait_ge(d_raw, t + 1)
                    name = ("gcB", t)
                    if t >= 2:
                        act.wait_ge(u_ready, 2 * LEVELS - 1 + i)
                    j = act.activation(Xm[i][:, :, :], psum(name)[:, :].rearrange("p (h n) -> p h n", h=NH), ACT.Exp)
                    release(j, name)
                    act.activation(Dm[i][:, :, :], Dm[i][:, :, :], ACT.Exp).then_inc(d_exp, 1)
                elif k[0] == "xt":
                    for t in (2 * k[1], 2 * k[1] + 1):
                        name = ("XT", t)
                        wait_full(act, name)
                        j = act.activation(Xm[t % 2][:, :, :], psum(name)[:, :].rearrange("p (h n) -> p h n", h=NH), ACT.Copy)
                        release(j, name)
                        act.wait_ge(free[BANK[name][0]], BANK[name][1] + 1)
                        act.sem_inc(xinit, 1)
                elif k[0] == "fin":
                    for t in (2 * k[1], 2 * k[1] + 1):
                        for name, dst, sc in ((("wT", t), kbg, -1.0), (("u0", t), vb, 1.0)):
                            wait_full(act, name)
                            j = act.activation(dst[:, t, :, :], psum(name)[:, :].rearrange("p (h n) -> p h n", h=NH),
                                               ACT.Copy, scale=sc)
                            release(j, name)
                        act.wait_ge(free[BANK[name][0]], BANK[name][1] + 1)
                        act.sem_inc(u0_ready, 1)

            for g in range(GR_IN):
                weight_high(act, g + 2)
                for k in AFTER[g]:
                    task(k)
            for i in range(4):
                name = ("rT", i)
                wait_full(act, name)
                j = act.activation((rqT if i < 2 else rkT)[:, i % 2, :], psum(name)[:, :], ACT.Copy)
                release(j, name)
                act.wait_ge(free[BANK[name][0]], BANK[name][1] + 1)
                act.sem_inc(rT_done, 1)
            for k in range(KSTEPS):
                if k < 16:
                    h, t = FOX[k]
                    w = (t + 1) * P
                    act.wait_ge(sx_ready, k + 1)
                    if k >= 2:
                        wait_full(act, ("fT", k - 2))
                    act.activation(Pf[k % 2][:, 0:w], Sx[k % 2][:, 0:w], ACT.Exp, scale=HD ** -0.5,
                                   bias=nmx[:, k:k + 1], accum_out=rs[:, k:k + 1]).then_inc(pf_ready, 1)
                if 1 <= k <= 16:
                    h, t = FOX[k - 1]
                    name = ("fT", k - 1)
                    wait_full(act, name)
                    if k >= 3:
                        wait_full(act, ("fO", k - 3))
                    j = act.activation(PT[(k - 1) % 2][:, 0:t + 1, :],
                                       psum(name)[:, 0:(t + 1) * P].rearrange("p (j n) -> p j n", n=P), ACT.Copy)
                    release(j, name)
                    act.wait_ge(free[BANK[name][0]], BANK[name][1] + 1)
                    act.sem_inc(pt_ready, 1)
                if k < 16:
                    n = k // 4
                    if k % 4 == 2:
                        name = ("o", n)
                        wait_full(act, name)
                        j = act.activation(kbg[:, n, :, :], psum(name)[:, :].rearrange("p (h n) -> p h n", h=NH), ACT.Copy)
                        release(j, name)
                        act.wait_ge(free[BANK[name][0]], BANK[name][1] + 1)
                        act.sem_inc(og_done, 1)
                    if k % 4 == 3:
                        name = ("rO", n)
                        wait_full(act, name)
                        j = act.activation(oret[:, :, n * HD:(n + 1) * HD],
                                           psum(name)[:, 0:T * HD].rearrange("p (t n) -> p t n", t=T), ACT.Copy)
                        release(j, name)
                        act.wait_ge(free[BANK[name][0]], BANK[name][1] + 1)
                        act.sem_inc(oret_done, 1)
            act.wait_ge(ssr_done, 1)
            act.activation(ssn, ssn, ACT.Sqrt, scale=1.0 / P, bias=eps).then_inc(rtr_done, 1)
            act.wait_ge(ssr_done, 2)
            act.activation(ssx4, ssx4, ACT.Sqrt, scale=1.0 / HD, bias=eps).then_inc(rtr_done, 1)
            for c in range(KC):
                name = ("mT", c)
                wait_full(act, name)
                act.activation(hHi[:, c, :], psum(name)[:, :], ACT.Copy).then_inc(hhi_done, 1)
            for g in range(GR_IN, GR - 2):
                weight_high(act, g + 2)
            for t in range(T):
                name = ("y", NIN + NOUT - 1, t)
                act.wait_ge(x2_done, T * (NOUT - 1) + t + 1)
                link(act.activation(h2[:, t, :], x2[:, t, :], ACT.Square, accum_out=ss2[:, t:t + 1]))
            act.activation(ss2, ss2, ACT.Sqrt, scale=1.0 / D, bias=eps).then_inc(ss2_done, 1)
            for t in range(T):
                act.wait_ge(h2_done, t + 1)
                act.dma_start(h2d.ap()[t * P:(t + 1) * P, :], h2[:, t, :]).then_inc(s_h2d, 16)
                for half in range(2):
                    name = ("hT", t, half)
                    wait_full(act, name)
                    if t:
                        wait_full(act, ("lg", t - 1))
                    release(act.activation(h2T[:, 4 * half:4 * half + 4, :],
                                           psum(name)[:, :].rearrange("p (c n) -> p c n", n=P), ACT.Copy), name)
                act.wait_ge(free[BANK[name][0]], BANK[name][1] + 1)
                act.sem_inc(hT_done, 1)
            act.wait_ge(rexp_in, 1)
            act.activation(gd, gd, ACT.Exp).then_inc(rexp_done, 1)
            act.wait_ge(rexp_in, 2)
            act.activation(e2, mm1, ACT.Exp).then_inc(rexp_done, 1)

            def turned(U):
                act.wait_ge(xt_full, U + 2)
                act.wait_ge(up_full, U + 1)
                act.activation(xT[:, 0:4, :], pb[1][:, :].rearrange("p (c n) -> p c n", n=P), ACT.Copy)
                act.activation(xT[:, 4:8, :], pb[2][:, :].rearrange("p (c n) -> p c n", n=P), ACT.Copy).then_inc(xt_ready, 1)

            def unit(U, q, s, use, last):
                act.wait_ge(up_full, U + 2)
                act.activation(sa[:, :], pb[3][:, 0:FF], ACT.Silu).then_inc(sa_ready, 1)
                if not last:
                    turned(U + 1)
                act.wait_ge(ht_full, U + 2)
                act.activation(hidT[:, :, :], pb[4][:, 0:2 * P].rearrange("p (c n) -> p c n", n=P), ACT.Copy).then_inc(ht_ready, 1)
                act.wait_ge(slots_freed, U + 4)
                act.wait_ge(scattered, U * 16 + 16)
                act.activation(oy[:, 512:D], pb[6][:, :], ACT.Copy).then_inc(oyB, 1)

            passes(act, unit, turned)
            for t in range(T):
                act.wait_ge(acc_done, t + 1)
                act.activation(jk[:, :], yt[t][:, 0, :], ACT.Square, accum_out=ssf[:, t:t + 1]).then_inc(ssf_done, 1)
                act.wait_ge(ssf_done, 2 * t + 1)
                act.activation(ssf[:, t:t + 1], ssf[:, t:t + 1], ACT.Sqrt, scale=1.0 / D, bias=eps).then_inc(ssf_done, 1)

        @block.gpsimd
        def _(pool):
            cnt = [0]

            def link(ins):
                cnt[0] += 1
                ins.then_inc(pool_self, 1)
                pool.wait_ge(pool_self, cnt[0])

            def weight_low(g):
                w = 256 if g >= GR_IN else GROUPS[g // 2][3]
                pool.wait_ge(whi_done, g + 1)
                pool.tensor_tensor(wlo[g % 2][:, :, 0:w], raw[g % 3][:, :, 0:w], whi[g % 2][:, :, 0:w].bitcast(F32),
                                   ALU.subtract).then_inc(wlo_done, 1)

            def bc(m):
                return m.unsqueeze(1).broadcast_to([P, NH, P])

            weight_low(0)
            weight_low(1)

            def squares(k):
                for h in range(NH):
                    n = NH * k + h
                    pool.wait_ge(silu_done, NH + n + 1)
                    if n >= 4:
                        pool.wait_ge(norm_done, n - 3)
                    src = (kT if k == 0 else qT)[:, h, :]
                    pool.tensor_tensor(nrm[n % 4][:, :], src, src, ALU.mult).then_inc(sq_done, 1)

            def task(k):
                if k[0] == "ss":
                    squares(k[1])
                elif k[0] == "prep":
                    t = k[1]
                    i = t % 2
                    tk = slice(t * P, (t + 1) * P)
                    pool.wait_ge(d_exp, t + 1)
                    pool.tensor_tensor(Ym[i][:, :, :], Dm[i][:, :, :], bc(strict), ALU.mult).then_inc(ds_ready, 1)
                    pool.tensor_tensor(Dm[i][:, :, :], Dm[i][:, :, :], bc(tri), ALU.mult).then_inc(di_ready, 1)
                    wait_full(pool, ("QK", t))
                    pool.tensor_tensor(qT[:, :, tk], qT[:, :, tk], Xm[i][:, :, :], ALU.mult).then_inc(qg_ready, 1)
                    pool.wait_ge(n_ready, t + 1)
                    link(pool.tensor_tensor(Ym[i][:, :, :], Nm[i][:, :, :], bc(const("nM1")), ALU.mult))
                    pool.tensor_tensor(Um[i][:, :, :], Ym[i][:, :, :], bc(ident), ALU.add).then_inc(uinit, 1)
                elif k == ("evac", 11):
                    rotary(rq, 1)
                elif k == ("evac", 12):
                    rotary(rk, 2)
                elif k == ("evac", 13):
                    pool.wait_ge(z_in, 3)
                    for t in range(T):
                        m4 = mix[:, t, GW:D].rearrange("p (h n) -> p h n", h=NH)
                        j = pool.tensor_tensor(m4, m4, bc(PGN[:, :]), ALU.mult)
                    j.then_inc(zg_done, 1)

            def rotary(r, n):
                pool.wait_ge(y_copied, n + 1)
                if n == 1:
                    pool.wait_ge(norm_done, 2 * NH)
                v = r[:, :, :].rearrange("p t (h s n) -> p t h s n", h=NH, s=2)
                t1, t2 = v[:, :, :, 0, :], v[:, :, :, 1, :]
                co = cosT.unsqueeze(2).broadcast_to([P, T, NH, 32])
                si = sinT.unsqueeze(2).broadcast_to([P, T, NH, 32])
                if n == 2:
                    pool.wait_ge(rot_done, 1)
                pool.tensor_tensor(rtmp[0][:, :, :, :], t1, co, ALU.mult)
                pool.tensor_tensor(rtmp[1][:, :, :, :], t2, si, ALU.mult)
                pool.tensor_tensor(rtmp[2][:, :, :, :], t1, si, ALU.mult)
                link(pool.tensor_tensor(rtmp[3][:, :, :, :], t2, co, ALU.mult))
                pool.tensor_tensor(t1, rtmp[0][:, :, :, :], rtmp[1][:, :, :, :], ALU.subtract)
                pool.tensor_tensor(t2, rtmp[2][:, :, :, :], rtmp[3][:, :, :, :], ALU.add).then_inc(rot_done, 1)

            for g in range(GR_IN):
                weight_low(g + 2)
                for k in AFTER[g]:
                    task(k)
            pool.wait_ge(og_done, T)
            pool.wait_ge(st_ready, T - 1)
            wait_full(pool, ("o", T - 1))
            o3 = kbg[:, :, :, :]
            pool.tensor_tensor(gsq[:, :, :, :], o3, o3, ALU.mult).then_inc(sqr_done, 1)
            pool.wait_ge(oret_done, NH)
            pool.tensor_tensor(osq[:, :, :], oret[:, :, :], oret[:, :, :], ALU.mult).then_inc(sqr_done, 1)
            for g in range(GR_IN, GR - 2):
                weight_low(g + 2)

            pool.wait_ge(s_h2d, 16 * T)

            def gather(U, s):
                pool.wait_ge(idx_ready, U + 2)
                pool.wait_ge(xt_full, U + 1)
                pool.sem_inc(pool_step, 1)
                pool.indirect_dma_start(xg[:, :], None, h2d.ap()[:, :],
                                        bass.IndirectOffsetOnAxis(ap=tok_i[s][:, 0:1].bitcast(U32), axis=0),
                                        bounds_check=S - 1, oob_is_err=False).then_inc(gathered, 16)

            def unit(U, q, s, use, last):
                if not last:
                    gather(U + 1, (s + 1) % 3)
                pool.wait_ge(oyA, U + 2)
                pool.wait_ge(oyB, U + 2)
                pool.sem_inc(pool_step, 1)
                pool.indirect_dma_start(yd.ap()[:, :],
                                        bass.IndirectOffsetOnAxis(ap=dst_i[s][:, 0:1].bitcast(U32), axis=0),
                                        oy[:, :], None, bounds_check=2 * S - 1, oob_is_err=False).then_inc(scattered, 16)

            pool.wait_ge(route_done, 1)
            pool.dma_start(fnb[:, :], fnw.rearrange("(a d) -> a d", a=1).broadcast_to([P, D])).then_inc(scattered, 16)
            passes(pool, unit, lambda U0: gather(U0, 0))

        @block.vector
        def _(dve):
            cnt = [0]

            def link(ins):
                cnt[0] += 1
                ins.then_inc(dve_self, 1)
                dve.wait_ge(dve_self, cnt[0])

            def v4(name):
                return psum(name)[:, :].rearrange("p (h n) -> p h n", h=NH)

            dve.wait_ge(ssx_done, 1)
            link(dve.reciprocal(rx, ssx))
            for t in range(T):
                dve.tensor_scalar(X0[:, t, :], X0[:, t, :], rx[:, t:t + 1], None, ALU.mult).then_inc(xn_done, 1)
            for c in range(KC):
                name = ("xT", c)
                dve.wait_ge(hhi_done, c + 1)
                j = dve.scalar_tensor_tensor(out=hLo[:, c, :], in0=psum(name)[:, :], scalar=PN1[:, c:c + 1],
                                             in1=hHi[:, c, :].bitcast(F32), op0=ALU.mult, op1=ALU.subtract)
                release(j, name)
                dve.wait_ge(free[BANK[name][0]], BANK[name][1] + 1)
                dve.sem_inc(hlo_done, 1)

            def evac(n):
                kind, what, _, _ = GROUPS[n]
                if what not in CONVN:
                    return
                for b in range(2):
                    name = ("y", n, b)
                    i = CONVN[what] + b
                    blk = tcol[what] + b
                    dve.wait_ge(tap0_done, i + 1)
                    a = cacc[i % 2]
                    for s in (1, 2, 3):
                        j = dve.scalar_tensor_tensor(out=a[:, s:S], in0=psum(name)[:, 0:S - s],
                                                     scalar=PCW[:, blk, 3 - s:4 - s], in1=a[:, s:S],
                                                     op0=ALU.mult, op1=ALU.add)
                        if s < 3:
                            link(j)
                    release(j, name)
                    dve.wait_ge(free[BANK[name][0]], BANK[name][1] + 1)
                    dve.sem_inc(conv_done, 1)

            def gates():
                dve.wait_ge(y_copied, 1)
                dve.wait_ge(z_in, 1)
                dtv = PDT[:, :].unsqueeze(1).broadcast_to([P, T, 4])
                fbv = PFB[:, :].unsqueeze(1).broadcast_to([P, T, 4])
                dve.tensor_tensor(z8[:, :, 0:4], GAB[:, :, 0:4], dtv, ALU.add)
                link(dve.tensor_tensor(hv[:, :, 4:8], FFT, fbv, ALU.add))
                link(dve.tensor_scalar(z8[:, :, 4:8], hv[:, :, 4:8], -1.0, None, ALU.mult))
                dve.scalar_tensor_tensor(out=az, in0=z8, scalar=-1.0, in1=z8, op0=ALU.mult, op1=ALU.max).then_inc(gexp_in, 1)
                dve.wait_ge(gexp_done, 1)
                link(dve.tensor_scalar(dd, e8, 2.0, None, ALU.add))
                link(dve.reciprocal(sv, dd))
                link(dve.tensor_tensor(sv, sv, e8, ALU.mult))
                link(dve.tensor_tensor(qv, sv, sv, ALU.mult))
                link(dve.tensor_scalar(hv, qv, 1.0 / 17, None, ALU.mult))
                for c in (15, 13, 11, 9, 7, 5, 3):
                    link(dve.scalar_tensor_tensor(out=hv, in0=hv, scalar=1.0 / c, in1=qv, op0=ALU.add, op1=ALU.mult))
                link(dve.scalar_tensor_tensor(out=hv, in0=hv, scalar=1.0, in1=sv, op0=ALU.add, op1=ALU.mult))
                link(dve.tensor_scalar(sp8, z8, 0.0, None, ALU.max))
                link(dve.scalar_tensor_tensor(out=sp8, in0=hv, scalar=2.0, in1=sp8, op0=ALU.mult, op1=ALU.add))
                link(dve.tensor_scalar(eb, eb, 1.0, None, ALU.add))
                dve.reciprocal(beta, eb)
                t3 = lambda a: a.rearrange("p (t n) -> p t n", t=T)
                link(dve.tensor_tensor(t3(gg), sp8[:, :, 0:4], ea.unsqueeze(1).broadcast_to([P, T, 4]), ALU.mult))
                dve.tensor_scalar(t3(lf), sp8[:, :, 4:8], -1.0, None, ALU.mult)
                dve.tensor_scalar(gg, gg, -1.0, None, ALU.mult).then_inc(gates_done, 1)

            def task(k):
                if k[0] == "evac":
                    evac(k[1])
                elif k[0] == "gates":
                    gates()
                elif k[0] == "gcum":
                    wait_full(dve, k)
                    dve.tensor_copy(cum, psum(k)[:, 0:48]).then_inc(cum_done, 1)
                    dve.wait_ge(cum_done, 1)
                    dve.tensor_scalar(c8, cum[:, 32:48], -float(HD ** 0.5), None, ALU.mult).then_inc(cum_done, 1)
                    release(dve.tensor_tensor(tl, cum[:, 16:32], cum[:, 0:16], ALU.subtract), k)
                    dve.wait_ge(free[BANK[k][0]], BANK[k][1] + 1)
                    dve.sem_inc(cum_done, 1)
                    dve.wait_ge(cexp_done, 1)
                    link(dve.tensor_tensor(bgc, beta, egc, ALU.mult))
                elif k[0] == "vt":
                    h = k[1]
                    wait_full(dve, k)
                    dve.wait_ge(gates_done, 1)
                    bv = beta.rearrange("p (t n) -> p t n", t=T)[:, :, h:h + 1].broadcast_to([P, T, P])
                    release(dve.tensor_tensor(vb[:, :, h, :], v4(k), bv, ALU.mult), k)
                    dve.wait_ge(free[BANK[k][0]], BANK[k][1] + 1)
                    dve.sem_inc(vb_done, 1)
                elif k[0] == "ss":
                    for h in range(NH):
                        n = NH * k[1] + h
                        dve.wait_ge(root_done, n + 1)
                        link(dve.reciprocal(nrm[n % 4][:, :], nrm[n % 4][:, :]))
                        dst = (kT if k[1] == 0 else qT)[:, h, :]
                        dve.tensor_tensor(dst, dst, nrm[n % 4][:, :], ALU.mult).then_inc(norm_done, 1)
                elif k[0] == "kt":
                    for h in range(NH):
                        name = ("kt", h)
                        wait_full(dve, name)
                        f = lambda a: a.rearrange("p (t n) -> p t n", t=T)[:, :, h:h + 1].broadcast_to([P, T, P])
                        dve.tensor_tensor(kbg[:, :, h, :], v4(name), f(bgc), ALU.mult)
                        release(dve.tensor_tensor(ktail[:, :, h, :], v4(name), f(etl), ALU.mult), name)
                        dve.wait_ge(free[BANK[name][0]], BANK[name][1] + 1)
                        dve.sem_inc(kt_done, 1)
                elif k[0] == "prep":
                    t = k[1]
                    i = t % 2
                    name = ("gcB", t)
                    wait_full(dve, name)
                    for h in range(NH):
                        j = dve.tensor_scalar(Dm[i][:, h, :], psum(name)[:, h * P:(h + 1) * P],
                                              cum[:, 4 * t + h:4 * t + h + 1], 0.0, ALU.subtract, ALU.min)
                    j.then_inc(d_raw, 1)
                    dve.wait_ge(ds_ready, t + 1)
                    wait_full(dve, ("KK", t))
                    release(dve.tensor_tensor(Nm[i][:, :, :], v4(("KK", t)), Ym[i][:, :, :], ALU.mult), ("KK", t))
                    b, n = BANK[("KK", t)]
                    dve.wait_ge(free[b], n + 1)
                    wait_full(dve, ("bB", t))
                    release(dve.tensor_tensor(Nm[i][:, :, :], Nm[i][:, :, :], v4(("bB", t)), ALU.mult), ("bB", t))
                    b, n = BANK[("bB", t)]
                    dve.wait_ge(free[b], n + 1)
                    dve.sem_inc(n_ready, 1)
                    dve.wait_ge(di_ready, t + 1)
                    wait_full(dve, ("QK", t))
                    release(dve.tensor_tensor(attnT[:, t, :, :], v4(("QK", t)), Dm[i][:, :, :], ALU.mult), ("QK", t))
                    b, n = BANK[("QK", t)]
                    dve.wait_ge(free[b], n + 1)
                    dve.sem_inc(attn_ready, 1)
                elif k[0] == "lv":
                    _, pr, lv = k
                    mask = nM[:, lv, :].unsqueeze(1).broadcast_to([P, NH, P])

                    def update(name, dst, in1, op, s):
                        wait_full(dve, name)
                        release(dve.tensor_tensor(dst, v4(name), in1, op), name)
                        b, n = BANK[name]
                        dve.wait_ge(free[b], n + 1)
                        dve.sem_inc(s, 1)

                    for i in range(2):
                        update(("Y", 2 * pr + i, lv), Ym[i][:, :, :], mask, ALU.mult, y_ready)
                    for i in range(2):
                        if lv < LEVELS - 1:
                            update(("Xp", 2 * pr + i, lv), Xm[i][:, :, :], Xm[i][:, :, :], ALU.add, x_ready)
                        update(("Up", 2 * pr + i, lv), Um[i][:, :, :], Um[i][:, :, :], ALU.add, u_ready)

            for g in range(GR_IN):
                for k in AFTER[g]:
                    task(k)
            dve.wait_ge(u0_ready, T)
            dve.sem_inc(uu_ready, 1)
            for k in range(KSTEPS):
                if k < 16:
                    h, t = FOX[k]
                    w = (t + 1) * P
                    name = ("fS", k)
                    wait_full(dve, name)
                    if k == 0:
                        dve.wait_ge(cB_done, 1)
                        dve.wait_ge(rot_done, 2)
                    if k >= 2:
                        dve.wait_ge(pf_ready, k - 1)
                    j = dve.tensor_tensor_reduce(out=Sx[k % 2][:, 0:w], in0=psum(name)[:, 0:w], in1=cB8[:, h, 0:w],
                                                 scale=1.0, scalar=-3.0e38, op0=ALU.add, op1=ALU.max,
                                                 accum_out=mx[:, k:k + 1])
                    release(j, name)
                    dve.wait_ge(free[BANK[name][0]], BANK[name][1] + 1)
                    dve.tensor_scalar(nmx[:, k:k + 1], mx[:, k:k + 1], -float(HD ** -0.5), None, ALU.mult).then_inc(sx_ready, 1)
                if k < 16:
                    n = k // 4
                    if k % 4 == 0 and n:
                        name = ("wS", n)
                        wait_full(dve, name)
                        release(dve.tensor_tensor(vb[:, n, :, :], v4(name), vb[:, n, :, :], ALU.add), name)
                        dve.wait_ge(free[BANK[name][0]], BANK[name][1] + 1)
                        dve.sem_inc(uu_ready, 1)
                    if k % 4 == 1:
                        for jj in range(T):
                            name = ("rS", n, jj)
                            wait_full(dve, name)
                            if n and jj == 0:
                                wait_full(dve, ("rO", n - 1))
                            release(dve.tensor_tensor(retP[:, POFF[jj]:POFF[jj] + PW[jj]], psum(name)[:, 0:PW[jj]],
                                                      dm[:, n, 0:PW[jj]], ALU.mult), name)
                            dve.wait_ge(free[BANK[name][0]], BANK[name][1] + 1)
                            dve.sem_inc(retP_done, 1)
                    if k % 4 == 2 and n < T - 1:
                        name = ("Sp", n)
                        wait_full(dve, name)
                        if n == 0:
                            j = dve.tensor_copy(St[:, :, :], v4(name))
                        else:
                            for h in range(NH):
                                j = dve.scalar_tensor_tensor(out=St[:, h, :], in0=St[:, h, :],
                                                             scalar=egl[:, 4 * n + h:4 * n + h + 1],
                                                             in1=psum(name)[:, h * P:(h + 1) * P],
                                                             op0=ALU.mult, op1=ALU.add)
                        release(j, name)
                        dve.wait_ge(free[BANK[name][0]], BANK[name][1] + 1)
                        dve.sem_inc(st_ready, 1)
                if k >= 2:
                    u = k - 2
                    h, t = FOX[u]
                    name = ("fO", u)
                    wait_full(dve, name)
                    link(dve.reciprocal(ri[:, u:u + 1], rs[:, u:u + 1]))
                    j = dve.tensor_scalar(mix[:, t, h * HD:(h + 1) * HD], psum(name)[:, 0:HD], ri[:, u:u + 1], None, ALU.mult)
                    release(j, name)
                    dve.wait_ge(free[BANK[name][0]], BANK[name][1] + 1)
                    dve.sem_inc(fox_done, 1)
            dve.wait_ge(sqr_done, 1)
            dve.tensor_reduce(ssn.rearrange("p (t h) -> p t h", t=T), gsq[:, :, :, :], AX_X, ALU.add).then_inc(ssr_done, 1)
            dve.wait_ge(sqr_done, 2)
            dve.tensor_reduce(ssx4.rearrange("p (t h) -> p t h", t=T),
                              osq[:, :, :].rearrange("p t (h n) -> p t h n", h=NH), AX_X, ALU.add).then_inc(ssr_done, 1)
            dve.wait_ge(rtr_done, 1)
            link(dve.reciprocal(rn, ssn))
            dve.wait_ge(zg_done, 1)
            for t in range(T):
                for h in range(NH):
                    m = mix[:, t, GW + h * P:GW + (h + 1) * P]
                    j = dve.scalar_tensor_tensor(out=m, in0=kbg[:, t, h, :], scalar=rn[:, 4 * t + h:4 * t + h + 1],
                                                 in1=m, op0=ALU.mult, op1=ALU.mult)
            j.then_inc(mix_done, 1)
            dve.wait_ge(rtr_done, 2)
            link(dve.reciprocal(ssx4, ssx4))
            o4 = oret[:, :, :].rearrange("p t (h n) -> p (t h) n", h=NH)
            j = dve.tensor_tensor(o4, o4, ssx4.unsqueeze(2).broadcast_to([P, 16, HD]), ALU.mult)
            j.then_inc(mix_done, 1)
            dve.wait_ge(mix_done, 2)
            dve.tensor_tensor(mix[:, :, 256:GW], oret[:, :, :], mix[:, :, 256:GW], ALU.mult).then_inc(mix_done, 1)
            dve.wait_ge(mix_done, 3)
            dve.sem_inc(slots_freed, 1)
            for c in range(KC):
                name = ("mT", c)
                dve.wait_ge(hhi_done, KC + c + 1)
                j = dve.tensor_tensor(hLo[:, c, :], psum(name)[:, :], hHi[:, c, :].bitcast(F32), ALU.subtract)
                release(j, name)
                dve.wait_ge(free[BANK[name][0]], BANK[name][1] + 1)
                dve.sem_inc(hlo_done, 1)
            dve.wait_ge(s_x2, 16 * T)
            for n in range(NOUT):
                for t in range(T):
                    name = ("y", NIN + n, t)
                    wait_full(dve, name)
                    xs = x2[:, t, n * 256:(n + 1) * 256]
                    release(dve.tensor_tensor(xs, psum(name)[:, 0:256], xs, ALU.add), name)
                    dve.wait_ge(free[BANK[name][0]], BANK[name][1] + 1)
                    dve.sem_inc(x2_done, 1)

            dve.sem_inc(slots_freed, 2)
            dve.wait_ge(ss2_done, 1)
            link(dve.reciprocal(r2, ss2))
            dve.wait_ge(s_n2, 48)
            for t in range(T):
                v = lambda a: a.rearrange("q (p c) -> q p c", c=KC)
                dve.scalar_tensor_tensor(out=h2[:, t, :].rearrange("q (c p) -> q p c", c=KC), in0=v(x2[:, t, :]),
                                         scalar=r2[:, t:t + 1], in1=v(n2b[:, :]), op0=ALU.mult, op1=ALU.mult).then_inc(h2_done, 1)
            bl = PRB[:, :]
            for t in range(T):
                name = ("lg", t)
                wait_full(dve, name)
                release(dve.tensor_tensor(LG[:, t, :], psum(name)[:, 0:NG + NE], bl, ALU.add), name)
                dve.wait_ge(free[BANK[name][0]], BANK[name][1] + 1)

            def top(src, desc, mx_, one, scratch, n):
                b = lambda a: a.unsqueeze(2).broadcast_to([P, T, n])
                link(dve.tensor_reduce(mx_, src, AX_X, ALU.max))
                link(dve.tensor_tensor(scratch, src, b(mx_), ALU.is_equal))
                link(dve.tensor_tensor(scratch, scratch, desc.unsqueeze(1).broadcast_to([P, T, n]), ALU.mult))
                link(dve.tensor_reduce(gmx, scratch, AX_X, ALU.max))
                link(dve.tensor_tensor(one, scratch, b(gmx), ALU.is_equal))

            gl, el = LG[:, :, 0:NG], LG[:, :, NG:]
            top(gl, const("gdesc"), gm, goh, ge, NG)
            dve.tensor_tensor(gd, gl, gm.unsqueeze(2).broadcast_to([P, T, NG]), ALU.subtract).then_inc(rexp_in, 1)
            link(dve.tensor_scalar(pen, goh, -1.0, -NEG, ALU.add, ALU.mult))
            e4 = lambda a: a.rearrange("p t (g e) -> p t g e", g=NG)
            for t in range(T):
                j = dve.tensor_tensor(ml[:, t, :].rearrange("p (g e) -> p g e", g=NG),
                                      el[:, t, :].rearrange("p (g e) -> p g e", g=NG),
                                      pen[:, t, :].unsqueeze(2).broadcast_to([P, NG, EG]), ALU.add)
            link(j)
            top(ml, const("desc"), m1, oh1, t32, NE)
            link(dve.scalar_tensor_tensor(out=ml, in0=oh1, scalar=3 * NEG, in1=ml, op0=ALU.mult, op1=ALU.add))
            top(ml, const("desc"), m2, oh2, t32, NE)
            dve.tensor_tensor(mm1, m2, m1, ALU.subtract).then_inc(rexp_in, 1)
            dve.tensor_tensor(M32, oh1, oh2, ALU.add).then_inc(m_done, 1)
            dve.wait_ge(m_done, 1)
            link(dve.tensor_tensor(t32, M32, const("tok1").unsqueeze(2).broadcast_to([P, T, NE]), ALU.mult))
            dve.scalar_tensor_tensor(out=Wt, in0=oh2, scalar=float(S), in1=t32, op0=ALU.mult, op1=ALU.add)
            dve.wait_ge(rexp_done, 1)
            link(dve.tensor_reduce(gsum, gd, AX_X, ALU.add))
            link(dve.reciprocal(gp, gsum))
            dve.wait_ge(rexp_done, 2)
            link(dve.tensor_scalar(den, e2, 1.0, None, ALU.add))
            link(dve.reciprocal(den, den))
            link(dve.tensor_tensor(gate0, gp, den, ALU.mult))
            dve.tensor_tensor(gate1, gate0, e2, ALU.mult)
            name = ("rank",)
            wait_full(dve, name)
            dve.tensor_copy(rank, psum(name)[:, 0:T * NE].rearrange("p (t n) -> p t n", t=T))
            link(dve.tensor_reduce(cmax, psum(name)[:, T * NE:(T + 1) * NE], AX_X, ALU.max))
            link(dve.tensor_scalar(t8, const("thr"), cmax, None, ALU.is_lt))
            link(dve.tensor_reduce(npf, t8, AX_X, ALU.add))
            for one_ahead in (idx_full, idx_ready, xt_full, xt_ready, up_full, hid_ready, ht_full, ht_ready, oyA, oyB):
                dve.sem_inc(one_ahead, 1)
            dve.tensor_copy(npi[:, :], npf).then_inc(route_done, 1)

            def entries(U, q, s):
                dve.wait_ge(idx_full, U + 1)
                ev = lambda a: a[:, :, bass.ds(q * 2, 2)] if not isinstance(q, int) else a[:, :, 2 * q:2 * q + 2]
                b = lambda a: ev(a).unsqueeze(3).broadcast_to([P, T, 2, CAP])
                it = const("iota").unsqueeze(1).broadcast_to([P, 2 * T, CAP]).rearrange("p (t e) n -> p t e n", t=T)
                link2(dve.tensor_tensor(sel[:, :, :, :], it, b(rank), ALU.is_equal), U * 3 + 1)
                dve.tensor_tensor(selw[:, :, :, :], sel[:, :, :, :], b(Wt), ALU.mult).then_inc(sel_ready, 1)
                dve.wait_ge(idx_full, U + 2)
                link2(dve.tensor_scalar(emp[:, :], pb[0][:, 0:1], 0.0, 4.0 * 2 * S, ALU.is_equal, ALU.mult), U * 3 + 2)
                link2(dve.scalar_tensor_tensor(out=dst_i[s][:, :], in0=pb[0][:, 0:1], scalar=-1.0, in1=emp[:, :],
                                               op0=ALU.add, op1=ALU.add), U * 3 + 3)
                dve.tensor_scalar(tok_i[s][:, :], dst_i[s][:, :], S - 1, None, ALU.bitwise_and).then_inc(idx_ready, 1)

            def link2(ins, n):
                ins.then_inc(loop_self, 1)
                dve.wait_ge(loop_self, n)

            def unit(U, q, s, use, last):
                if not last:
                    entries(U + 1, q + 1, (s + 1) % 3)
                dve.wait_ge(sa_ready, U + 1)
                dve.wait_ge(ht_full, U + 1)
                v = lambda a: a.rearrange("q (p c) -> q p c", c=2)
                dve.tensor_tensor(hid[:, :, :].rearrange("q c p -> q p c"), v(sa[:, :]), v(pb[3][:, FF:2 * FF]),
                                  ALU.mult).then_inc(hid_ready, 1)
                dve.wait_ge(slots_freed, U + 4)
                dve.wait_ge(scattered, U * 16 + 16)
                dve.tensor_copy(oy[:, 0:512], pb[5][:, :]).then_inc(oyA, 1)

            def stop(p):
                dve.tensor_scalar(rank, rank, -float(CAP), None, ALU.add).then_inc(next_rank, 1)
                dve.wait_ge(next_rank, p + 1)

            dve.wait_ge(s_h2d, 16 * T)
            passes(dve, unit, lambda U0: entries(U0, 0, 0), stop)
            dve.wait_ge(scattered, 16)
            for t in range(T):
                dve.wait_ge(s_y[t], 16)
                link(dve.scalar_tensor_tensor(out=x2[:, t, :], in0=yt[t][:, 0, :], scalar=gate0[:, t:t + 1],
                                              in1=x2[:, t, :], op0=ALU.mult, op1=ALU.add))
                dve.scalar_tensor_tensor(out=yt[t][:, 0, :], in0=yt[t][:, 1, :], scalar=gate1[:, t:t + 1],
                                         in1=x2[:, t, :], op0=ALU.mult, op1=ALU.add).then_inc(acc_done, 1)
            for t in range(T):
                dve.wait_ge(ssf_done, 2 * t + 2)
                link(dve.reciprocal(rf[:, t:t + 1], ssf[:, t:t + 1]))
                dve.scalar_tensor_tensor(out=x2[:, t, :], in0=yt[t][:, 0, :], scalar=rf[:, t:t + 1], in1=fnb[:, :],
                                         op0=ALU.mult, op1=ALU.mult).then_inc(fin_done, 1)


_INS = ["x", "norm1_w", "w_in", "fox_forget_bias", "gdn_conv_w", "gdn_a_log", "gdn_dt_bias", "gdn_norm_w", "w_out",
        "norm2_w", "router_group_w", "router_group_b", "router_expert_w", "router_expert_b",
        "expert_w1", "expert_w3", "expert_w2", "final_norm_w"]
_OUTS = [((1, S, D), "float32")]


def kernel(**inputs):
    import numpy as _np
    import concourse.bacc as _bacc
    from concourse import mybir as _mybir
    from concourse.bass_utils import run_bass_kernel_spmd as _run

    nc = _bacc.Bacc("TRN2", target_bir_lowering=False, num_devices=1)
    table = constant_table()
    arrays = {"const_dram": table}
    args = [nc.dram_tensor("const_dram", table.shape, _mybir.dt.from_np(table.dtype), kind="ExternalInput").ap()]
    for name in _INS:
        a = _np.ascontiguousarray(inputs[name])
        arrays[f"in_{name}_dram"] = a
        args.append(nc.dram_tensor(f"in_{name}_dram", a.shape, _mybir.dt.from_np(a.dtype), kind="ExternalInput").ap())
    for i, (shape, dtype) in enumerate(_OUTS):
        dt = _mybir.dt.from_np(_np.dtype(dtype))
        args.append(nc.dram_tensor(f"out_{i}_dram", shape, dt, kind="ExternalOutput").ap())
    build(nc, *args)
    r = _run(nc, [arrays], core_ids=[0])
    return r.results[0]["out_0_dram"]
```

```python
from contextlib import ExitStack
import math

import numpy as np

import concourse.bass as bass
from concourse import mybir

F32 = mybir.dt.float32
F32R = mybir.dt.float32r
I32 = mybir.dt.int32
U32 = mybir.dt.uint32
ACT = mybir.ActivationFunctionType
ALU = mybir.AluOpType
AX_X = mybir.AxisListType.X

P = 128
D = 1024
S = 512
T = S // P
KC = D // P
HK = KC // 2
NH = 4
HD = 64
GW = NH * P
EPS = 1e-6
NG = 4
EG = 8
NE = NG * EG
FF = 256
CAP = 64
PAIRS = NE // 2
NEG = -1e30
LEVELS = 6

FQ, FK, FV, FFG = 0, 256, 512, 768
RQ, RK, RV, RG = 772, 1028, 1284, 1540
GQ, GK, GV, GZ, GA, GB = 1796, 2308, 2820, 3332, 3844, 3848
WMAX = 260

GROUPS = [("n", "zb", GZ + 260, 260), ("n", "fv", FV, 260),
          ("t", "v0", GV, 256), ("t", "v1", GV + 256, 256), ("t", "k0", GK, 256), ("t", "k1", GK + 256, 256),
          ("t", "q0", GQ, 256), ("t", "q1", GQ + 256, 256),
          ("n", "rq", RQ, 256), ("n", "rk", RK, 256), ("n", "rv", RV, 256), ("n", "za", GZ, 260), ("n", "rg", RG, 256),
          ("t", "fq", FQ, 256), ("t", "fk", FK, 256)]
GIDX = {g[1]: i for i, g in enumerate(GROUPS)}
NIN = len(GROUPS)
NOUT = 4
GR_IN = 2 * NIN
GR = GR_IN + 2 * NOUT

AFTER = {g: [] for g in range(GR_IN)}
for _i in range(NIN):
    AFTER[2 * _i + 1].append(("evac", _i))
AFTER[3].append(("gates",))
AFTER[5].append(("gcum",))
AFTER[6] += [("vt", 0), ("vt", 1)]
AFTER[7].append(("cB",))
AFTER[8] += [("vt", 2), ("vt", 3)]
AFTER[12].append(("ss", 0))
AFTER[16] += [("ss", 1), ("kt",)]
AFTER[17] += [("prep", 0), ("prep", 1)]
AFTER[18].append(("xt", 0))
for _i in range(LEVELS):
    AFTER[18 + _i].append(("lv", 0, _i))
AFTER[24] += [("fin", 0), ("prep", 2), ("prep", 3)]
AFTER[25].append(("xt", 1))
for _i in range(LEVELS - 1):
    AFTER[25 + _i].append(("lv", 1, _i))
AFTER[29] += [("lv", 1, LEVELS - 1), ("fin", 1)]

FOX = [(u // T, u % T) for u in range(NH * T)]
KSTEPS = len(FOX) + 2
WS = {3 * n: n for n in range(1, T)}
OO = {3 * n + 1: n for n in range(T)}
RS = {3 * n + 2: n for n in range(NH)}
RO = {3 * n + 3: n for n in range(NH)}
MT = [2, 3, 0, 1, 4, 5, 6, 7]
PW = [S - j * P for j in range(T)]
POFF = [sum(PW[:j]) for j in range(T)]


def tensor_orders():
    a, b = [("par",)] + [("xT", t, i) for t in range(T) for i in range(2)], []
    for g in range(GR_IN):
        if g % 2 == 0:
            kind = GROUPS[g // 2][0]
            a += [("y", g // 2, n) for n in range(T if kind == "n" else 2)]
        for task in AFTER[g]:
            if task[0] == "vt":
                b.append(task)
            elif task[0] == "gcum":
                b.append(task)
            elif task[0] == "cB":
                b += [("cB", h) for h in range(NH)]
            elif task[0] == "ss":
                b.append(task)
            elif task[0] == "kt":
                b += [("kt", h) for h in range(NH)]
            elif task[0] == "prep":
                b += [(n, task[1]) for n in ("gcB", "bB", "KK", "QK")]
            elif task[0] == "xt":
                b += [("XT", 2 * task[1]), ("XT", 2 * task[1] + 1)]
            elif task[0] == "lv":
                _, pr, lv = task
                b += [("Y", 2 * pr, lv), ("Y", 2 * pr + 1, lv)]
                if lv:
                    b += [("UT", 2 * pr, lv), ("UT", 2 * pr + 1, lv)]
                b += [("Xp" if lv < LEVELS - 1 else "Up", 2 * pr + i, lv) for i in range(2)]
            elif task[0] == "fin":
                for t in (2 * task[1], 2 * task[1] + 1):
                    b += [("wT", t), ("u0", t)]
    b += [("rT", i) for i in range(4)]
    for k in range(KSTEPS):
        if k < 16:
            a.append(("fS", k))
        if 1 <= k <= 16:
            a.append(("fT", k - 1))
        if k >= 2:
            a.append(("fO", k - 2))
        if k in WS:
            b.append(("wS", WS[k]))
        if k in OO:
            b.append(("o", OO[k]))
            if OO[k] < T - 1:
                b.append(("Sp", OO[k]))
        if k in RS:
            b += [("rS", RS[k], j) for j in range(T)]
        if k in RO:
            b.append(("rO", RO[k]))
    a += [("mT", c) for c in MT]
    for n in range(NOUT):
        a += [("y", NIN + n, t) for t in range(T)]
    for t in range(T):
        b += [("hT", t, 0), ("hT", t, 1), ("lg", t)]
    b += [("rank",)]
    return a, b


ORDER_A, ORDER_B = tensor_orders()
BANK = {}
for _base, _order in ((0, ORDER_A), (4, ORDER_B)):
    for _i, _name in enumerate(_order):
        BANK[_name] = (_base + _i % 4, _i // 4)

CONST = {}
_at = 0
for _name, _n in [("ident", P), ("eps", 1), ("eps128", 1), ("ones", P), ("iota", CAP), ("tok1", T), ("thr", 8),
                  ("desc", NE), ("gdesc", NG), ("rankm", P), ("tri", P), ("strict", P), ("negmask", P), ("nM1", P),
                  ("cos", T * 32), ("sin", T * 32), ("nM", LEVELS * P), ("dm", NH * S)]:
    CONST[_name] = (_at, _n)
    _at += _n
NCONST = _at
NSTAY = CONST["tri"][0]


def constant_table():
    c = np.zeros((P, NCONST), np.float32)

    def put(name, v):
        a, n = CONST[name]
        c[:, a:a + n] = np.asarray(v, np.float32).reshape(P, n)

    r = np.arange(P)
    row, col = r[:, None], r[None, :]
    put("tri", row <= col)
    put("rankm", row < col)
    put("ident", row == col)
    put("strict", row < col)
    put("ones", np.ones((P, P)))
    put("negmask", np.where(col > row, NEG, 0.0))
    put("nM1", -((row % 2 == 0) & (col == row + 1)).astype(np.float32))
    lv = []
    for n in range(LEVELS):
        b = 2 << n
        lv.append(-((row // (2 * b) == col // (2 * b)) & (row % (2 * b) >= b) & (col % (2 * b) < b)).astype(np.float32))
    put("nM", np.stack(lv, 1))
    dm = []
    for h in range(NH):
        rel = np.arange(S)[None, :] - row
        dm.append(np.where(rel >= 0, np.exp(np.maximum(rel, 0) * math.log1p(-(2.0 ** (-5 - h)))), 0.0) * HD ** -0.5)
    put("dm", np.stack(dm, 1))
    lin = (np.arange(HD // 2, dtype=np.float32) / np.float32(HD // 2 - 1)).astype(np.float32)
    inv = (np.float32(1.0) / np.power(np.float32(10000.0), lin).astype(np.float32)).astype(np.float32)
    pos = (np.arange(T)[None, :] * P + row).astype(np.float32)
    ang = (pos[:, :, None] * inv[None, None, :]).astype(np.float32).astype(np.float64)
    put("cos", np.cos(ang))
    put("sin", np.sin(ang))
    put("iota", np.tile(np.arange(CAP), (P, 1)))
    put("tok1", pos + 1)
    put("thr", np.tile(np.arange(8) * CAP, (P, 1)))
    put("desc", np.tile(NE - np.arange(NE), (P, 1)))
    put("gdesc", np.tile(NG - np.arange(NG), (P, 1)))
    put("eps", np.full((P, 1), EPS))
    put("eps128", np.full((P, 1), EPS * P))
    return c


def build(nc, consts, x, n1w, w_in, foxb, convw, alog, dtb, gnw, w_out, n2w, rgw, rgb, rew, reb,
          ew1, ew3, ew2, fnw, out):
    KB = 1024
    BASE = 16512
    C0 = 0
    R1 = 17 * KB
    R2 = R1 + 32 * KB
    RM = R2 + 29 * KB
    R7 = RM + 16 * KB
    R8 = R7 + 12 * KB
    R9 = R8 + 12 * KB
    R5 = R9 + 20 * KB
    R4 = R5 + 8 * KB
    R3 = R4 + 20 * KB
    with ExitStack() as ctx:
        def at(name, shape, offset, dt=F32):
            return nc.alloc_sbuf_tensor_at(name, shape, dt, offset=BASE + offset)

        def sem(name):
            return ctx.enter_context(nc.semaphore(name))

        arena = ctx.enter_context(nc.sbuf_tensor("arena", [P, (229344 - BASE) // 4 - 16], F32))
        CT = at("CT", [P, NCONST], C0)

        def const(name, *dims):
            a, n = CONST[name]
            v = CT[:, a:a + n]
            return v if not dims else v.rearrange(dims[0], **dims[1])

        tri, ident, strict, negmask = const("tri"), const("ident"), const("strict"), const("negmask")
        ones, eps = const("ones"), const("eps")
        nM = const("nM", "p (l n) -> p l n", dict(l=LEVELS))
        dm = const("dm", "p (h n) -> p h n", dict(h=NH))
        cosT = const("cos", "p (t n) -> p t n", dict(t=T))
        sinT = const("sin", "p (t n) -> p t n", dict(t=T))

        q0 = 17 * KB - 992
        assert NCONST * 4 <= q0 - 64
        PDT = at("PDT", [P, 4], q0 + 32)
        PAL = at("PAL", [P, 4], q0 + 64)
        PFB = at("PFB", [P, 4], q0 + 96)
        PRB = at("PRB", [P, NG + NE], q0 + 128)
        PCW = at("PCW", [P, 4, 12], q0 + 288)
        PGN = at("PGN", [P, P], q0 + 480)
        assert q0 + 480 + 512 <= R1
        hHi = at("hHi", [P, KC, S], R1, F32R)
        hLo = at("hLo", [P, KC, S], R1 + 16 * KB, F32R)
        gsz = HK * WMAX * 4
        raw = [at(f"raw{i}", [P, HK, WMAX], R2 + i * gsz) for i in range(3)]
        whi = [at(f"whi{i}", [P, HK, WMAX], R2 + (3 + i) * gsz, F32R) for i in range(2)]
        wlo = [at(f"wlo{i}", [P, HK, WMAX], R2 + (5 + i) * gsz, F32R) for i in range(2)]
        assert 7 * gsz <= 29 * KB
        X0 = at("X0", [P, T, D], RM)
        mix = at("mix", [P, T, D], RM)
        rq = at("rq", [P, T, 256], R7)
        rk = at("rk", [P, T, 256], R7 + 4 * KB)
        rv = at("rv", [P, T, 256], R7 + 8 * KB)
        oret = at("oret", [P, T, 256], R7)
        osq = at("osq", [P, T, 256], R7 + 4 * KB)
        fqT = at("fqT", [P, 2, S], R8)
        fkT = at("fkT", [P, 2, S], R8 + 4 * KB)
        fv = at("fv", [P, T, 256], R8 + 8 * KB)
        cB8 = at("cB8", [P, NH, S], R9)
        n1b = at("n1b", [P, D], R9 + 12 * KB)
        PW48 = at("PW48", [4 * 12, P], R9)
        rqs = at("rqs", [P, 16], q0 - 64)
        junk = at("junk", [P, D], R9 + 8 * KB)
        cacc = [at(f"cacc{i}", [P, S], R9 + (8 + 2 * i) * KB) for i in range(2)]
        vS = [at(f"vS{i}", [P, S], R9 + (12 + 2 * i) * KB) for i in range(2)]
        nrm = [at(f"nrm{i}", [P, S], R4 + 2 * i * KB) for i in range(4)]
        rtmp = [at(f"rtmp{i}", [P, T, NH, 32], R9 + (8 + 2 * i) * KB) for i in range(4)]
        Sx = [at(f"Sx{i}", [P, S], R9 + (8 + 2 * i) * KB) for i in range(2)]
        Pf = [at(f"Pf{i}", [P, S], R9 + (12 + 2 * i) * KB) for i in range(2)]
        PT = [at(f"PT{i}", [P, T, P], R9 + (16 + 2 * i) * KB) for i in range(2)]
        small = at("small", [P, 1024], R9 + 16 * KB)
        attnT = at("attnT", [P, T, NH, P], R5)
        def pair(name, slot):
            return [at(f"{name}{i}", [P, NH, P], R4 + (slot * 2 + i) * 2 * KB) for i in range(2)]
        Nm, Xm, Um, Ym, Dm = (pair(n, i) for i, n in enumerate(("Nm", "Xm", "Um", "Ym", "Dm")))
        rqT = at("rqT", [P, 2, S], R4)
        rkT = at("rkT", [P, 2, S], R4 + 4 * KB)
        retP = at("retP", [P, sum(PW)], R4 + 8 * KB)
        St = at("St", [P, NH, P], R4 + 18 * KB)
        qT = at("qT", [P, NH, S], R3)
        kT = at("kT", [P, NH, S], R3 + 8 * KB)
        vb = at("vb", [P, T, NH, P], R3 + 16 * KB)
        kbg = at("kbg", [P, T, NH, P], R3 + 24 * KB)
        ktail = at("ktail", [P, T, NH, P], R3 + 32 * KB)
        gsq = [at(f"gsq{t}", [P, NH, P], R3 + (8 + 2 * t) * KB) for t in range(T)]
        sm0 = -(-(R2 + 7 * gsz) // 32) * 32
        keep = at("keep", [P, 136], sm0)
        assert sm0 + 544 <= RM
        ssx, rx = keep[:, 0:4], keep[:, 4:8]
        egl = keep[:, 8:24]
        mx, nmx, rs, ri = keep[:, 24:40], keep[:, 40:56], keep[:, 56:72], keep[:, 72:88]
        ssn, rn, ssx4 = keep[:, 88:104], keep[:, 104:120], keep[:, 120:136]
        def sml(a, n):
            return small[:, a:a + n]
        GAB = sml(0, 32).rearrange("p (t n) -> p t n", t=T)
        FFT = sml(32, 16).rearrange("p (t n) -> p t n", t=T)
        z8 = sml(48, 32).rearrange("p (t n) -> p t n", t=T)
        az, e8, dd, sv, qv, hv = (sml(80 + 32 * i, 32).rearrange("p (t n) -> p t n", t=T) for i in range(6))
        eb, beta, gg, ea = sml(272, 16), sml(288, 16), sml(304, 16), sml(320, 4)
        cum = sml(336, 48)
        c8, egc, tl, etl, bgc, sp8 = sml(384, 16), sml(400, 16), sml(416, 16), sml(432, 16), sml(448, 16), sml(464, 32)
        sp8 = sp8.rearrange("p (t n) -> p t n", t=T)
        lf = sml(496, 16)
        ssk, ssq, rks, br, bgr, etr = (sml(512 + 16 * i, 16) for i in range(6))

        pb = [ctx.enter_context(nc.psum_tensor(f"bank{i}", [P, 512], F32)) for i in range(8)]

        full = [sem(f"full{i}") for i in range(8)]
        free = [sem(f"free{i}") for i in range(8)]
        s_const = sem("s_const"); s_const2 = sem("s_const2"); s_n1 = sem("s_n1"); s_cw = sem("s_cw"); par_done = sem("par_done"); s_par = sem("s_par")
        s_x = [sem(f"s_x{t}") for t in range(T)]
        raw_full = [sem(f"raw_full{i}") for i in range(3)]
        whi_done = sem("whi_done"); wlo_done = sem("wlo_done"); gran_used = sem("gran_used")
        ssx_done = sem("ssx_done"); xn_done = sem("xn_done"); hhi_done = sem("hhi_done"); hlo_done = sem("hlo_done")
        act_self = sem("act_self"); dve_self = sem("dve_self"); pool_self = sem("pool_self")
        tap0_done = sem("tap0_done"); conv_done = sem("conv_done"); silu_done = sem("silu_done")
        z_in = sem("z_in"); gexp_in = sem("gexp_in"); gexp_done = sem("gexp_done"); gates_done = sem("gates_done")
        cum_done = sem("cum_done"); cexp_done = sem("cexp_done"); cfac_done = sem("cfac_done")
        vb_done = sem("vb_done"); cB_done = sem("cB_done")
        sq_done = sem("sq_done"); root_done = sem("root_done"); ss_read = sem("ss_read"); kt_done = sem("kt_done")
        d_raw = sem("d_raw"); e_ready = sem("e_ready"); d_exp = sem("d_exp"); ds_ready = sem("ds_ready")
        di_ready = sem("di_ready"); qg_ready = sem("qg_ready"); n_ready = sem("n_ready"); attn_ready = sem("attn_ready")
        uinit = sem("uinit"); xinit = sem("xinit"); y_ready = sem("y_ready"); x_ready = sem("x_ready"); u_ready = sem("u_ready")
        w_ready = sem("w_ready"); u0_ready = sem("u0_ready")
        y_copied = sem("y_copied")
        rot_done = sem("rot_done"); rT_done = sem("rT_done"); retP_done = sem("retP_done"); oret_done = sem("oret_done")
        uu_ready = sem("uu_ready"); st_ready = sem("st_ready"); og_done = sem("og_done")
        sx_ready = sem("sx_ready"); pf_ready = sem("pf_ready"); pt_ready = sem("pt_ready"); fox_done = sem("fox_done")
        zg_done = sem("zg_done"); sqr_done = sem("sqr_done"); ssr_done = sem("ssr_done"); rtr_done = sem("rtr_done")
        mixr_done = sem("mixr_done"); mixg_done = sem("mixg_done"); rk_done = sem("rk_done"); silu2_done = sem("silu2_done"); s_x2 = sem("s_x2in"); x2_done = sem("x2_done")
        s_out = sem("s_out")

        def psum(name):
            return pb[BANK[name][0]]

        def wait_full(e, name):
            b, n = BANK[name]
            e.wait_ge(full[b], n + 1)

        def release(ins, name):
            return ins.then_inc(free[BANK[name][0]], 1)

        tcol = {"v0": 8, "v1": 10, "k0": 4, "k1": 6, "q0": 0, "q1": 2}
        CONVN = {"v0": 0, "v1": 2, "k0": 4, "k1": 6, "q0": 8, "q1": 10}
        x2 = at("x2", [P, T, D], R3)

        SLOT = [113 * KB, 17 * KB, 65 * KB]
        h2T = at("h2T", [P, KC, P], 161 * KB)
        h2 = at("h2", [P, T, D], R3 + 16 * KB)
        rtA = at("rtA", [P, 1024], R3 + 32 * KB)
        n2b = at("n2b", [P, D], R3 + 36 * KB)
        rtB = at("rtB", [P, 1024], R3 + 36 * KB)
        fnb = at("fnb", [P, D], SLOT[0] + 36 * KB)
        rw = at("rw", [P, KC, NG + NE], R3 + 40 * KB)
        assert R3 + 40 * KB + KC * (NG + NE) * 4 <= 229344 - BASE
        w13 = [at(f"w13_{i}", [P, 2, 2, KC * FF], SLOT[i]) for i in range(3)]
        w2 = [at(f"w2_{i}", [P, 2, 2 * D], SLOT[i] + 32 * KB) for i in range(3)]
        xT = at("xT", [P, KC, P], 161 * KB)
        xg = [at(f"xg{i}", [P, D], R3 + (16 + 4 * i) * KB) for i in range(3)]
        oy0 = C0 + -(-NSTAY * 4 // 32) * 32
        oy = [at(f"oy{i}", [P, D], oy0 + 4 * i * KB) for i in range(3)]
        assert oy0 + 12 * KB <= q0
        sa = at("sa", [P, FF], R3 + 28 * KB)
        hid = at("hid", [P, 2, P], R3 + 29 * KB)
        hidT = at("hidT", [P, 2, P], R3 + 30 * KB)
        sel = at("sel", [P, T, 2, CAP], R3 + 36 * KB)
        selw = at("selw", [P, T, 2, CAP], R3 + 38 * KB)
        emp = at("emp", [P, 1], R3 + 31 * KB)
        dst_i = [at(f"dst{i}", [P, 1], R3 + 31 * KB + 32 * (i + 1), I32) for i in range(3)]
        tok_i = [at(f"tok{i}", [P, 1], R3 + 31 * KB + 32 * (i + 4), I32) for i in range(3)]
        dsts = at("dsts", [P, PAIRS], R3 + 31 * KB + 256, I32)
        yt = [at(f"yt{i}", [P, 2, D], SLOT[0] + 8 * KB * i) for i in range(T)]
        jk = at("jk", [P, D], SLOT[0] + 32 * KB)
        rv4 = lambda a, n, w: (rtA if n == 0 else rtB)[:, a:a + T * w].rearrange("p (t n) -> p t n", t=T)
        Wt, rank, oh1, oh2, LG = rv4(0, 0, NE), rv4(128, 0, NE), rv4(256, 0, NE), rv4(384, 0, NE), rv4(512, 0, NG + NE)
        r1 = lambda i: rtA[:, 656 + 4 * i:660 + 4 * i]
        gm, gmx, gsum, gp, m1, m2, mm1, e2, den, gate0, gate1, ss2, r2, ssf, rf = (r1(i) for i in range(15))
        cmax = rtA[:, 720:721]
        npf = rtA[:, 721:722]
        npi = at("npi", [P, 1], R3 + 32 * KB + 4 * 736, I32)
        ml, t32, M32, ge = rv4(0, 1, NE), rv4(128, 1, NE), rv4(256, 1, NE), rv4(384, 1, NG)
        goh, gd, pen, t8 = rv4(400, 1, NG), rv4(416, 1, NG), rv4(432, 1, NG), rtB[:, 448:456]

        h2d = nc.dram_tensor("h2d", [S, D], F32, kind="Internal")
        yd = nc.dram_tensor("yd", [2 * S, D], F32, kind="Internal")
        w1v = ew1[0].rearrange("g e (p c) f -> (g e) p (c f)", c=KC)
        w3v = ew3[0].rearrange("g e (p c) f -> (g e) p (c f)", c=KC)
        w2v = ew2[0].rearrange("g e (p c) d -> (g e) p (c d)", c=2)
        outv = out[0].rearrange("(t p) d -> t p d", p=P)

        s_n2 = sem("s_n2"); ss2_done = sem("ss2_done"); h2_done = sem("h2_done"); s_h2d = sem("s_h2d")
        hT_done = sem("hT_done"); lg_done = sem("lg_done"); rexp_in = sem("rexp_in"); rexp_done = sem("rexp_done")
        m_done = sem("m_done"); route_done = sem("route_done")
        slots_freed = sem("slots_freed")
        w13_full = [sem(f"w13_full{i}") for i in range(3)]
        w2_full = [sem(f"w2_full{i}") for i in range(3)]
        sel_ready = sem("sel_ready"); idx_full = sem("idx_full"); idx_ready = sem("idx_ready"); gathered = [sem(f"gathered{i}") for i in range(3)]
        xt_full = sem("xt_full"); xt_ready = sem("xt_ready"); up_full = sem("up_full"); sa_ready = sem("sa_ready"); loop_self = sem("loop_self"); next_rank = sem("next_rank"); pool_step = sem("pool_step")
        hid_ready = sem("hid_ready"); ht_full = sem("ht_full"); ht_ready = sem("ht_ready")
        oyA = sem("oyA"); oyB = sem("oyB"); scattered = [sem(f"scattered{i}") for i in range(3)]; s_fn = sem("s_fn")
        s_y = [sem(f"s_y{t}") for t in range(T)]
        acc_done = sem("acc_done"); ssf_done = sem("ssf_done"); fin_done = sem("fin_done")

        def passes(e, unit, start=None, stop=None):
            e.wait_ge(route_done, 1)
            n = e.value_load(npi[0:1, 0:1], min_val=1, max_val=S // CAP)
            with e.Fori(0, n) as p:

                def of(i, s):
                    n0, n12 = p * 6 + i, p * 5 + i
                    return p * PAIRS + i * 3 + s, i * 3 + s, s, n12 if s else n0, n0 + 1 if s == 2 else n12

                if start is not None:
                    start(p)
                with e.Fori(0, 4) as i:
                    for s in range(3):
                        unit(*of(i, s), True, True)
                unit(*of(4, 0), True, True)
                unit(*of(4, 1), False, True)
                unit(*of(4, 2), False, True)
                unit(*of(5, 0), False, False)
                if stop is not None:
                    stop(p)

        block = ctx.enter_context(nc.Block())

        @block.sync
        def _(sp):
            for t in range(T):
                sp.dma_start(X0[:, t, :], x[0, t * P:(t + 1) * P, :]).then_inc(s_x[t], 16)
                if t == 0:
                    sp.dma_start(CT[:, 0:NSTAY], consts[:, 0:NSTAY]).then_inc(s_const, 16)
                    sp.dma_start(n1b[:, :], n1w[0:1, :].broadcast_to([P, D])).then_inc(s_n1, 16)

            def granule(g):
                if g >= 3:
                    sp.wait_ge(wlo_done, g - 2)
                if g < GR_IN:
                    _, _, c0, w = GROUPS[g // 2]
                    src = w_in[0]
                else:
                    c0, w = 256 * ((g - GR_IN) // 2), 256
                    src = w_out[0]
                k0 = (g % 2) * HK * P
                sp.dma_start(raw[g % 3][:, :, 0:w],
                             src[k0:k0 + HK * P, c0:c0 + w].rearrange("(c p) n -> p c n", p=P)
                             ).then_inc(raw_full[g % 3], 16)

            for g in range(3):
                granule(g)
            sp.dma_start(CT[:, NSTAY:], consts[:, NSTAY:]).then_inc(s_const2, 16)
            for g in range(3, GR_IN + 4):
                granule(g)
            sp.wait_ge(mixg_done, NH)
            for t in range(T):
                sp.dma_start(x2[:, t, :], x[0, t * P:(t + 1) * P, :]).then_inc(s_x2, 16)
            sp.dma_start(n2b[:, :], n2w[0:1, :].broadcast_to([P, D])).then_inc(s_n2, 16)
            sp.dma_start(rw[:, :, 0:NG], rgw[0].rearrange("(p c) g -> p c g", c=KC)).then_inc(s_n2, 16)
            sp.dma_start(rw[:, :, NG:], rew[0].rearrange("(p c) g -> p c g", c=KC)).then_inc(s_n2, 16)
            for g in range(GR_IN + 4, GR):
                granule(g)

            def load(U, q, s, behind=3):
                sp.wait_ge(slots_freed, U + 4 - behind)
                es = bass.ds(q * 2, 2) if not isinstance(q, int) else slice(2 * q, 2 * q + 2)
                sp.dma_start(w13[s][:, :, 0, :], w1v[es].rearrange("e p n -> p e n")).then_inc(w13_full[s], 16)
                sp.dma_start(w13[s][:, :, 1, :], w3v[es].rearrange("e p n -> p e n")).then_inc(w13_full[s], 16)
                sp.dma_start(w2[s][:, :, :], w2v[es].rearrange("e p n -> p e n")).then_inc(w2_full[s], 16)

            for s in range(3):
                load(s, s, s)
            sp.wait_ge(route_done, 1)
            n = sp.value_load(npi[0:1, 0:1], min_val=1, max_val=S // CAP)
            with sp.Fori(0, n) as p:
                with sp.Fori(1, 5) as i:
                    for s in range(3):
                        load(p * PAIRS + i * 3 + s, i * 3 + s, s)
                load(p * PAIRS + 15, 15, 0)
                with sp.If(p + 1 < n):
                    for s in range(3):
                        load(p * PAIRS + PAIRS + s, s, s, 1 if s == 0 else 3)
            for s in range(3):
                sp.wait_ge(scattered[s], n * (96 if s == 0 else 80) + 16)
            sp.dma_start(fnb[:, :], fnw.rearrange("(a d) -> a d", a=1).broadcast_to([P, D])).then_inc(s_fn, 16)
            for t in range(T):
                sp.dma_start(yt[t][:, :, :], yd.ap().rearrange("(k t p) d -> t p k d", k=2, p=P)[t]).then_inc(s_y[t], 16)
            for t in range(T):
                sp.wait_ge(fin_done, t + 1)
                sp.dma_start(outv[t], x2[:, t, :]).then_inc(s_out, 16)
            sp.wait_ge(s_out, 16 * T)

        @block.tensor
        def _(pe):
            order = {0: list(ORDER_A), 1: list(ORDER_B)}

            def begin(name):
                b, n = BANK[name]
                assert order[b // 4].pop(0) == name, name
                if n:
                    pe.wait_ge(free[b], n)
                return pb[b]

            def end(ins, name):
                ins.then_inc(full[BANK[name][0]], 1)

            def granule(g):
                pe.wait_ge(wlo_done, g + 1)
                half = g % 2
                n = g // 2
                hi, lo = whi[g % 2], wlo[g % 2]
                kind, w = ("n", 256) if g >= GR_IN else (GROUPS[n][0], GROUPS[n][3])
                for b in range(T if kind == "n" else 2):
                    name = ("y", n, b)
                    ps = begin(name) if half == 0 else psum(name)
                    if g == 0:
                        pe.wait_ge(hlo_done, 2 * (b + 1))
                    for c in range(HK):
                        kc = half * HK + c
                        if kind == "n":
                            tk = slice(b * P, (b + 1) * P)
                            o = ps[:, 0:w]
                            terms = ((hHi[:, kc, tk], hi[:, c, 0:w]), (hHi[:, kc, tk], lo[:, c, 0:w]),
                                     (hLo[:, kc, tk], hi[:, c, 0:w]))
                        else:
                            ch = slice(b * P, (b + 1) * P)
                            o = ps[:, :]
                            terms = ((hi[:, c, ch], hHi[:, kc, :]), (hi[:, c, ch], hLo[:, kc, :]),
                                     (lo[:, c, ch], hHi[:, kc, :]))
                        for i, (l, r) in enumerate(terms):
                            m = pe.matmul(o, l, r, start=(kc == 0 and i == 0), stop=(kc == KC - 1 and i == 2),
                                          skip_group_check=True)
                    if half == 1:
                        if b == (T if kind == "n" else 2) - 1:
                            end(m, name)
                        else:
                            end(m, name)
                if half == 0:
                    m.then_inc(gran_used, 1)
                else:
                    pe.wait_ge(full[BANK[name][0]], BANK[name][1] + 1)
                    pe.sem_inc(gran_used, 1)

            def four(name, f):
                ps = begin(name)
                for h in range(NH):
                    o = ps[:, h * P:(h + 1) * P]
                    m = f(h, o)
                end(m, name)

            def mm(o, l, r):
                return pe.matmul(o, l, r, start=True, stop=True)

            def task(k):
                if k[0] == "vt":
                    h = k[1]
                    pe.wait_ge(silu_done, h + 1)
                    four(k, lambda t, o: pe.transpose(o, vS[h % 2][:, t * P:(t + 1) * P], ident))
                elif k[0] == "gcum":
                    pe.wait_ge(gates_done, 1)
                    ps = begin(k)
                    for t in range(T):
                        g4 = gg[:, 4 * t:4 * t + 4]
                        mm(ps[:, 4 * t:4 * t + 4], tri, g4)
                        mm(ps[:, 16 + 4 * t:20 + 4 * t], ones, g4)
                        for tt in range(t + 1):
                            m = pe.matmul(ps[:, 32 + 4 * t:36 + 4 * t], tri if tt == t else ones,
                                          lf[:, 4 * tt:4 * tt + 4], start=(tt == 0), stop=(tt == t))
                    end(m, k)
                elif k[0] == "cB":
                    pe.wait_ge(cum_done, 2)
                    for h in range(NH):
                        four(("cB", h), lambda t, o: mm(o, c8[:, 4 * t + h:4 * t + h + 1].broadcast_to([P, P]), ident))
                elif k[0] == "ss":
                    ps = begin(k)
                    for h in range(NH):
                        pe.wait_ge(sq_done, NH * k[1] + h + 1)
                        for t in range(T):
                            m = mm(ps[:, 4 * t + h:4 * t + h + 1], nrm[h][:, t * P:(t + 1) * P], ones[:, 0:1])
                    end(m, k)
                elif k[0] == "kt":
                    for h in range(NH):
                        four(("kt", h), lambda t, o: pe.transpose(o, kT[:, h, t * P:(t + 1) * P], ident))
                elif k[0] == "prep":
                    t = k[1]
                    tk = slice(t * P, (t + 1) * P)
                    pe.wait_ge(rk_done, 1)
                    four(("gcB", t), lambda h, o: mm(o, cum[:, 4 * t + h:4 * t + h + 1].broadcast_to([P, P]), ident))
                    four(("bB", t), lambda h, o: mm(o, br[:, 4 * t + h:4 * t + h + 1].broadcast_to([P, P]), ident))
                    four(("KK", t), lambda h, o: mm(o, kT[:, h, tk], kT[:, h, tk]))
                    four(("QK", t), lambda h, o: mm(o, kT[:, h, tk], qT[:, h, tk]))
                elif k[0] == "xt":
                    for t in (2 * k[1], 2 * k[1] + 1):
                        pe.wait_ge(uinit, t + 1)
                        four(("XT", t), lambda h, o: pe.transpose(o, Um[t % 2][:, h, :], ident))
                elif k[0] == "lv":
                    _, pr, lv = k
                    for i in range(2):
                        t = 2 * pr + i
                        if lv == 0:
                            pe.wait_ge(xinit, t + 1)
                        else:
                            pe.wait_ge(x_ready, (pr * (LEVELS - 1) + lv - 1) * 2 + i + 1)
                        four(("Y", t, lv), lambda h, o: mm(o, Nm[i][:, h, :], Xm[i][:, h, :]))
                    if lv:
                        for i in range(2):
                            four(("UT", 2 * pr + i, lv), lambda h, o: pe.transpose(o, Xm[i][:, h, :], ident))
                    for i in range(2):
                        t = 2 * pr + i
                        pe.wait_ge(y_ready, (pr * LEVELS + lv) * 2 + i + 1)
                        if lv:
                            b, n = BANK[("UT", t, lv)]
                            pe.wait_ge(free[b], n + 1)
                        if lv < LEVELS - 1:
                            four(("Xp", t, lv), lambda h, o: mm(o, Um[i][:, h, :], Ym[i][:, h, :]))
                        else:
                            four(("Up", t, lv), lambda h, o: mm(o, Ym[i][:, h, :], Um[i][:, h, :]))
                elif k[0] == "fin":
                    for i in range(2):
                        t = 2 * k[1] + i
                        pe.wait_ge(u_ready, k[1] * 2 + i + 1)
                        pe.wait_ge(kt_done, NH)
                        four(("wT", t), lambda h, o: mm(o, kbg[:, t, h, :], Um[i][:, h, :]))
                        four(("u0", t), lambda h, o: mm(o, Um[i][:, h, :], vb[:, t, h, :]))

            pe.wait_ge(s_const, 16)
            pe.wait_ge(s_cw, 16)
            name = ("par",)
            end(pe.transpose(begin(name)[:, 0:48], PW48[:, :], ident[0:48, 0:48]), name)
            for t in range(T):
                pe.wait_ge(xn_done, t + 1)
                for i in range(2):
                    four(("xT", t, i), lambda c, o: pe.transpose(o, X0[:, t, (4 * i + c) * P:(4 * i + c + 1) * P], ident))
            for g in range(GR_IN):
                granule(g)
                for k in AFTER[g]:
                    task(k)

            for i in range(4):
                src = rq if i < 2 else rk
                pe.wait_ge(rot_done, 1 if i < 2 else 2)
                four(("rT", i), lambda t, o: pe.transpose(o, src[:, t, (i % 2) * P:(i % 2 + 1) * P], ident))
            pe.wait_ge(y_copied, 6)
            for k in range(KSTEPS):
                if k < 16:
                    h, t = FOX[k]
                    hp = slice((h % 2) * HD, (h % 2) * HD + HD)
                    name = ("fS", k)
                    ps = begin(name)
                    w = (t + 1) * P
                    pe.matmul(ps[:, 0:w], fqT[hp, h // 2, t * P:(t + 1) * P], fkT[hp, h // 2, 0:w], start=True, stop=False)
                    end(pe.matmul(ps[:, t * P:w], ident, negmask, start=False, stop=True), name)
                if 1 <= k <= 16:
                    h, t = FOX[k - 1]
                    name = ("fT", k - 1)
                    pe.wait_ge(pf_ready, k)
                    ps = begin(name)
                    for j in range(t + 1):
                        m = pe.transpose(ps[:, j * P:(j + 1) * P], Pf[(k - 1) % 2][:, j * P:(j + 1) * P], ident)
                    end(m, name)
                if k >= 2:
                    h, t = FOX[k - 2]
                    name = ("fO", k - 2)
                    pe.wait_ge(pt_ready, k - 1)
                    ps = begin(name)
                    for j in range(t + 1):
                        m = pe.matmul(ps[:, 0:HD], PT[(k - 2) % 2][:, j, :], fv[:, j, h * HD:(h + 1) * HD],
                                      start=(j == 0), stop=(j == t))
                    end(m, name)
                if k in WS:
                    n = WS[k]
                    pe.wait_ge(st_ready, n)
                    four(("wS", n), lambda h, o: mm(o, kbg[:, n, h, :], St[:, h, :]))
                if k in OO:
                    n = OO[k]
                    name = ("o", n)
                    ps = begin(name)
                    pe.wait_ge(uu_ready, n + 1)
                    pe.wait_ge(attn_ready, n + 1)
                    for h in range(NH):
                        o = ps[:, h * P:(h + 1) * P]
                        if n:
                            pe.matmul(o, qT[:, h, n * P:(n + 1) * P], St[:, h, :], start=True, stop=False)
                        m = pe.matmul(o, attnT[:, n, h, :], vb[:, n, h, :], start=(n == 0), stop=True)
                    end(m, name)
                    if n < T - 1:
                        four(("Sp", n), lambda h, o: mm(o, ktail[:, n, h, :], vb[:, n, h, :]))
                if k in RS:
                    n = RS[k]
                    hp = slice((n % 2) * HD, (n % 2) * HD + HD)
                    pe.wait_ge(rT_done, 4)
                    for j in range(T):
                        name = ("rS", n, j)
                        ps = begin(name)
                        end(mm(ps[:, 0:PW[j]], rkT[hp, n // 2, j * P:(j + 1) * P], rqT[hp, n // 2, j * P:S]), name)
                if k in RO:
                    n = RO[k]
                    name = ("rO", n)
                    ps = begin(name)
                    pe.wait_ge(retP_done, T * (n + 1))
                    for t in range(T):
                        for j in range(t + 1):
                            c0 = POFF[j] + (t - j) * P
                            m = pe.matmul(ps[:, t * HD:(t + 1) * HD], retP[:, c0:c0 + P],
                                          rv[:, j, n * HD:(n + 1) * HD], start=(j == 0), stop=(j == t))
                    end(m, name)
            for c in MT:
                if c == 2:
                    pe.wait_ge(mixr_done, 2)
                elif c == 0:
                    pe.wait_ge(fox_done, 16)
                elif c >= 4:
                    pe.wait_ge(mixg_done, c - 3)
                four(("mT", c), lambda t, o: pe.transpose(o, mix[:, t, c * P:(c + 1) * P], ident))
            pe.wait_ge(hlo_done, 2 * T + KC)
            for g in range(GR_IN, GR):
                granule(g)

            pe.wait_ge(s_n2, 48)
            for t in range(T):
                pe.wait_ge(h2_done, t + 1)
                for half in range(2):
                    four(("hT", t, half), lambda c, o: pe.transpose(
                        o, h2[:, t, (4 * half + c) * P:(4 * half + c + 1) * P], ident))
                pe.wait_ge(hT_done, t + 1)
                name = ("lg", t)
                ps = begin(name)
                for c in range(KC):
                    m = pe.matmul(ps[:, 0:NG + NE], h2T[:, c, :], rw[:, c, :], start=(c == 0), stop=(c == KC - 1))
                end(m, name)
            pe.wait_ge(m_done, 1)
            name = ("rank",)
            ps = begin(name)
            for t in range(T):
                for j in range(t + 1):
                    pe.matmul(ps[:, t * NE:(t + 1) * NE], const("rankm") if j == t else ones, M32[:, j, :],
                              start=(j == 0), stop=(j == t))
            for j in range(T):
                m = pe.matmul(ps[:, T * NE:(T + 1) * NE], ones, M32[:, j, :], start=(j == 0), stop=(j == T - 1))
            end(m, name)

            def indices(U):
                pe.wait_ge(sel_ready, U + 1)
                pe.wait_ge(idx_ready, U + 1)
                for t in range(T):
                    m = pe.matmul(pb[0][:, 0:1], selw[:, t, :, :], ones[:, 0:1], start=(t == 0), stop=(t == T - 1))
                m.then_inc(idx_full, 1)

            def turn(U, s, use):
                pe.wait_ge(gathered[s], use * 16 + 16)
                pe.wait_ge(xt_ready, U + 1)
                for c in range(KC):
                    m = pe.transpose(pb[1 + c // 4][:, (c % 4) * P:(c % 4 + 1) * P], xg[s][:, c * P:(c + 1) * P], ident)
                m.then_inc(xt_full, 1)

            def start(p):
                for k in range(3):
                    indices(p * PAIRS + k)
                turn(p * PAIRS, 0, p * 6)

            def unit(U, q, s, use, nuse, ahead, more):
                if ahead:
                    indices(U + 3)
                pe.wait_ge(xt_ready, U + 2)
                pe.wait_ge(w13_full[s], use * 32 + 32)
                pe.wait_ge(hid_ready, U + 1)
                for c in range(KC):
                    for e in range(2):
                        r = slice(e * CAP, (e + 1) * CAP)
                        m = pe.matmul(pb[3][r, :], xT[:, c, r], w13[s][:, e, :, c * FF:(c + 1) * FF],
                                      start=(c == 0), stop=(c == KC - 1), skip_group_check=True)
                m.then_inc(up_full, 1)
                if more:
                    turn(U + 1, (s + 1) % 3, nuse)
                pe.wait_ge(hid_ready, U + 2)
                pe.wait_ge(ht_ready, U + 1)
                for c in range(2):
                    m = pe.transpose(pb[4][:, c * P:(c + 1) * P], hid[:, c, :], ident)
                m.then_inc(ht_full, 1)
                pe.wait_ge(ht_ready, U + 2)
                pe.wait_ge(w2_full[s], use * 16 + 16)
                pe.wait_ge(oyA, U + 1)
                pe.wait_ge(oyB, U + 1)
                for n in range(2):
                    for c in range(2):
                        for e in range(2):
                            r = slice(e * CAP, (e + 1) * CAP)
                            m = pe.matmul(pb[5 + n][r, :], hidT[:, c, r],
                                          w2[s][:, e, c * D + n * 512:c * D + (n + 1) * 512],
                                          start=(c == 0), stop=(c == 1), skip_group_check=True)
                m.then_inc(slots_freed, 1)

            passes(pe, unit, start)

        def weight_high(e, g):
            w = 256 if g >= GR_IN else GROUPS[g // 2][3]
            e.wait_ge(raw_full[g % 3], 16 * (g // 3 + 1))
            if g >= 2:
                e.wait_ge(gran_used, g - 1)
            e.activation(whi[g % 2][:, :, 0:w], raw[g % 3][:, :, 0:w], ACT.Copy).then_inc(whi_done, 1)

        @block.scalar
        def _(act):
            cnt = [0]

            def link(ins):
                cnt[0] += 1
                ins.then_inc(act_self, 1)
                act.wait_ge(act_self, cnt[0])

            act.dma_start(PW48[:, :], convw[0].rearrange("k (b p) -> (k b) p", p=P)).then_inc(s_cw, 16)
            for dst, src in ((PDT[:, :], dtb[0:1, :].broadcast_to([P, 4])),
                             (PAL[:, :], alog[0:1, :].broadcast_to([P, 4])),
                             (PFB[:, :], foxb[0:1, :].broadcast_to([P, 4])),
                             (PRB[:, 0:NG], rgb[0:1, :].broadcast_to([P, NG])),
                             (PRB[:, NG:], reb.rearrange("a g e -> a (g e)").broadcast_to([P, NE])),
                             (PGN[:, :], gnw[0:1, :].broadcast_to([P, P]))):
                act.dma_start(dst, src).then_inc(s_par, 16)
            act.wait_ge(s_const, 16)
            for t in range(T):
                act.wait_ge(s_x[t], 16)
                link(act.activation(junk[:, :], X0[:, t, :], ACT.Square, accum_out=ssx[:, t:t + 1]))
                act.activation(ssx[:, t:t + 1], ssx[:, t:t + 1], ACT.Sqrt, scale=1.0 / D, bias=eps).then_inc(ssx_done, 1)
            weight_high(act, 0)
            weight_high(act, 1)
            wait_full(act, ("par",))
            release(act.activation(PCW[:, :, :].rearrange("p k b -> p (k b)"), pb[BANK[("par",)][0]][:, 0:48], ACT.Copy), ("par",))
            for t in range(T):
                for i in range(2):
                    name = ("xT", t, i)
                    wait_full(act, name)
                    act.activation(hHi[:, 4 * i:4 * i + 4, t * P:(t + 1) * P],
                                   psum(name)[:, :].rearrange("p (c n) -> p c n", n=P), ACT.Copy).then_inc(hhi_done, 1)

            def evac(n):
                kind, what, _, w = GROUPS[n]
                if kind == "n":
                    for t in range(T):
                        name = ("y", n, t)
                        wait_full(act, name)
                        ps = psum(name)
                        cp = lambda dst, src: act.activation(dst, src, ACT.Copy)
                        if what == "fv":
                            cp(fv[:, t, :], ps[:, 0:256])
                            i = cp(FFT[:, t, :], ps[:, 256:260])
                        elif what == "zb":
                            cp(mix[:, t, GW + 260:D], ps[:, 0:252])
                            i = cp(GAB[:, t, :], ps[:, 252:260])
                        elif what == "za":
                            i = cp(mix[:, t, GW:GW + 260], ps[:, 0:260])
                        elif what == "rg":
                            i = cp(mix[:, t, 256:GW], ps[:, 0:256])
                        else:
                            i = cp({"rq": rq, "rk": rk, "rv": rv}[what][:, t, :], ps[:, 0:256])
                        release(i, name)
                    act.wait_ge(free[BANK[name][0]], BANK[name][1] + 1)
                    act.sem_inc(y_copied, 1) if what not in ("zb", "za", "rg") else act.sem_inc(z_in, 1)
                elif what in ("fq", "fk"):
                    for b in range(2):
                        name = ("y", n, b)
                        wait_full(act, name)
                        release(act.activation((fqT if what == "fq" else fkT)[:, b, :], psum(name)[:, :], ACT.Copy), name)
                    act.wait_ge(free[BANK[name][0]], BANK[name][1] + 1)
                    act.sem_inc(y_copied, 1)
                else:
                    for b in range(2):
                        name = ("y", n, b)
                        blk = tcol[what] + b
                        i = CONVN[what] + b
                        wait_full(act, name)
                        if i >= 2:
                            act.wait_ge(silu_done, i - 1)
                        act.activation(cacc[i % 2][:, :], psum(name)[:, :], ACT.Copy,
                                       scale=PCW[:, 3, blk:blk + 1]).then_inc(tap0_done, 1)
                        act.wait_ge(conv_done, i + 1)
                        h = i % 4
                        if what[0] == "v":
                            dst = vS[h % 2][:, :]
                            if h >= 2:
                                act.wait_ge(vb_done, h - 1)
                        else:
                            dst = (kT if what[0] == "k" else qT)[:, h, :]
                        act.activation(dst, cacc[i % 2][:, :], ACT.Silu).then_inc(silu_done, 1)

            def task(k):
                if k[0] == "evac":
                    evac(k[1])
                elif k[0] == "gates":
                    act.wait_ge(gexp_in, 1)
                    act.activation(e8, az, ACT.Exp, scale=-1.0)
                    act.activation(eb.rearrange("p (t n) -> p t n", t=T), GAB[:, :, 4:8], ACT.Exp, scale=-1.0)
                    act.activation(ea, PAL[:, :], ACT.Exp).then_inc(gexp_done, 1)
                elif k[0] == "gcum":
                    act.wait_ge(cum_done, 3)
                    act.activation(egc, cum[:, 0:16], ACT.Exp)
                    act.activation(egl, cum[:, 16:32], ACT.Exp)
                    act.activation(etl, tl, ACT.Exp).then_inc(cexp_done, 1)
                elif k[0] == "cB":
                    for h in range(NH):
                        name = ("cB", h)
                        wait_full(act, name)
                        release(act.activation(cB8[:, h, :], psum(name)[:, :], ACT.Copy), name)
                    act.wait_ge(free[BANK[name][0]], BANK[name][1] + 1)
                    act.sem_inc(cB_done, 1)
                elif k[0] == "ss" and k[1] == 1:
                    act.wait_ge(ss_read, 2)
                    act.activation(rks, ssk, ACT.Sqrt, bias=eps)
                    act.activation(rqs[:, :], ssq, ACT.Sqrt, scale=float(P), bias=const("eps128")).then_inc(root_done, 1)
                elif k[0] == "prep":
                    t = k[1]
                    i = t % 2
                    act.wait_ge(d_raw, t + 1)
                    name = ("gcB", t)
                    if t >= 2:
                        act.wait_ge(u_ready, 1 + i)
                    j = act.activation(Xm[i][:, :, :], psum(name)[:, :].rearrange("p (h n) -> p h n", h=NH), ACT.Exp)
                    release(j, name)
                    act.activation(Dm[i][:, :, :], Dm[i][:, :, :], ACT.Exp).then_inc(d_exp, 1)
                elif k[0] == "xt":
                    for t in (2 * k[1], 2 * k[1] + 1):
                        name = ("XT", t)
                        wait_full(act, name)
                        j = act.activation(Xm[t % 2][:, :, :], psum(name)[:, :].rearrange("p (h n) -> p h n", h=NH), ACT.Copy)
                        release(j, name)
                        act.wait_ge(free[BANK[name][0]], BANK[name][1] + 1)
                        act.sem_inc(xinit, 1)
                elif k[0] == "lv" and k[2]:
                    for i in range(2):
                        name = ("UT", 2 * k[1] + i, k[2])
                        wait_full(act, name)
                        release(act.activation(Um[i][:, :, :], psum(name)[:, :].rearrange("p (h n) -> p h n", h=NH), ACT.Copy), name)
                elif k[0] == "fin":
                    for t in (2 * k[1], 2 * k[1] + 1):
                        for name, dst, sc in ((("wT", t), kbg, -1.0), (("u0", t), vb, 1.0)):
                            wait_full(act, name)
                            j = act.activation(dst[:, t, :, :], psum(name)[:, :].rearrange("p (h n) -> p h n", h=NH),
                                               ACT.Copy, scale=sc)
                            release(j, name)
                        act.wait_ge(free[BANK[name][0]], BANK[name][1] + 1)
                        act.sem_inc(u0_ready, 1)

            for g in range(GR_IN):
                weight_high(act, g + 2)
                for k in AFTER[g]:
                    task(k)
            act.wait_ge(z_in, 3)
            act.activation(mix[:, :, 256:D], mix[:, :, 256:D], ACT.Silu).then_inc(silu2_done, 1)
            for i in range(4):
                name = ("rT", i)
                wait_full(act, name)
                j = act.activation((rqT if i < 2 else rkT)[:, i % 2, :], psum(name)[:, :], ACT.Copy)
                release(j, name)
                act.wait_ge(free[BANK[name][0]], BANK[name][1] + 1)
                act.sem_inc(rT_done, 1)
            for k in range(KSTEPS):
                if k < 16:
                    h, t = FOX[k]
                    w = (t + 1) * P
                    act.wait_ge(sx_ready, k + 1)
                    if k >= 2:
                        wait_full(act, ("fT", k - 2))
                    act.activation(Pf[k % 2][:, 0:w], Sx[k % 2][:, 0:w], ACT.Exp, scale=HD ** -0.5,
                                   bias=nmx[:, k:k + 1], accum_out=rs[:, k:k + 1]).then_inc(pf_ready, 1)
                if 1 <= k <= 16:
                    h, t = FOX[k - 1]
                    name = ("fT", k - 1)
                    wait_full(act, name)
                    if k >= 3:
                        wait_full(act, ("fO", k - 3))
                    j = act.activation(PT[(k - 1) % 2][:, 0:t + 1, :],
                                       psum(name)[:, 0:(t + 1) * P].rearrange("p (j n) -> p j n", n=P), ACT.Copy)
                    release(j, name)
                    act.wait_ge(free[BANK[name][0]], BANK[name][1] + 1)
                    act.sem_inc(pt_ready, 1)
                if k in OO:
                    n = OO[k]
                    name = ("o", n)
                    wait_full(act, name)
                    j = act.activation(kbg[:, n, :, :], psum(name)[:, :].rearrange("p (h n) -> p h n", h=NH), ACT.Copy)
                    release(j, name)
                    act.wait_ge(free[BANK[name][0]], BANK[name][1] + 1)
                    act.sem_inc(og_done, 1)
                if k in RO:
                    n = RO[k]
                    name = ("rO", n)
                    wait_full(act, name)
                    j = act.activation(oret[:, :, n * HD:(n + 1) * HD],
                                       psum(name)[:, 0:T * HD].rearrange("p (t n) -> p t n", t=T), ACT.Copy)
                    release(j, name)
                    act.wait_ge(free[BANK[name][0]], BANK[name][1] + 1)
                    act.sem_inc(oret_done, 1)
                if k == 16:
                    act.wait_ge(ssr_done, 2)
                    act.activation(ssx4, ssx4, ACT.Sqrt, scale=1.0 / HD, bias=eps).then_inc(rtr_done, 1)
                    act.activation(ssn, ssn, ACT.Sqrt, scale=1.0 / P, bias=eps).then_inc(rtr_done, 1)
            for c in MT:
                name = ("mT", c)
                wait_full(act, name)
                act.activation(hHi[:, c, :], psum(name)[:, :], ACT.Copy).then_inc(hhi_done, 1)
            for g in range(GR_IN, GR - 2):
                weight_high(act, g + 2)
            for t in range(T):
                name = ("y", NIN + NOUT - 1, t)
                act.wait_ge(x2_done, T * (NOUT - 1) + t + 1)
                link(act.activation(h2[:, t, :], x2[:, t, :], ACT.Square, accum_out=ss2[:, t:t + 1]))
            act.activation(ss2, ss2, ACT.Sqrt, scale=1.0 / D, bias=eps).then_inc(ss2_done, 1)
            for t in range(T):
                act.wait_ge(h2_done, t + 1)
                act.dma_start(h2d.ap()[t * P:(t + 1) * P, :], h2[:, t, :]).then_inc(s_h2d, 16)
                for half in range(2):
                    name = ("hT", t, half)
                    wait_full(act, name)
                    if t:
                        wait_full(act, ("lg", t - 1))
                    release(act.activation(h2T[:, 4 * half:4 * half + 4, :],
                                           psum(name)[:, :].rearrange("p (c n) -> p c n", n=P), ACT.Copy), name)
                act.wait_ge(free[BANK[name][0]], BANK[name][1] + 1)
                act.sem_inc(hT_done, 1)
            act.wait_ge(rexp_in, 1)
            act.activation(gd, gd, ACT.Exp).then_inc(rexp_done, 1)
            act.wait_ge(rexp_in, 2)
            act.activation(e2, mm1, ACT.Exp).then_inc(rexp_done, 1)

            def turned(U):
                act.wait_ge(xt_full, U + 2)
                act.wait_ge(up_full, U + 1)
                act.activation(xT[:, 0:4, :], pb[1][:, :].rearrange("p (c n) -> p c n", n=P), ACT.Copy)
                act.activation(xT[:, 4:8, :], pb[2][:, :].rearrange("p (c n) -> p c n", n=P), ACT.Copy).then_inc(xt_ready, 1)

            def unit(U, q, s, use, nuse, ahead, more):
                act.wait_ge(up_full, U + 2)
                act.activation(sa[:, :], pb[3][:, 0:FF], ACT.Silu).then_inc(sa_ready, 1)
                if more:
                    turned(U + 1)
                act.wait_ge(ht_full, U + 2)
                act.activation(hidT[:, :, :], pb[4][:, 0:2 * P].rearrange("p (c n) -> p c n", n=P), ACT.Copy).then_inc(ht_ready, 1)
                act.wait_ge(slots_freed, U + 4)
                act.wait_ge(scattered[s], use * 16 + 16)
                act.activation(oy[s][:, 512:D], pb[6][:, :], ACT.Copy).then_inc(oyB, 1)

            passes(act, unit, lambda p: turned(p * PAIRS))
            for t in range(T):
                act.wait_ge(acc_done, t + 1)
                act.activation(jk[:, :], yt[t][:, 0, :], ACT.Square, accum_out=ssf[:, t:t + 1]).then_inc(ssf_done, 1)
                act.wait_ge(ssf_done, 2 * t + 1)
                act.activation(ssf[:, t:t + 1], ssf[:, t:t + 1], ACT.Sqrt, scale=1.0 / D, bias=eps).then_inc(ssf_done, 1)

        @block.gpsimd
        def _(pool):
            cnt = [0]

            def link(ins):
                cnt[0] += 1
                ins.then_inc(pool_self, 1)
                pool.wait_ge(pool_self, cnt[0])

            def weight_low(g):
                w = 256 if g >= GR_IN else GROUPS[g // 2][3]
                pool.wait_ge(whi_done, g + 1)
                pool.tensor_tensor(wlo[g % 2][:, :, 0:w], raw[g % 3][:, :, 0:w], whi[g % 2][:, :, 0:w].bitcast(F32),
                                   ALU.subtract).then_inc(wlo_done, 1)

            def bc(m):
                return m.unsqueeze(1).broadcast_to([P, NH, P])

            weight_low(0)
            weight_low(1)

            def squares(k):
                for h in range(NH):
                    n = NH * k + h
                    pool.wait_ge(silu_done, NH + n + 1)
                    if k:
                        wait_full(pool, ("ss", 0))
                    src = (kT if k == 0 else qT)[:, h, :]
                    pool.tensor_tensor(nrm[n % 4][:, :], src, src, ALU.mult).then_inc(sq_done, 1)

            def task(k):
                if k[0] == "ss":
                    squares(k[1])
                elif k[0] == "prep":
                    t = k[1]
                    i = t % 2
                    tk = slice(t * P, (t + 1) * P)
                    pool.wait_ge(d_exp, t + 1)
                    pool.tensor_tensor(Ym[i][:, :, :], Dm[i][:, :, :], bc(strict), ALU.mult).then_inc(ds_ready, 1)
                    pool.tensor_tensor(Dm[i][:, :, :], Dm[i][:, :, :], bc(tri), ALU.mult).then_inc(di_ready, 1)
                    wait_full(pool, ("QK", t))
                    pool.tensor_tensor(qT[:, :, tk], qT[:, :, tk], Xm[i][:, :, :], ALU.mult).then_inc(qg_ready, 1)
                    pool.wait_ge(n_ready, t + 1)
                    link(pool.tensor_tensor(Ym[i][:, :, :], Nm[i][:, :, :], bc(const("nM1")), ALU.mult))
                    pool.tensor_tensor(Um[i][:, :, :], Ym[i][:, :, :], bc(ident), ALU.add).then_inc(uinit, 1)
                elif k == ("evac", GIDX["rv"]):
                    rotary(rq, 1)
                elif k == ("evac", GIDX["za"]):
                    rotary(rk, 2)

            def rotary(r, n):
                pool.wait_ge(y_copied, n + 1)
                v = r[:, :, :].rearrange("p t (h s n) -> p t h s n", h=NH, s=2)
                t1, t2 = v[:, :, :, 0, :], v[:, :, :, 1, :]
                co = cosT.unsqueeze(2).broadcast_to([P, T, NH, 32])
                si = sinT.unsqueeze(2).broadcast_to([P, T, NH, 32])
                if n == 2:
                    pool.wait_ge(rot_done, 1)
                pool.tensor_tensor(rtmp[0][:, :, :, :], t1, co, ALU.mult)
                pool.tensor_tensor(rtmp[1][:, :, :, :], t2, si, ALU.mult)
                pool.tensor_tensor(rtmp[2][:, :, :, :], t1, si, ALU.mult)
                link(pool.tensor_tensor(rtmp[3][:, :, :, :], t2, co, ALU.mult))
                pool.tensor_tensor(t1, rtmp[0][:, :, :, :], rtmp[1][:, :, :, :], ALU.subtract)
                pool.tensor_tensor(t2, rtmp[2][:, :, :, :], rtmp[3][:, :, :, :], ALU.add).then_inc(rot_done, 1)

            for g in range(GR_IN):
                weight_low(g + 2)
                for k in AFTER[g]:
                    task(k)
            pool.wait_ge(silu2_done, 1)
            for t in range(T):
                m4 = mix[:, t, GW:D].rearrange("p (h n) -> p h n", h=NH)
                j = pool.tensor_tensor(m4, m4, bc(PGN[:, :]), ALU.mult)
            j.then_inc(zg_done, 1)
            for t in range(T):
                pool.wait_ge(og_done, t + 1)
                pool.tensor_tensor(gsq[t][:, :, :], kbg[:, t, :, :], kbg[:, t, :, :], ALU.mult).then_inc(sqr_done, 1)
            pool.wait_ge(oret_done, NH)
            pool.tensor_tensor(osq[:, :, :], oret[:, :, :], oret[:, :, :], ALU.mult).then_inc(sqr_done, 1)
            for g in range(GR_IN, GR - 2):
                weight_low(g + 2)

            pool.wait_ge(s_h2d, 16 * T)

            def gather(U, s, turned):
                pool.wait_ge(idx_ready, U + 2)
                pool.wait_ge(xt_full, turned + 1)
                pool.sem_inc(pool_step, 1)
                pool.indirect_dma_start(xg[s][:, :], None, h2d.ap()[:, :],
                                        bass.IndirectOffsetOnAxis(ap=tok_i[s][:, 0:1].bitcast(U32), axis=0),
                                        bounds_check=S - 1, oob_is_err=False).then_inc(gathered[s], 16)

            def unit(U, q, s, use, nuse, ahead, more):
                if ahead:
                    gather(U + 3, s, U + 1)
                pool.wait_ge(oyA, U + 2)
                pool.wait_ge(oyB, U + 2)
                pool.sem_inc(pool_step, 1)
                pool.indirect_dma_start(yd.ap()[:, :],
                                        bass.IndirectOffsetOnAxis(ap=dst_i[s][:, 0:1].bitcast(U32), axis=0),
                                        oy[s][:, :], None, bounds_check=2 * S - 1, oob_is_err=False).then_inc(scattered[s], 16)


            pool.wait_ge(route_done, 1)
            for k in range(3):
                pool.dma_start(oy[k][:, 0:KC], fnw.rearrange("(p c) -> p c", c=KC)).then_inc(scattered[k], 16)

            def start(p):
                for k in range(3):
                    gather(p * PAIRS + k, k, p * PAIRS)

            passes(pool, unit, start)

        @block.vector
        def _(dve):
            cnt = [0]

            def link(ins):
                cnt[0] += 1
                ins.then_inc(dve_self, 1)
                dve.wait_ge(dve_self, cnt[0])

            def v4(name):
                return psum(name)[:, :].rearrange("p (h n) -> p h n", h=NH)

            dve.wait_ge(s_n1, 16)
            for t in range(T):
                dve.wait_ge(ssx_done, t + 1)
                link(dve.reciprocal(rx[:, t:t + 1], ssx[:, t:t + 1]))
                dve.scalar_tensor_tensor(out=X0[:, t, :], in0=X0[:, t, :], scalar=rx[:, t:t + 1], in1=n1b[:, :],
                                         op0=ALU.mult, op1=ALU.mult).then_inc(xn_done, 1)
            for t in range(T):
                for i in range(2):
                    name = ("xT", t, i)
                    dve.wait_ge(hhi_done, 2 * t + i + 1)
                    tk = slice(t * P, (t + 1) * P)
                    cs = slice(4 * i, 4 * i + 4)
                    j = dve.tensor_tensor(hLo[:, cs, tk], psum(name)[:, :].rearrange("p (c n) -> p c n", n=P),
                                          hHi[:, cs, tk].bitcast(F32), ALU.subtract)
                    release(j, name)
                    dve.wait_ge(free[BANK[name][0]], BANK[name][1] + 1)
                    dve.sem_inc(hlo_done, 1)

            def evac(n):
                kind, what, _, _ = GROUPS[n]
                if what not in CONVN:
                    return
                for b in range(2):
                    name = ("y", n, b)
                    i = CONVN[what] + b
                    blk = tcol[what] + b
                    dve.wait_ge(tap0_done, i + 1)
                    a = cacc[i % 2]
                    for s in (1, 2, 3):
                        j = dve.scalar_tensor_tensor(out=a[:, s:S], in0=psum(name)[:, 0:S - s],
                                                     scalar=PCW[:, 3 - s, blk:blk + 1], in1=a[:, s:S],
                                                     op0=ALU.mult, op1=ALU.add)
                        if s < 3:
                            link(j)
                    release(j, name)
                    dve.wait_ge(free[BANK[name][0]], BANK[name][1] + 1)
                    dve.sem_inc(conv_done, 1)

            def gates():
                dve.wait_ge(y_copied, 1)
                dve.wait_ge(z_in, 1)
                dve.wait_ge(s_par, 16 * 6)
                dtv = PDT[:, :].unsqueeze(1).broadcast_to([P, T, 4])
                fbv = PFB[:, :].unsqueeze(1).broadcast_to([P, T, 4])
                dve.tensor_tensor(z8[:, :, 0:4], GAB[:, :, 0:4], dtv, ALU.add)
                link(dve.tensor_tensor(hv[:, :, 4:8], FFT, fbv, ALU.add))
                link(dve.tensor_scalar(z8[:, :, 4:8], hv[:, :, 4:8], -1.0, None, ALU.mult))
                dve.scalar_tensor_tensor(out=az, in0=z8, scalar=-1.0, in1=z8, op0=ALU.mult, op1=ALU.max).then_inc(gexp_in, 1)
                dve.wait_ge(gexp_done, 1)
                link(dve.tensor_scalar(dd, e8, 2.0, None, ALU.add))
                link(dve.reciprocal(sv, dd))
                link(dve.tensor_tensor(sv, sv, e8, ALU.mult))
                link(dve.tensor_tensor(qv, sv, sv, ALU.mult))
                link(dve.tensor_scalar(hv, qv, 1.0 / 17, None, ALU.mult))
                for c in (15, 13, 11, 9, 7, 5, 3):
                    link(dve.scalar_tensor_tensor(out=hv, in0=hv, scalar=1.0 / c, in1=qv, op0=ALU.add, op1=ALU.mult))
                link(dve.scalar_tensor_tensor(out=hv, in0=hv, scalar=1.0, in1=sv, op0=ALU.add, op1=ALU.mult))
                link(dve.tensor_scalar(sp8, z8, 0.0, None, ALU.max))
                link(dve.scalar_tensor_tensor(out=sp8, in0=hv, scalar=2.0, in1=sp8, op0=ALU.mult, op1=ALU.add))
                link(dve.tensor_scalar(eb, eb, 1.0, None, ALU.add))
                dve.reciprocal(beta, eb)
                t3 = lambda a: a.rearrange("p (t n) -> p t n", t=T)
                link(dve.tensor_tensor(t3(gg), sp8[:, :, 0:4], ea.unsqueeze(1).broadcast_to([P, T, 4]), ALU.mult))
                dve.tensor_scalar(t3(lf), sp8[:, :, 4:8], -1.0, None, ALU.mult)
                dve.tensor_scalar(gg, gg, -1.0, None, ALU.mult).then_inc(gates_done, 1)

            def task(k):
                if k[0] == "evac":
                    evac(k[1])
                elif k[0] == "gates":
                    gates()
                elif k[0] == "gcum":
                    wait_full(dve, k)
                    dve.tensor_copy(cum, psum(k)[:, 0:48]).then_inc(cum_done, 1)
                    dve.wait_ge(cum_done, 1)
                    dve.tensor_scalar(c8, cum[:, 32:48], -float(HD ** 0.5), None, ALU.mult).then_inc(cum_done, 1)
                    release(dve.tensor_tensor(tl, cum[:, 16:32], cum[:, 0:16], ALU.subtract), k)
                    dve.wait_ge(free[BANK[k][0]], BANK[k][1] + 1)
                    dve.sem_inc(cum_done, 1)
                    dve.wait_ge(cexp_done, 1)
                    link(dve.tensor_tensor(bgc, beta, egc, ALU.mult))
                elif k[0] == "vt":
                    h = k[1]
                    wait_full(dve, k)
                    dve.wait_ge(gates_done, 1)
                    bv = beta.rearrange("p (t n) -> p t n", t=T)[:, :, h:h + 1].broadcast_to([P, T, P])
                    release(dve.tensor_tensor(vb[:, :, h, :], v4(k), bv, ALU.mult), k)
                    dve.wait_ge(free[BANK[k][0]], BANK[k][1] + 1)
                    dve.sem_inc(vb_done, 1)
                elif k[0] == "ss":
                    wait_full(dve, k)
                    release(dve.tensor_copy(ssk if k[1] == 0 else ssq, psum(k)[:, 0:16]), k)
                    dve.wait_ge(free[BANK[k][0]], BANK[k][1] + 1)
                    dve.sem_inc(ss_read, 1)
                    if k[1]:
                        dve.wait_ge(root_done, 1)
                        link(dve.reciprocal(rks, rks))
                        dve.reciprocal(rqs[:, :], rqs[:, :])
                        dve.tensor_tensor(br, beta, rks, ALU.mult)
                        dve.tensor_tensor(bgr, bgc, rks, ALU.mult)
                        link(dve.tensor_tensor(etr, etl, rks, ALU.mult))
                        dve.sem_inc(rk_done, 1)
                elif k[0] == "kt":
                    for h in range(NH):
                        name = ("kt", h)
                        wait_full(dve, name)
                        f = lambda a: a.rearrange("p (t n) -> p t n", t=T)[:, :, h:h + 1].broadcast_to([P, T, P])
                        dve.tensor_tensor(kbg[:, :, h, :], v4(name), f(bgr), ALU.mult)
                        release(dve.tensor_tensor(ktail[:, :, h, :], v4(name), f(etr), ALU.mult), name)
                        dve.wait_ge(free[BANK[name][0]], BANK[name][1] + 1)
                        dve.sem_inc(kt_done, 1)
                elif k[0] == "prep":
                    t = k[1]
                    i = t % 2
                    name = ("gcB", t)
                    wait_full(dve, name)
                    for h in range(NH):
                        j = dve.tensor_scalar(Dm[i][:, h, :], psum(name)[:, h * P:(h + 1) * P],
                                              cum[:, 4 * t + h:4 * t + h + 1], 0.0, ALU.subtract, ALU.min)
                    j.then_inc(d_raw, 1)
                    dve.wait_ge(ds_ready, t + 1)
                    wait_full(dve, ("KK", t))
                    for h in range(NH):
                        j = dve.scalar_tensor_tensor(out=Nm[i][:, h, :], in0=psum(("KK", t))[:, h * P:(h + 1) * P],
                                                     scalar=rks[:, 4 * t + h:4 * t + h + 1], in1=Ym[i][:, h, :],
                                                     op0=ALU.mult, op1=ALU.mult)
                    release(j, ("KK", t))
                    b, n = BANK[("KK", t)]
                    dve.wait_ge(free[b], n + 1)
                    wait_full(dve, ("bB", t))
                    release(dve.tensor_tensor(Nm[i][:, :, :], Nm[i][:, :, :], v4(("bB", t)), ALU.mult), ("bB", t))
                    b, n = BANK[("bB", t)]
                    dve.wait_ge(free[b], n + 1)
                    dve.sem_inc(n_ready, 1)
                    dve.wait_ge(di_ready, t + 1)
                    wait_full(dve, ("QK", t))
                    for h in range(NH):
                        j = dve.scalar_tensor_tensor(out=attnT[:, t, h, :], in0=psum(("QK", t))[:, h * P:(h + 1) * P],
                                                     scalar=rks[:, 4 * t + h:4 * t + h + 1], in1=Dm[i][:, h, :],
                                                     op0=ALU.mult, op1=ALU.mult)
                    release(j, ("QK", t))
                    b, n = BANK[("QK", t)]
                    dve.wait_ge(free[b], n + 1)
                    dve.sem_inc(attn_ready, 1)
                elif k[0] == "lv":
                    _, pr, lv = k
                    mask = nM[:, lv, :].unsqueeze(1).broadcast_to([P, NH, P])

                    def update(name, dst, in1, op, s):
                        wait_full(dve, name)
                        release(dve.tensor_tensor(dst, v4(name), in1, op), name)
                        b, n = BANK[name]
                        dve.wait_ge(free[b], n + 1)
                        dve.sem_inc(s, 1)

                    for i in range(2):
                        update(("Y", 2 * pr + i, lv), Ym[i][:, :, :], mask, ALU.mult, y_ready)
                    for i in range(2):
                        if lv < LEVELS - 1:
                            update(("Xp", 2 * pr + i, lv), Xm[i][:, :, :], Xm[i][:, :, :], ALU.add, x_ready)
                        else:
                            update(("Up", 2 * pr + i, lv), Um[i][:, :, :], Um[i][:, :, :], ALU.add, u_ready)

            for g in range(GR_IN):
                for k in AFTER[g]:
                    task(k)
            dve.wait_ge(u0_ready, T)
            dve.sem_inc(uu_ready, 1)
            for k in range(KSTEPS):
                if k < 16:
                    h, t = FOX[k]
                    w = (t + 1) * P
                    name = ("fS", k)
                    wait_full(dve, name)
                    if k == 0:
                        dve.wait_ge(cB_done, 1)
                        dve.wait_ge(rot_done, 2)
                    if k >= 2:
                        dve.wait_ge(pf_ready, k - 1)
                    j = dve.tensor_tensor_reduce(out=Sx[k % 2][:, 0:w], in0=psum(name)[:, 0:w], in1=cB8[:, h, 0:w],
                                                 scale=1.0, scalar=-3.0e38, op0=ALU.add, op1=ALU.max,
                                                 accum_out=mx[:, k:k + 1])
                    release(j, name)
                    dve.wait_ge(free[BANK[name][0]], BANK[name][1] + 1)
                    dve.tensor_scalar(nmx[:, k:k + 1], mx[:, k:k + 1], -float(HD ** -0.5), None, ALU.mult).then_inc(sx_ready, 1)
                if k in WS:
                    n = WS[k]
                    name = ("wS", n)
                    wait_full(dve, name)
                    release(dve.tensor_tensor(vb[:, n, :, :], v4(name), vb[:, n, :, :], ALU.add), name)
                    dve.wait_ge(free[BANK[name][0]], BANK[name][1] + 1)
                    dve.sem_inc(uu_ready, 1)
                if k in OO and OO[k] < T - 1:
                    n = OO[k]
                    name = ("Sp", n)
                    wait_full(dve, name)
                    if n == 0:
                        j = dve.tensor_copy(St[:, :, :], v4(name))
                    else:
                        for h in range(NH):
                            j = dve.scalar_tensor_tensor(out=St[:, h, :], in0=St[:, h, :],
                                                         scalar=egl[:, 4 * n + h:4 * n + h + 1],
                                                         in1=psum(name)[:, h * P:(h + 1) * P],
                                                         op0=ALU.mult, op1=ALU.add)
                    release(j, name)
                    dve.wait_ge(free[BANK[name][0]], BANK[name][1] + 1)
                    dve.sem_inc(st_ready, 1)
                if k in RS:
                    n = RS[k]
                    for jj in range(T):
                        name = ("rS", n, jj)
                        wait_full(dve, name)
                        if n and jj == 0:
                            wait_full(dve, ("rO", n - 1))
                        release(dve.tensor_tensor(retP[:, POFF[jj]:POFF[jj] + PW[jj]], psum(name)[:, 0:PW[jj]],
                                                  dm[:, n, 0:PW[jj]], ALU.mult), name)
                        dve.wait_ge(free[BANK[name][0]], BANK[name][1] + 1)
                        dve.sem_inc(retP_done, 1)
                if k in (3, 6, 9, 12):
                    t = k // 3 - 1
                    dve.wait_ge(sqr_done, t + 1)
                    dve.tensor_reduce(ssn[:, 4 * t:4 * t + 4], gsq[t][:, :, :], AX_X, ALU.add)
                if k == 14:
                    dve.wait_ge(sqr_done, T + 1)
                    link(dve.tensor_reduce(ssx4.rearrange("p (t h) -> p t h", t=T),
                                           osq[:, :, :].rearrange("p t (h n) -> p t h n", h=NH), AX_X, ALU.add))
                    link(dve.tensor_tensor(rn, rqs[:, :], rqs[:, :], ALU.mult))
                    dve.tensor_tensor(ssn, ssn, rn, ALU.mult).then_inc(ssr_done, 2)
                if k >= 2:
                    u = k - 2
                    h, t = FOX[u]
                    name = ("fO", u)
                    wait_full(dve, name)
                    link(dve.reciprocal(ri[:, u:u + 1], rs[:, u:u + 1]))
                    j = dve.tensor_scalar(mix[:, t, h * HD:(h + 1) * HD], psum(name)[:, 0:HD], ri[:, u:u + 1], None, ALU.mult)
                    release(j, name)
                    dve.wait_ge(free[BANK[name][0]], BANK[name][1] + 1)
                    dve.sem_inc(fox_done, 1)
            dve.wait_ge(rtr_done, 1)
            link(dve.reciprocal(ssx4, ssx4))
            o4 = oret[:, :, :].rearrange("p t (h n) -> p (t h) n", h=NH)
            link(dve.tensor_tensor(o4, o4, ssx4.unsqueeze(2).broadcast_to([P, 16, HD]), ALU.mult))
            dve.wait_ge(silu2_done, 1)
            dve.tensor_tensor(mix[:, :, 256:GW], oret[:, :, :], mix[:, :, 256:GW], ALU.mult).then_inc(mixr_done, 2)
            dve.wait_ge(rtr_done, 2)
            link(dve.reciprocal(rn, ssn))
            link(dve.tensor_tensor(rn, rn, rqs[:, :], ALU.mult))
            dve.wait_ge(zg_done, 1)
            for h in range(NH):
                for t in range(T):
                    m = mix[:, t, GW + h * P:GW + (h + 1) * P]
                    j = dve.scalar_tensor_tensor(out=m, in0=kbg[:, t, h, :], scalar=rn[:, 4 * t + h:4 * t + h + 1],
                                                 in1=m, op0=ALU.mult, op1=ALU.mult)
                j.then_inc(mixg_done, 1)
            dve.wait_ge(mixg_done, NH)
            dve.sem_inc(slots_freed, 1)
            for ci, c in enumerate(MT):
                name = ("mT", c)
                dve.wait_ge(hhi_done, 2 * T + ci + 1)
                j = dve.tensor_tensor(hLo[:, c, :], psum(name)[:, :], hHi[:, c, :].bitcast(F32), ALU.subtract)
                release(j, name)
                dve.wait_ge(free[BANK[name][0]], BANK[name][1] + 1)
                dve.sem_inc(hlo_done, 1)
            dve.wait_ge(s_x2, 16 * T)
            for n in range(NOUT):
                for t in range(T):
                    name = ("y", NIN + n, t)
                    wait_full(dve, name)
                    xs = x2[:, t, n * 256:(n + 1) * 256]
                    release(dve.tensor_tensor(xs, psum(name)[:, 0:256], xs, ALU.add), name)
                    dve.wait_ge(free[BANK[name][0]], BANK[name][1] + 1)
                    dve.sem_inc(x2_done, 1)

            dve.sem_inc(slots_freed, 2)
            dve.wait_ge(ss2_done, 1)
            link(dve.reciprocal(r2, ss2))
            dve.wait_ge(s_n2, 48)
            for t in range(T):
                v = lambda a: a.rearrange("q (p c) -> q p c", c=KC)
                dve.scalar_tensor_tensor(out=h2[:, t, :].rearrange("q (c p) -> q p c", c=KC), in0=v(x2[:, t, :]),
                                         scalar=r2[:, t:t + 1], in1=v(n2b[:, :]), op0=ALU.mult, op1=ALU.mult).then_inc(h2_done, 1)
            bl = PRB[:, :]
            for t in range(T):
                name = ("lg", t)
                wait_full(dve, name)
                release(dve.tensor_tensor(LG[:, t, :], psum(name)[:, 0:NG + NE], bl, ALU.add), name)
                dve.wait_ge(free[BANK[name][0]], BANK[name][1] + 1)

            def top(src, desc, mx_, one, scratch, n):
                b = lambda a: a.unsqueeze(2).broadcast_to([P, T, n])
                link(dve.tensor_reduce(mx_, src, AX_X, ALU.max))
                link(dve.tensor_tensor(scratch, src, b(mx_), ALU.is_equal))
                link(dve.tensor_tensor(scratch, scratch, desc.unsqueeze(1).broadcast_to([P, T, n]), ALU.mult))
                link(dve.tensor_reduce(gmx, scratch, AX_X, ALU.max))
                link(dve.tensor_tensor(one, scratch, b(gmx), ALU.is_equal))

            gl, el = LG[:, :, 0:NG], LG[:, :, NG:]
            top(gl, const("gdesc"), gm, goh, ge, NG)
            dve.tensor_tensor(gd, gl, gm.unsqueeze(2).broadcast_to([P, T, NG]), ALU.subtract).then_inc(rexp_in, 1)
            link(dve.tensor_scalar(pen, goh, -1.0, -NEG, ALU.add, ALU.mult))
            e4 = lambda a: a.rearrange("p t (g e) -> p t g e", g=NG)
            for t in range(T):
                j = dve.tensor_tensor(ml[:, t, :].rearrange("p (g e) -> p g e", g=NG),
                                      el[:, t, :].rearrange("p (g e) -> p g e", g=NG),
                                      pen[:, t, :].unsqueeze(2).broadcast_to([P, NG, EG]), ALU.add)
            link(j)
            top(ml, const("desc"), m1, oh1, t32, NE)
            link(dve.scalar_tensor_tensor(out=ml, in0=oh1, scalar=3 * NEG, in1=ml, op0=ALU.mult, op1=ALU.add))
            top(ml, const("desc"), m2, oh2, t32, NE)
            dve.tensor_tensor(mm1, m2, m1, ALU.subtract).then_inc(rexp_in, 1)
            dve.tensor_tensor(M32, oh1, oh2, ALU.add).then_inc(m_done, 1)
            dve.wait_ge(m_done, 1)
            link(dve.tensor_tensor(t32, M32, const("tok1").unsqueeze(2).broadcast_to([P, T, NE]), ALU.mult))
            dve.scalar_tensor_tensor(out=Wt, in0=oh2, scalar=float(S), in1=t32, op0=ALU.mult, op1=ALU.add)
            dve.wait_ge(rexp_done, 1)
            link(dve.tensor_reduce(gsum, gd, AX_X, ALU.add))
            link(dve.reciprocal(gp, gsum))
            dve.wait_ge(rexp_done, 2)
            link(dve.tensor_scalar(den, e2, 1.0, None, ALU.add))
            link(dve.reciprocal(den, den))
            link(dve.tensor_tensor(gate0, gp, den, ALU.mult))
            dve.tensor_tensor(gate1, gate0, e2, ALU.mult)
            name = ("rank",)
            wait_full(dve, name)
            dve.tensor_copy(rank, psum(name)[:, 0:T * NE].rearrange("p (t n) -> p t n", t=T))
            link(dve.tensor_reduce(cmax, psum(name)[:, T * NE:(T + 1) * NE], AX_X, ALU.max))
            link(dve.tensor_scalar(t8, const("thr"), cmax, None, ALU.is_lt))
            link(dve.tensor_reduce(npf, t8, AX_X, ALU.add))
            for one_ahead in (idx_full, idx_ready, xt_full, xt_ready, up_full, hid_ready, ht_full, ht_ready, oyA, oyB):
                dve.sem_inc(one_ahead, 1)
            dve.tensor_copy(npi[:, :], npf).then_inc(route_done, 1)

            def entries(U, q, s, turned):
                dve.wait_ge(idx_full, U + 1)
                ev = lambda a: a[:, :, bass.ds(q * 2, 2)] if not isinstance(q, int) else a[:, :, 2 * q:2 * q + 2]
                b = lambda a: ev(a).unsqueeze(3).broadcast_to([P, T, 2, CAP])
                it = const("iota").unsqueeze(1).broadcast_to([P, 2 * T, CAP]).rearrange("p (t e) n -> p t e n", t=T)
                link2(dve.tensor_tensor(sel[:, :, :, :], it, b(rank), ALU.is_equal), U * 3 + 1)
                dve.tensor_tensor(selw[:, :, :, :], sel[:, :, :, :], b(Wt), ALU.mult).then_inc(sel_ready, 1)
                dve.wait_ge(idx_full, U + 2)
                link2(dve.tensor_scalar(emp[:, :], pb[0][:, 0:1], 0.0, 4.0 * 2 * S, ALU.is_equal, ALU.mult), U * 3 + 2)
                link2(dve.scalar_tensor_tensor(out=col(dsts, q), in0=pb[0][:, 0:1], scalar=-1.0, in1=emp[:, :],
                                               op0=ALU.add, op1=ALU.add), U * 3 + 3)
                dve.wait_ge(xt_full, turned + 1)
                dve.tensor_scalar(tok_i[s][:, :], col(dsts, q), S - 1, None, ALU.bitwise_and).then_inc(idx_ready, 1)

            def link2(ins, n):
                ins.then_inc(loop_self, 1)
                dve.wait_ge(loop_self, n)

            def col(a, q):
                return a[:, bass.ds(q, 1)] if not isinstance(q, int) else a[:, q:q + 1]

            def unit(U, q, s, use, nuse, ahead, more):
                if ahead:
                    entries(U + 3, q + 3, s, U + 1)
                dve.wait_ge(sa_ready, U + 1)
                dve.wait_ge(ht_full, U + 1)
                v = lambda a: a.rearrange("q (p c) -> q p c", c=2)
                dve.tensor_tensor(hid[:, :, :].rearrange("q c p -> q p c"), v(sa[:, :]), v(pb[3][:, FF:2 * FF]),
                                  ALU.mult).then_inc(hid_ready, 1)
                dve.wait_ge(slots_freed, U + 4)
                dve.wait_ge(scattered[s], use * 16 + 16)
                dve.tensor_copy(dst_i[s][:, :], col(dsts, q))
                dve.tensor_copy(oy[s][:, 0:512], pb[5][:, :]).then_inc(oyA, 1)

            def stop(p):
                dve.tensor_scalar(rank, rank, -float(CAP), None, ALU.add).then_inc(next_rank, 1)
                dve.wait_ge(next_rank, p + 1)

            dve.wait_ge(s_h2d, 16 * T)

            def start(p):
                for k in range(3):
                    entries(p * PAIRS + k, k, k, p * PAIRS)

            passes(dve, unit, start, stop)
            dve.wait_ge(s_fn, 16)
            for t in range(T):
                dve.wait_ge(s_y[t], 16)
                link(dve.scalar_tensor_tensor(out=x2[:, t, :], in0=yt[t][:, 0, :], scalar=gate0[:, t:t + 1],
                                              in1=x2[:, t, :], op0=ALU.mult, op1=ALU.add))
                dve.scalar_tensor_tensor(out=yt[t][:, 0, :], in0=yt[t][:, 1, :], scalar=gate1[:, t:t + 1],
                                         in1=x2[:, t, :], op0=ALU.mult, op1=ALU.add).then_inc(acc_done, 1)
            for t in range(T):
                dve.wait_ge(ssf_done, 2 * t + 2)
                link(dve.reciprocal(rf[:, t:t + 1], ssf[:, t:t + 1]))
                dve.scalar_tensor_tensor(out=x2[:, t, :], in0=yt[t][:, 0, :], scalar=rf[:, t:t + 1], in1=fnb[:, :],
                                         op0=ALU.mult, op1=ALU.mult).then_inc(fin_done, 1)


_INS = ["x", "norm1_w", "w_in", "fox_forget_bias", "gdn_conv_w", "gdn_a_log", "gdn_dt_bias", "gdn_norm_w", "w_out",
        "norm2_w", "router_group_w", "router_group_b", "router_expert_w", "router_expert_b",
        "expert_w1", "expert_w3", "expert_w2", "final_norm_w"]
_OUTS = [((1, S, D), "float32")]


def kernel(**inputs):
    import numpy as _np
    import concourse.bacc as _bacc
    from concourse import mybir as _mybir
    from concourse.bass_utils import run_bass_kernel_spmd as _run

    nc = _bacc.Bacc("TRN2", target_bir_lowering=False, num_devices=1)
    table = constant_table()
    arrays = {"const_dram": table}
    args = [nc.dram_tensor("const_dram", table.shape, _mybir.dt.from_np(table.dtype), kind="ExternalInput").ap()]
    for name in _INS:
        a = _np.ascontiguousarray(inputs[name])
        arrays[f"in_{name}_dram"] = a
        args.append(nc.dram_tensor(f"in_{name}_dram", a.shape, _mybir.dt.from_np(a.dtype), kind="ExternalInput").ap())
    for i, (shape, dtype) in enumerate(_OUTS):
        dt = _mybir.dt.from_np(_np.dtype(dtype))
        args.append(nc.dram_tensor(f"out_{i}_dram", shape, dt, kind="ExternalOutput").ap())
    build(nc, *args)
    r = _run(nc, [arrays], core_ids=[0])
    return r.results[0]["out_0_dram"]
```

```python
from contextlib import ExitStack
import math

import numpy as np

import concourse.bass as bass
from concourse import mybir

F32 = mybir.dt.float32
F32R = mybir.dt.float32r
I32 = mybir.dt.int32
U32 = mybir.dt.uint32
ACT = mybir.ActivationFunctionType
ALU = mybir.AluOpType
AX_X = mybir.AxisListType.X

P = 128
D = 1024
S = 512
T = S // P
KC = D // P
HK = KC // 2
NH = 4
HD = 64
GW = NH * P
EPS = 1e-6
NG = 4
EG = 8
NE = NG * EG
FF = 256
CAP = 64
PAIRS = NE // 2
NEG = -1e30
LEVELS = 6

FQ, FK, FV, FFG = 0, 256, 512, 768
RQ, RK, RV, RG = 772, 1028, 1284, 1540
GQ, GK, GV, GZ, GA, GB = 1796, 2308, 2820, 3332, 3844, 3848
WMAX = 260

GROUPS = [("n", "zb", GZ + 260, 260), ("n", "fv", FV, 260),
          ("t", "v0", GV, 256), ("t", "v1", GV + 256, 256), ("t", "k0", GK, 256), ("t", "k1", GK + 256, 256),
          ("t", "q0", GQ, 256), ("t", "q1", GQ + 256, 256),
          ("n", "rq", RQ, 256), ("n", "rk", RK, 256), ("n", "rv", RV, 256), ("n", "za", GZ, 260), ("n", "rg", RG, 256),
          ("t", "fq", FQ, 256), ("t", "fk", FK, 256)]
GIDX = {g[1]: i for i, g in enumerate(GROUPS)}
NIN = len(GROUPS)
NOUT = 4
GR_IN = 2 * NIN
GR = GR_IN + 2 * NOUT

AFTER = {g: [] for g in range(GR_IN)}
for _i in range(NIN):
    AFTER[2 * _i + 1].append(("evac", _i))
AFTER[3].append(("gates",))
AFTER[5].append(("gcum",))
AFTER[6] += [("vt", 0), ("vt", 1)]
AFTER[7].append(("cB",))
AFTER[8] += [("vt", 2), ("vt", 3)]
AFTER[9].append(("sq", 0, 0))
AFTER[11].append(("sq", 0, 1))
AFTER[12].append(("ss", 0))
AFTER[13].append(("sq", 1, 0))
AFTER[15].append(("sq", 1, 1))
AFTER[16] += [("ss", 1), ("kt",)]
AFTER[17] += [("prep", 0), ("prep", 1)]
AFTER[18].append(("xt", 0))
for _i in range(LEVELS):
    AFTER[18 + _i].append(("lv", 0, _i))
AFTER[24] += [("fin", 0), ("prep", 2), ("prep", 3)]
AFTER[25].append(("xt", 1))
for _i in range(LEVELS - 1):
    AFTER[25 + _i].append(("lv", 1, _i))
AFTER[26].append(("silu",))
AFTER[29] += [("lv", 1, LEVELS - 1), ("fin", 1)]

FOX = [(u // T, u % T) for u in range(NH * T)]
KSTEPS = len(FOX) + 2
WS = {3 * n: n for n in range(1, T)}
OO = {3 * n + 1: n for n in range(T)}
RS = {3 * n + 2: n for n in range(NH)}
RO = {3 * n + 3: n for n in range(NH)}
MT = [0, 1, 4, 5, 6, 7, 2, 3]
PW = [S - j * P for j in range(T)]
POFF = [sum(PW[:j]) for j in range(T)]


def tensor_orders():
    a, b = [("par",)] + [("xT", t, i) for t in range(T) for i in range(2)], []
    for g in range(GR_IN):
        if g % 2 == 0:
            kind = GROUPS[g // 2][0]
            a += [("y", g // 2, n) for n in range(T if kind == "n" else 2)]
        for task in AFTER[g]:
            if task[0] == "vt":
                b.append(task)
            elif task[0] == "gcum":
                b.append(task)
            elif task[0] == "cB":
                b += [("cB", h) for h in range(NH)]
            elif task[0] == "ss":
                b.append(task)
            elif task[0] == "kt":
                b += [("kt", h) for h in range(NH)]
            elif task[0] == "prep":
                b += [(n, task[1]) for n in ("gcB", "bB", "KK", "QK")]
            elif task[0] == "xt":
                b += [("XT", 2 * task[1]), ("XT", 2 * task[1] + 1)]
            elif task[0] == "lv":
                _, pr, lv = task
                b += [("Y", 2 * pr, lv), ("Y", 2 * pr + 1, lv)]
                if lv:
                    b += [("UT", 2 * pr, lv), ("UT", 2 * pr + 1, lv)]
                b += [("Xp" if lv < LEVELS - 1 else "Up", 2 * pr + i, lv) for i in range(2)]
            elif task[0] == "fin":
                for t in (2 * task[1], 2 * task[1] + 1):
                    b += [("wT", t), ("u0", t)]
    b += [("rT", i) for i in range(4)]
    for k in range(KSTEPS):
        if k < 16:
            a.append(("fS", k))
        if 1 <= k <= 16:
            a.append(("fT", k - 1))
        if k >= 2:
            a.append(("fO", k - 2))
        if k in WS:
            b.append(("wS", WS[k]))
        if k in OO:
            b.append(("o", OO[k]))
            if OO[k] < T - 1:
                b.append(("Sp", OO[k]))
        if k in RS:
            b += [("rS", RS[k], j) for j in range(T)]
        if k in RO:
            b.append(("rO", RO[k]))
    a += [("mT", c) for c in MT]
    for n in range(NOUT):
        a += [("y", NIN + n, t) for t in range(T)]
    b += [("hT", 0), ("hT", 1), ("lgT",)] + [("hT", c) for c in range(2, KC)] + [("lg",), ("rank",)]
    return a, b


ORDER_A, ORDER_B = tensor_orders()
BANK = {}
for _base, _order in ((0, ORDER_A), (4, ORDER_B)):
    _uses, _at, _held = [0] * 4, 0, None
    for _name in _order:
        if _at % 4 == _held:
            _at += 1
        _b = _at % 4
        BANK[_name] = (_base + _b, _uses[_b])
        _uses[_b] += 1
        if _name == ("lgT",):
            _held = _b
        _at += 1

CONST = {}
_at = 0
for _name, _n in [("ident", P), ("eps", 1), ("eps128", 1), ("ones", P), ("iota", CAP), ("tok1", T), ("thr", 8),
                  ("desc", NE), ("gdesc", NG), ("rankm", P), ("tri", P), ("strict", P), ("negmask", P), ("nM1", P),
                  ("cos", T * 32), ("sin", T * 32), ("nM", LEVELS * P), ("dm", NH * S)]:
    CONST[_name] = (_at, _n)
    _at += _n
NCONST = _at
NSTAY = CONST["tri"][0]


def constant_table():
    c = np.zeros((P, NCONST), np.float32)

    def put(name, v):
        a, n = CONST[name]
        c[:, a:a + n] = np.asarray(v, np.float32).reshape(P, n)

    r = np.arange(P)
    row, col = r[:, None], r[None, :]
    put("tri", row <= col)
    put("rankm", row < col)
    put("ident", row == col)
    put("strict", row < col)
    put("ones", np.ones((P, P)))
    put("negmask", np.where(col > row, NEG, 0.0))
    put("nM1", -((row % 2 == 0) & (col == row + 1)).astype(np.float32))
    lv = []
    for n in range(LEVELS):
        b = 2 << n
        lv.append(-((row // (2 * b) == col // (2 * b)) & (row % (2 * b) >= b) & (col % (2 * b) < b)).astype(np.float32))
    put("nM", np.stack(lv, 1))
    dm = []
    for h in range(NH):
        rel = np.arange(S)[None, :] - row
        dm.append(np.where(rel >= 0, np.exp(np.maximum(rel, 0) * math.log1p(-(2.0 ** (-5 - h)))), 0.0) * HD ** -0.5)
    put("dm", np.stack(dm, 1))
    lin = (np.arange(HD // 2, dtype=np.float32) / np.float32(HD // 2 - 1)).astype(np.float32)
    inv = (np.float32(1.0) / np.power(np.float32(10000.0), lin).astype(np.float32)).astype(np.float32)
    pos = (np.arange(T)[None, :] * P + row).astype(np.float32)
    ang = (pos[:, :, None] * inv[None, None, :]).astype(np.float32).astype(np.float64)
    put("cos", np.cos(ang))
    put("sin", np.sin(ang))
    put("iota", np.tile(np.arange(CAP), (P, 1)))
    put("tok1", pos + 1)
    put("thr", np.tile(np.arange(8) * CAP, (P, 1)))
    put("desc", np.tile(NE - np.arange(NE), (P, 1)))
    put("gdesc", np.tile(NG - np.arange(NG), (P, 1)))
    put("eps", np.full((P, 1), EPS))
    put("eps128", np.full((P, 1), EPS * P))
    return c


def build(nc, consts, x, n1w, w_in, foxb, convw, alog, dtb, gnw, w_out, n2w, rgw, rgb, rew, reb,
          ew1, ew3, ew2, fnw, out):
    KB = 1024
    BASE = 16512
    C0 = 0
    R1 = 17 * KB
    R2 = R1 + 32 * KB
    RM = R2 + 29 * KB
    R7 = RM + 16 * KB
    R8 = R7 + 12 * KB
    R9 = R8 + 12 * KB
    R5 = R9 + 20 * KB
    R4 = R5 + 8 * KB
    R3 = R4 + 20 * KB
    with ExitStack() as ctx:
        def at(name, shape, offset, dt=F32):
            return nc.alloc_sbuf_tensor_at(name, shape, dt, offset=BASE + offset)

        def sem(name):
            return ctx.enter_context(nc.semaphore(name))

        arena = ctx.enter_context(nc.sbuf_tensor("arena", [P, (229344 - BASE) // 4 - 16], F32))
        CT = at("CT", [P, NCONST], C0)

        def const(name, *dims):
            a, n = CONST[name]
            v = CT[:, a:a + n]
            return v if not dims else v.rearrange(dims[0], **dims[1])

        tri, ident, strict, negmask = const("tri"), const("ident"), const("strict"), const("negmask")
        ones, eps = const("ones"), const("eps")
        nM = const("nM", "p (l n) -> p l n", dict(l=LEVELS))
        dm = const("dm", "p (h n) -> p h n", dict(h=NH))
        cosT = const("cos", "p (t n) -> p t n", dict(t=T))
        sinT = const("sin", "p (t n) -> p t n", dict(t=T))

        q0 = 17 * KB - 992
        assert NCONST * 4 <= q0 - 64
        PDT = at("PDT", [P, 4], q0 + 32)
        PAL = at("PAL", [P, 4], q0 + 64)
        PFB = at("PFB", [P, 4], q0 + 96)
        PRB = at("PRB", [P, NG + NE], q0 + 128)
        PCW = at("PCW", [P, 4, 12], q0 + 288)
        PGN = at("PGN", [P, P], q0 + 480)
        assert q0 + 480 + 512 <= R1
        hHi = at("hHi", [P, KC, S], R1, F32R)
        hLo = at("hLo", [P, KC, S], R1 + 16 * KB, F32R)
        gsz = HK * WMAX * 4
        raw = [at(f"raw{i}", [P, HK, WMAX], R2 + i * gsz) for i in range(3)]
        whi = [at(f"whi{i}", [P, HK, WMAX], R2 + (3 + i) * gsz, F32R) for i in range(2)]
        wlo = [at(f"wlo{i}", [P, HK, WMAX], R2 + (5 + i) * gsz, F32R) for i in range(2)]
        assert 7 * gsz <= 29 * KB
        X0 = at("X0", [P, T, D], RM)
        mix = at("mix", [P, T, D], RM)
        rq = at("rq", [P, T, 256], R7)
        rk = at("rk", [P, T, 256], R7 + 4 * KB)
        rv = at("rv", [P, T, 256], R7 + 8 * KB)
        oret = at("oret", [P, T, 256], R7)
        osq = at("osq", [P, T, 256], R7 + 4 * KB)
        fqT = at("fqT", [P, 2, S], R8)
        fkT = at("fkT", [P, 2, S], R8 + 4 * KB)
        fv = at("fv", [P, T, 256], R8 + 8 * KB)
        cB8 = at("cB8", [P, NH, S], R9)
        n1b = at("n1b", [P, D], R9 + 12 * KB)
        PW48 = at("PW48", [4 * 12, P], R9)
        rqs = at("rqs", [P, 16], q0 - 64)
        junk = at("junk", [P, D], R9 + 8 * KB)
        cacc = [at(f"cacc{i}", [P, S], R9 + (8 + 2 * i) * KB) for i in range(2)]
        vS = [at(f"vS{i}", [P, S], R9 + (12 + 2 * i) * KB) for i in range(2)]
        nrm = [at(f"nrm{i}", [P, S], R4 + 2 * i * KB) for i in range(4)]
        rtmp = [at(f"rtmp{i}", [P, T, NH, 32], R9 + (8 + 2 * i) * KB) for i in range(4)]
        Sx = [at(f"Sx{i}", [P, S], R9 + (8 + 2 * i) * KB) for i in range(2)]
        Pf = [at(f"Pf{i}", [P, S], R9 + (12 + 2 * i) * KB) for i in range(2)]
        PT = [at(f"PT{i}", [P, T, P], R9 + (16 + 2 * i) * KB) for i in range(2)]
        small = at("small", [P, 1024], R9 + 16 * KB)
        attnT = at("attnT", [P, T, NH, P], R5)
        def pair(name, slot):
            return [at(f"{name}{i}", [P, NH, P], R4 + (slot * 2 + i) * 2 * KB) for i in range(2)]
        Nm, Xm, Um, Ym, Dm = (pair(n, i) for i, n in enumerate(("Nm", "Xm", "Um", "Ym", "Dm")))
        rqT = at("rqT", [P, 2, S], R4)
        rkT = at("rkT", [P, 2, S], R4 + 4 * KB)
        retP = at("retP", [P, sum(PW)], R4 + 8 * KB)
        St = at("St", [P, NH, P], R4 + 18 * KB)
        qT = at("qT", [P, NH, S], R3)
        kT = at("kT", [P, NH, S], R3 + 8 * KB)
        vb = at("vb", [P, T, NH, P], R3 + 16 * KB)
        kbg = at("kbg", [P, T, NH, P], R3 + 24 * KB)
        ktail = at("ktail", [P, T, NH, P], R3 + 32 * KB)
        gsq = [at(f"gsq{t}", [P, NH, P], R3 + (8 + 2 * t) * KB) for t in range(T)]
        sm0 = -(-(R2 + 7 * gsz) // 32) * 32
        keep = at("keep", [P, 136], sm0)
        assert sm0 + 544 <= RM
        ssx, rx = keep[:, 0:4], keep[:, 4:8]
        egl = keep[:, 8:24]
        mx, nmx, rs, ri = keep[:, 24:40], keep[:, 40:56], keep[:, 56:72], keep[:, 72:88]
        ssn, rn, ssx4 = keep[:, 88:104], keep[:, 104:120], keep[:, 120:136]
        def sml(a, n):
            return small[:, a:a + n]
        GAB = sml(0, 32).rearrange("p (t n) -> p t n", t=T)
        FFT = sml(32, 16).rearrange("p (t n) -> p t n", t=T)
        z8 = sml(48, 32).rearrange("p (t n) -> p t n", t=T)
        az, e8, dd, sv, qv, hv = (sml(80 + 32 * i, 32).rearrange("p (t n) -> p t n", t=T) for i in range(6))
        eb, beta, gg, ea = sml(272, 16), sml(288, 16), sml(304, 16), sml(320, 4)
        cum = sml(336, 48)
        c8, egc, tl, etl, bgc, sp8 = sml(384, 16), sml(400, 16), sml(416, 16), sml(432, 16), sml(448, 16), sml(464, 32)
        sp8 = sp8.rearrange("p (t n) -> p t n", t=T)
        lf, lfc = sml(496, 16), sml(608, 16)
        ssk, ssq, rks, br, bgr, etr = (sml(512 + 16 * i, 16) for i in range(6))

        pb = [ctx.enter_context(nc.psum_tensor(f"bank{i}", [P, 512], F32)) for i in range(8)]

        full = [sem(f"full{i}") for i in range(8)]
        free = [sem(f"free{i}") for i in range(8)]
        s_const = sem("s_const"); s_const2 = sem("s_const2"); s_n1 = sem("s_n1"); s_cw = sem("s_cw"); s_par = sem("s_par")
        s_x = [sem(f"s_x{t}") for t in range(T)]
        raw_full = [sem(f"raw_full{i}") for i in range(3)]
        whi_done = sem("whi_done"); wlo_done = sem("wlo_done"); half_used = sem("half_used")
        ssx_done = sem("ssx_done"); xn_done = sem("xn_done"); hhi_done = sem("hhi_done")
        act_self = sem("act_self"); dve_self = sem("dve_self"); pool_self = sem("pool_self")
        tap0_done = sem("tap0_done"); silu_done = sem("silu_done")
        z_in = sem("z_in"); gexp_in = sem("gexp_in"); gexp_done = sem("gexp_done"); gates_done = sem("gates_done")
        cum_done = sem("cum_done"); cexp_done = sem("cexp_done")
        vb_done = sem("vb_done"); cB_done = sem("cB_done")
        sq_done = sem("sq_done"); root_done = sem("root_done"); ss_read = sem("ss_read"); kt_done = sem("kt_done")
        d_raw = sem("d_raw"); d_exp = sem("d_exp"); ds_ready = sem("ds_ready")
        di_ready = sem("di_ready"); qg_ready = sem("qg_ready")
        uinit = sem("uinit")
        y_copied = sem("y_copied")
        rot_done = sem("rot_done")
        sx_ready = sem("sx_ready"); pf_ready = sem("pf_ready")
        zg_done = sem("zg_done"); sqr_done = sem("sqr_done"); ssr_done = sem("ssr_done"); rtr_done = sem("rtr_done")
        mixr_done = sem("mixr_done"); mixg_done = sem("mixg_done"); rk_done = sem("rk_done"); silu2_done = sem("silu2_done"); s_x2 = sem("s_x2in")
        s_out = sem("s_out")

        def psum(name):
            return pb[BANK[name][0]]

        def wait_full(e, name):
            b, n = BANK[name]
            e.wait_ge(full[b], n + 1)

        def wait_read(e, name):
            b, n = BANK[name]
            e.wait_ge(free[b], n + 1)

        def release(ins, name):
            return ins.then_inc(free[BANK[name][0]], 1)

        tcol = {"v0": 8, "v1": 10, "k0": 4, "k1": 6, "q0": 0, "q1": 2}
        CONVN = {"v0": 0, "v1": 2, "k0": 4, "k1": 6, "q0": 8, "q1": 10}
        x2 = at("x2", [P, T, D], R3)

        SLOT = [113 * KB, 65 * KB, 17 * KB]
        W13_AT = [SLOT[0], SLOT[1] + 16 * KB, SLOT[2]]
        W2_AT = [SLOT[0] + 32 * KB, SLOT[1], SLOT[2] + 32 * KB]
        x2T = at("x2T", [P, KC, S], R3 + 16 * KB)
        sqj = at("sqj", [P, 256], R3 + 32 * KB)
        h2 = at("h2", [P, T, D], R3 + 16 * KB)
        rtA = at("rtA", [P, 1024], R3 + 32 * KB)
        n2b = at("n2b", [P, D], 161 * KB)
        rtB = at("rtB", [P, 1024], R3 + 36 * KB)
        fnb = at("fnb", [P, D], SLOT[2])
        rw = at("rw", [P, KC, NG + NE], R3 + 40 * KB)
        n2p = at("n2p", [P, KC], R3 + 40 * KB + KC * (NG + NE) * 4)
        lgs = at("lgs", [P, S], R3 + 38 * KB)
        assert R3 + 40 * KB + KC * (NG + NE + 1) * 4 <= 229344 - BASE
        w13 = [at(f"w13_{i}", [P, 2, 2, KC * FF], W13_AT[i]) for i in range(3)]
        w2 = [at(f"w2_{i}", [P, 2, 2 * D], W2_AT[i]) for i in range(3)]
        xT = at("xT", [P, KC, P], 161 * KB)
        xg = [at(f"xg{i}", [P, D], R3 + (16 + 4 * i) * KB) for i in range(3)]
        oy0 = C0 + -(-NSTAY * 4 // 32) * 32
        oy = [at(f"oy{i}", [P, D], oy0 + 4 * i * KB) for i in range(3)]
        assert oy0 + 12 * KB <= q0
        sa = at("sa", [P, FF], R3 + 28 * KB)
        hid = at("hid", [P, 2, P], R3 + 29 * KB)
        hidT = at("hidT", [P, 2, P], R3 + 30 * KB)
        sel = at("sel", [P, T, 2, CAP], R3 + 36 * KB)
        selw = at("selw", [P, T, 2, CAP], R3 + 38 * KB)
        ix0 = R3 + 41 * KB + 192
        emp = at("emp", [P, 1], ix0)
        dst_i = [at(f"dst{i}", [P, 1], ix0 + 32 * (i + 1), I32) for i in range(3)]
        tok_i = [at(f"tok{i}", [P, 1], ix0 + 32 * (i + 4), I32) for i in range(3)]
        dsts = at("dsts", [P, PAIRS], ix0 + 224, I32)
        assert ix0 + 224 + 4 * PAIRS <= 229344 - BASE
        yt = [at(f"yt{i}", [P, 2, D], SLOT[0] + 8 * KB * i) for i in range(T)]
        jk = at("jk", [P, D], SLOT[0] + 32 * KB)
        rv4 = lambda a, n, w: (rtA if n == 0 else rtB)[:, a:a + T * w].rearrange("p (t n) -> p t n", t=T)
        Wt, rank, oh1, oh2, LG = rv4(0, 0, NE), rv4(128, 0, NE), rv4(256, 0, NE), rv4(384, 0, NE), rv4(512, 0, NG + NE)
        r1 = lambda i: rtA[:, 656 + 4 * i:660 + 4 * i]
        gm, gmx, gsum, gp, m1, m2, mm1, e2, den, gate0, gate1, ss2, r2, ssf, rf = (r1(i) for i in range(15))
        ssp = rtA[:, 740:756]
        Mc = rtA[:, 760:760 + (T + 1) * NE]
        cmax = rtA[:, 720:721]
        npf = rtA[:, 721:722]
        npi = at("npi", [P, 1], R3 + 32 * KB + 4 * 736, I32)
        ml, t32, M32, ge = rv4(0, 1, NE), rv4(128, 1, NE), rv4(256, 1, NE), rv4(384, 1, NG)
        goh, gd, pen, t8 = rv4(400, 1, NG), rv4(416, 1, NG), rv4(432, 1, NG), rtB[:, 448:456]

        h2d = nc.dram_tensor("h2d", [S, D], F32, kind="Internal")
        yd = nc.dram_tensor("yd", [2 * S, D], F32, kind="Internal")
        w1v = ew1[0].rearrange("g e (p c) f -> (g e) p (c f)", c=KC)
        w3v = ew3[0].rearrange("g e (p c) f -> (g e) p (c f)", c=KC)
        w2v = ew2[0].rearrange("g e (p c) d -> (g e) p (c d)", c=2)
        outv = out[0].rearrange("(t p) d -> t p d", p=P)

        s_n2 = sem("s_n2"); s_rw = sem("s_rw"); ss2_done = sem("ss2_done"); h2_done = sem("h2_done"); s_h2d = sem("s_h2d")
        h2p_done = sem("h2p_done"); rf_done = sem("rf_done"); fins_done = sem("fins_done"); finp_done = sem("finp_done"); rx4_done = sem("rx4_done"); one_set = sem("one_set"); pass_done = sem("pass_done"); h2s_done = sem("h2s_done"); rw_ready = sem("rw_ready"); lg_used = sem("lg_used"); ssp_done = sem("ssp_done"); ssp_sum = sem("ssp_sum"); r2_done = sem("r2_done")
        rexp_in = sem("rexp_in"); rexp_done = sem("rexp_done")
        m_done = sem("m_done"); route_done = sem("route_done")
        slots_freed = sem("slots_freed")
        w1_full = [sem(f"w1_full{i}") for i in range(3)]
        w3_full = [sem(f"w3_full{i}") for i in range(3)]
        w2_full = [sem(f"w2_full{i}") for i in range(3)]
        sel_ready = sem("sel_ready"); idx_full = sem("idx_full"); idx_ready = sem("idx_ready"); gathered = [sem(f"gathered{i}") for i in range(3)]
        xt_full = sem("xt_full"); xt_ready = sem("xt_ready"); up_full = sem("up_full"); gate_full = sem("gate_full"); sa_ready = sem("sa_ready"); loop_self = sem("loop_self"); next_rank = sem("next_rank"); pool_step = sem("pool_step")
        hid_ready = sem("hid_ready"); ht_full = sem("ht_full"); ht_ready = sem("ht_ready")
        oyA = sem("oyA"); oyB = sem("oyB"); scattered = [sem(f"scattered{i}") for i in range(3)]; s_fn = sem("s_fn")
        s_y = [sem(f"s_y{t}") for t in range(T)]
        acc_done = sem("acc_done"); ssf_done = sem("ssf_done"); fin_done = sem("fin_done")

        def turned_view(a):
            return a.rearrange("q (c p) -> q p c", c=KC)

        def plain_view(a):
            return a.rearrange("q (p c) -> q p c", c=KC)

        def passes(e, unit, start, stop=None):
            e.wait_ge(route_done, 1)
            start(0)
            n = e.value_load(npi[0:1, 0:1], min_val=1, max_val=S // CAP)
            with e.Fori(0, n) as p:

                def of(i, s):
                    n0, n12 = p * 6 + i, p * 5 + i
                    return p * PAIRS + i * 3 + s, i * 3 + s, s, n12 if s else n0, n0 + 1 if s == 2 else n12

                with e.Fori(0, 4) as i:
                    for s in range(3):
                        unit(*of(i, s), 2, True)
                unit(*of(4, 0), 1, True)
                unit(*of(4, 1), 0, True)
                unit(*of(4, 2), 0, True)
                unit(*of(5, 0), 0, False)
                if stop is not None:
                    stop(p)
                e.sem_inc(pass_done, 1)
                with e.If(p + 1 < n):
                    start(p + 1)

        block = ctx.enter_context(nc.Block())

        @block.sync
        def _(sp):
            for t in range(T):
                sp.dma_start(X0[:, t, :], x[0, t * P:(t + 1) * P, :]).then_inc(s_x[t], 16)
                if t == 0:
                    sp.dma_start(CT[:, 0:NSTAY], consts[:, 0:NSTAY]).then_inc(s_const, 16)
                if t == 1:
                    sp.dma_start(n1b[:, :], n1w[0:1, :].broadcast_to([P, D])).then_inc(s_n1, 16)

            def granule(g):
                if g >= 3:
                    sp.wait_ge(wlo_done, g - 2)
                if g < GR_IN:
                    _, _, c0, w = GROUPS[g // 2]
                    src = w_in[0]
                else:
                    c0, w = 256 * ((g - GR_IN) // 2), 256
                    src = w_out[0]
                k0 = (g % 2) * HK * P
                sp.dma_start(raw[g % 3][:, :, 0:w],
                             src[k0:k0 + HK * P, c0:c0 + w].rearrange("(c p) n -> p c n", p=P)
                             ).then_inc(raw_full[g % 3], 16)

            for g in range(3):
                granule(g)
            sp.dma_start(CT[:, NSTAY:], consts[:, NSTAY:]).then_inc(s_const2, 16)
            for dst, src in ((PDT[:, :], dtb[0:1, :].broadcast_to([P, 4])),
                             (PAL[:, :], alog[0:1, :].broadcast_to([P, 4])),
                             (PFB[:, :], foxb[0:1, :].broadcast_to([P, 4])),
                             (PRB[:, 0:NG], rgb[0:1, :].broadcast_to([P, NG])),
                             (PRB[:, NG:], reb.rearrange("a g e -> a (g e)").broadcast_to([P, NE])),
                             (PGN[:, :], gnw[0:1, :].broadcast_to([P, P]))):
                sp.dma_start(dst, src).then_inc(s_par, 16)
            for g in range(3, GR_IN + 4):
                granule(g)
            sp.wait_ge(mixg_done, NH)
            for t in range(T):
                sp.dma_start(x2[:, t, :], x[0, t * P:(t + 1) * P, :]).then_inc(s_x2, 16)
            sp.dma_start(n2p[:, :], n2w[0].rearrange("(c p) -> p c", p=P),
                         allow_slow_non_contiguous=True).then_inc(s_rw, 16)
            sp.dma_start(rw[:, :, 0:NG], rgw[0].rearrange("(c p) g -> p c g", p=P)).then_inc(s_rw, 16)
            sp.dma_start(rw[:, :, NG:], rew[0].rearrange("(c p) g -> p c g", p=P)).then_inc(s_rw, 16)

            def pick(q):
                return bass.ds(q * 2, 2) if not isinstance(q, int) else slice(2 * q, 2 * q + 2)

            def load_w1(q, s):
                sp.dma_start(w13[s][:, :, 0, :], w1v[pick(q)].rearrange("e p n -> p e n")).then_inc(w1_full[s], 16)

            def load_w3(q, s):
                sp.dma_start(w13[s][:, :, 1, :], w3v[pick(q)].rearrange("e p n -> p e n")).then_inc(w3_full[s], 16)

            def load_w2(q, s):
                sp.dma_start(w2[s][:, :, :], w2v[pick(q)].rearrange("e p n -> p e n")).then_inc(w2_full[s], 16)

            def load(U, q, s, behind=3):
                sp.wait_ge(gate_full, U - behind + 2)
                load_w1(q, s)
                sp.wait_ge(up_full, U - behind + 2)
                load_w3(q, s)
                sp.wait_ge(slots_freed, U + 4 - behind)
                load_w2(q, s)

            granule(GR_IN + 4)
            sp.wait_ge(slots_freed, 1)
            load_w1(0, 0)
            granule(GR_IN + 5)
            load_w3(0, 0)
            sp.dma_start(n2b[:, :], n2w[0:1, :].broadcast_to([P, D])).then_inc(s_n2, 16)
            granule(GR_IN + 6)
            load_w2(0, 0)
            granule(GR_IN + 7)
            wait_read(sp, ("mT", MT[-1]))
            load_w1(1, 1)
            load_w3(1, 1)
            sp.wait_ge(slots_freed, 3)
            load_w2(1, 1)
            for t in range(T):
                if t < T // 2:
                    sp.wait_ge(h2_done, t + 1)
                else:
                    sp.wait_ge(h2p_done, t - T // 2 + 1)
                sp.dma_start(h2d.ap()[t * P:(t + 1) * P, :], h2[:, t, :]).then_inc(s_h2d, 16)
            load_w1(2, 2)
            load_w3(2, 2)
            sp.wait_ge(gathered[0], 16)
            load_w2(2, 2)
            sp.wait_ge(route_done, 1)
            n = sp.value_load(npi[0:1, 0:1], min_val=1, max_val=S // CAP)
            with sp.Fori(0, n) as p:
                with sp.Fori(1, 5) as i:
                    for s in range(3):
                        load(p * PAIRS + i * 3 + s, i * 3 + s, s)
                load(p * PAIRS + 15, 15, 0)
                with sp.If(p + 1 < n):
                    for s in range(3):
                        load(p * PAIRS + PAIRS + s, s, s, 1 if s == 0 else 3)
            sp.wait_ge(slots_freed, n * PAIRS + 2)
            sp.dma_start(fnb[:, :], fnw.rearrange("(a d) -> a d", a=1).broadcast_to([P, D])).then_inc(s_fn, 16)
            for s in range(3):
                sp.wait_ge(scattered[s], n * (96 if s == 0 else 80) + 16)
            for t in range(T):
                sp.dma_start(yt[t][:, :, :], yd.ap().rearrange("(k t p) d -> t p k d", k=2, p=P)[t]).then_inc(s_y[t], 16)
            for t in range(T):
                if t < T - 1:
                    sp.wait_ge(finp_done, t + 1)
                else:
                    sp.wait_ge(fin_done, 1)
                sp.dma_start(outv[t], x2[:, t, :]).then_inc(s_out, 16)
            sp.wait_ge(s_out, 16 * T)

        @block.tensor
        def _(pe):
            order = {0: list(ORDER_A), 1: list(ORDER_B)}

            def begin(name):
                b, n = BANK[name]
                assert order[b // 4].pop(0) == name, name
                if n:
                    pe.wait_ge(free[b], n)
                return pb[b]

            def end(ins, name):
                ins.then_inc(full[BANK[name][0]], 1)

            def granule(g):
                pe.wait_ge(wlo_done, g + 1)
                half = g % 2
                n = g // 2
                hi, lo = whi[g % 2], wlo[g % 2]
                kind, w = ("n", 256) if g >= GR_IN else (GROUPS[n][0], GROUPS[n][3])
                for b in range(T if kind == "n" else 2):
                    name = ("y", n, b)
                    ps = begin(name) if half == 0 else psum(name)
                    if g == 0:
                        wait_read(pe, ("xT", b, 0))
                        wait_read(pe, ("xT", b, 1))
                    for c in range(HK):
                        kc = half * HK + c
                        if kind == "n":
                            tk = slice(b * P, (b + 1) * P)
                            o = ps[:, 0:w]
                            terms = ((hHi[:, kc, tk], hi[:, c, 0:w]), (hHi[:, kc, tk], lo[:, c, 0:w]),
                                     (hLo[:, kc, tk], hi[:, c, 0:w]))
                        else:
                            ch = slice(b * P, (b + 1) * P)
                            o = ps[:, :]
                            terms = ((hi[:, c, ch], hHi[:, kc, :]), (hi[:, c, ch], hLo[:, kc, :]),
                                     (lo[:, c, ch], hHi[:, kc, :]))
                        for i, (l, r) in enumerate(terms):
                            m = pe.matmul(o, l, r, start=(kc == 0 and i == 0), stop=(kc == KC - 1 and i == 2),
                                          skip_group_check=True)
                    if half == 1:
                        end(m, name)
                if half == 0:
                    m.then_inc(half_used, 1)

            def four(name, f):
                ps = begin(name)
                for h in range(NH):
                    o = ps[:, h * P:(h + 1) * P]
                    m = f(h, o)
                end(m, name)

            def mm(o, l, r):
                return pe.matmul(o, l, r, start=True, stop=True)

            def task(k):
                if k[0] == "vt":
                    h = k[1]
                    pe.wait_ge(silu_done, h + 1)
                    four(k, lambda t, o: pe.transpose(o, vS[h % 2][:, t * P:(t + 1) * P], ident))
                elif k[0] == "gcum":
                    pe.wait_ge(gates_done, 1)
                    ps = begin(k)
                    mm(ps[:, 0:16], tri, gg)
                    mm(ps[:, 16:32], ones, gg)
                    pe.matmul(ps[:, 32:48], tri, lf, start=True, stop=False)
                    end(pe.matmul(ps[:, 32:48], ones, lfc, start=False, stop=True), k)
                elif k[0] == "cB":
                    pe.wait_ge(cum_done, 2)
                    for h in range(NH):
                        four(("cB", h), lambda t, o: mm(o, c8[:, 4 * t + h:4 * t + h + 1].broadcast_to([P, P]), ident))
                elif k[0] == "ss":
                    ps = begin(k)
                    for h in range(NH):
                        pe.wait_ge(sq_done, NH * k[1] + h + 1)
                        for t in range(T):
                            m = mm(ps[:, 4 * t + h:4 * t + h + 1], nrm[h][:, t * P:(t + 1) * P], ones[:, 0:1])
                    end(m, k)
                elif k[0] == "kt":
                    for h in range(NH):
                        four(("kt", h), lambda t, o: pe.transpose(o, kT[:, h, t * P:(t + 1) * P], ident))
                elif k[0] == "prep":
                    t = k[1]
                    tk = slice(t * P, (t + 1) * P)
                    pe.wait_ge(rk_done, 1)
                    four(("gcB", t), lambda h, o: mm(o, cum[:, 4 * t + h:4 * t + h + 1].broadcast_to([P, P]), ident))
                    four(("bB", t), lambda h, o: mm(o, br[:, 4 * t + h:4 * t + h + 1].broadcast_to([P, P]), ident))
                    four(("KK", t), lambda h, o: mm(o, kT[:, h, tk], kT[:, h, tk]))
                    four(("QK", t), lambda h, o: mm(o, kT[:, h, tk], qT[:, h, tk]))
                elif k[0] == "xt":
                    for t in (2 * k[1], 2 * k[1] + 1):
                        pe.wait_ge(uinit, t + 1)
                        four(("XT", t), lambda h, o: pe.transpose(o, Um[t % 2][:, h, :], ident))
                elif k[0] == "lv":
                    _, pr, lv = k
                    for i in range(2):
                        t = 2 * pr + i
                        wait_read(pe, ("Xp", t, lv - 1) if lv else ("XT", t))
                        four(("Y", t, lv), lambda h, o: mm(o, Nm[i][:, h, :], Xm[i][:, h, :]))
                    if lv:
                        for i in range(2):
                            four(("UT", 2 * pr + i, lv), lambda h, o: pe.transpose(o, Xm[i][:, h, :], ident))
                    for i in range(2):
                        t = 2 * pr + i
                        wait_read(pe, ("Y", t, lv))
                        if lv:
                            wait_read(pe, ("UT", t, lv))
                        if lv < LEVELS - 1:
                            four(("Xp", t, lv), lambda h, o: mm(o, Um[i][:, h, :], Ym[i][:, h, :]))
                        else:
                            four(("Up", t, lv), lambda h, o: mm(o, Ym[i][:, h, :], Um[i][:, h, :]))
                elif k[0] == "fin":
                    for i in range(2):
                        t = 2 * k[1] + i
                        wait_read(pe, ("Up", t, LEVELS - 1))
                        pe.wait_ge(kt_done, NH)
                        four(("wT", t), lambda h, o: mm(o, kbg[:, t, h, :], Um[i][:, h, :]))
                        four(("u0", t), lambda h, o: mm(o, Um[i][:, h, :], vb[:, t, h, :]))

            pe.wait_ge(s_const, 16)
            pe.wait_ge(s_cw, 16)
            name = ("par",)
            end(pe.transpose(begin(name)[:, 0:48], PW48[:, :], ident[0:48, 0:48]), name)
            for t in range(T):
                pe.wait_ge(xn_done, t + 1)
                for i in range(2):
                    four(("xT", t, i), lambda c, o: pe.transpose(o, X0[:, t, (4 * i + c) * P:(4 * i + c + 1) * P], ident))
            for g in range(GR_IN):
                granule(g)
                for k in AFTER[g]:
                    task(k)

            for i in range(4):
                src = rq if i < 2 else rk
                pe.wait_ge(rot_done, 1 if i < 2 else 2)
                four(("rT", i), lambda t, o: pe.transpose(o, src[:, t, (i % 2) * P:(i % 2 + 1) * P], ident))
            pe.wait_ge(y_copied, 6)
            for k in range(KSTEPS):
                if k < 16:
                    h, t = FOX[k]
                    hp = slice((h % 2) * HD, (h % 2) * HD + HD)
                    name = ("fS", k)
                    ps = begin(name)
                    w = (t + 1) * P
                    pe.matmul(ps[:, 0:w], fqT[hp, h // 2, t * P:(t + 1) * P], fkT[hp, h // 2, 0:w], start=True, stop=False)
                    end(pe.matmul(ps[:, t * P:w], ident, negmask, start=False, stop=True), name)
                if 1 <= k <= 16:
                    h, t = FOX[k - 1]
                    name = ("fT", k - 1)
                    pe.wait_ge(pf_ready, k)
                    ps = begin(name)
                    for j in range(t + 1):
                        m = pe.transpose(ps[:, j * P:(j + 1) * P], Pf[(k - 1) % 2][:, j * P:(j + 1) * P], ident)
                    end(m, name)
                if k >= 2:
                    h, t = FOX[k - 2]
                    name = ("fO", k - 2)
                    wait_read(pe, ("fT", k - 2))
                    ps = begin(name)
                    for j in range(t + 1):
                        m = pe.matmul(ps[:, 0:HD], PT[(k - 2) % 2][:, j, :], fv[:, j, h * HD:(h + 1) * HD],
                                      start=(j == 0), stop=(j == t))
                    end(m, name)
                if k in WS:
                    n = WS[k]
                    wait_read(pe, ("Sp", n - 1))
                    four(("wS", n), lambda h, o: mm(o, kbg[:, n, h, :], St[:, h, :]))
                if k in OO:
                    n = OO[k]
                    name = ("o", n)
                    ps = begin(name)
                    wait_read(pe, ("wS", n) if n else ("u0", 0))
                    wait_read(pe, ("QK", n))
                    for h in range(NH):
                        o = ps[:, h * P:(h + 1) * P]
                        if n:
                            pe.matmul(o, qT[:, h, n * P:(n + 1) * P], St[:, h, :], start=True, stop=False)
                        m = pe.matmul(o, attnT[:, n, h, :], vb[:, n, h, :], start=(n == 0), stop=True)
                    end(m, name)
                    if n < T - 1:
                        four(("Sp", n), lambda h, o: mm(o, ktail[:, n, h, :], vb[:, n, h, :]))
                if k in RS:
                    n = RS[k]
                    hp = slice((n % 2) * HD, (n % 2) * HD + HD)
                    for i in range(4):
                        wait_read(pe, ("rT", i))
                    for j in range(T):
                        name = ("rS", n, j)
                        ps = begin(name)
                        end(mm(ps[:, 0:PW[j]], rkT[hp, n // 2, j * P:(j + 1) * P], rqT[hp, n // 2, j * P:S]), name)
                if k in RO:
                    n = RO[k]
                    name = ("rO", n)
                    ps = begin(name)
                    for j in range(T):
                        wait_read(pe, ("rS", n, j))
                    for t in range(T):
                        for j in range(t + 1):
                            c0 = POFF[j] + (t - j) * P
                            m = pe.matmul(ps[:, t * HD:(t + 1) * HD], retP[:, c0:c0 + P],
                                          rv[:, j, n * HD:(n + 1) * HD], start=(j == 0), stop=(j == t))
                    end(m, name)
            for c in MT:
                if c == 2:
                    pe.wait_ge(mixr_done, 1)
                elif c == 0:
                    for u in range(12, 16):
                        wait_read(pe, ("fO", u))
                elif c >= 4:
                    pe.wait_ge(mixg_done, c - 3)
                four(("mT", c), lambda t, o: pe.transpose(o, mix[:, t, c * P:(c + 1) * P], ident))
            for c in MT[-4:]:
                wait_read(pe, ("mT", c))
            def turn_x2(n):
                for c in (2 * n, 2 * n + 1):
                    for t in range(T):
                        wait_read(pe, ("y", NIN + n, t))
                    four(("hT", c), lambda t, o: pe.transpose(o, x2[:, t, c * P:(c + 1) * P], ident))

            def logits(n):
                ps = begin(("lgT",)) if n == 0 else psum(("lgT",))
                if n == 0:
                    pe.wait_ge(rw_ready, 1)
                for c in (2 * n, 2 * n + 1):
                    b, used = BANK[("hT", c)]
                    pe.wait_ge(free[b], used + 1)
                    m = pe.matmul(ps[0:NG + NE, :], rw[:, c, :], x2T[:, c, :], start=(c == 0), stop=(c == KC - 1),
                                  skip_group_check=True)
                if n < NOUT - 1:
                    m.then_inc(lg_used, 1)
                else:
                    end(m, ("lgT",))

            for n in range(NOUT):
                granule(GR_IN + 2 * n)
                if n:
                    turn_x2(n - 1)
                granule(GR_IN + 2 * n + 1)
                if n:
                    logits(n - 1)
            turn_x2(NOUT - 1)
            logits(NOUT - 1)
            b, used = BANK[("lgT",)]
            pe.wait_ge(free[b], used + 1)
            ps = begin(("lg",))
            for t in range(T):
                m = pe.transpose(ps[:, t * (NG + NE):(t + 1) * (NG + NE)], lgs[0:NG + NE, t * P:(t + 1) * P],
                                 ident[0:NG + NE, 0:NG + NE])
            end(m, ("lg",))
            pe.wait_ge(m_done, 1)
            name = ("rank",)
            ps = begin(name)
            pe.matmul(ps[:, 0:T * NE], const("rankm"), rtB[:, 256:256 + T * NE], start=True, stop=False)
            pe.wait_ge(m_done, 2)
            pe.matmul(ps[:, 0:T * NE], ones, Mc[:, 0:T * NE], start=False, stop=True)
            end(mm(ps[:, T * NE:(T + 1) * NE], ones, Mc[:, T * NE:(T + 1) * NE]), name)

            def indices(U):
                pe.wait_ge(sel_ready, U + 1)
                pe.wait_ge(idx_ready, U + 1)
                for t in range(T):
                    m = pe.matmul(pb[0][:, 0:1], selw[:, t, :, :], ones[:, 0:1], start=(t == 0), stop=(t == T - 1))
                m.then_inc(idx_full, 1)

            def turn(U, s, use):
                pe.wait_ge(gathered[s], use * 16 + 16)
                pe.wait_ge(xt_ready, U + 1)
                for c in range(KC):
                    m = pe.transpose(pb[1 + c // 4][:, (c % 4) * P:(c % 4 + 1) * P], xg[s][:, c * P:(c + 1) * P], ident)
                m.then_inc(xt_full, 1)

            def start(p):
                indices(p * PAIRS)
                indices(p * PAIRS + 1)
                turn(p * PAIRS, 0, p * 6)
                indices(p * PAIRS + 2)

            def unit(U, q, s, use, nuse, ahead, more):
                pe.wait_ge(xt_ready, U + 2)
                for half, (weights_in, bank, bank_read) in enumerate(((w1_full, 3, sa_ready), (w3_full, 7, hid_ready))):
                    pe.wait_ge(weights_in[s], use * 16 + 16)
                    pe.wait_ge(bank_read, U + 1)
                    if half and ahead:
                        indices(U + 3)
                    for c in range(KC):
                        for e in range(2):
                            r = slice(e * CAP, (e + 1) * CAP)
                            m = pe.matmul(pb[bank][r, 0:FF], xT[:, c, r], w13[s][:, e, half, c * FF:(c + 1) * FF],
                                          start=(c == 0), stop=(c == KC - 1), skip_group_check=True)
                    if half == 0:
                        m.then_inc(gate_full, 1)
                m.then_inc(up_full, 1)
                pe.wait_ge(hid_ready, U + 2)
                pe.wait_ge(ht_ready, U + 1)
                for c in range(2):
                    m = pe.transpose(pb[4][:, c * P:(c + 1) * P], hid[:, c, :], ident)
                m.then_inc(ht_full, 1)
                pe.wait_ge(ht_ready, U + 2)
                pe.wait_ge(w2_full[s], use * 16 + 16)
                pe.wait_ge(oyA, U + 1)
                pe.wait_ge(oyB, U + 1)
                for n in range(2):
                    for c in range(2):
                        for e in range(2):
                            r = slice(e * CAP, (e + 1) * CAP)
                            m = pe.matmul(pb[5 + n][r, :], hidT[:, c, r],
                                          w2[s][:, e, c * D + n * 512:c * D + (n + 1) * 512],
                                          start=(c == 0), stop=(c == 1), skip_group_check=True)
                m.then_inc(slots_freed, 1)
                if more:
                    turn(U + 1, (s + 1) % 3, nuse)

            passes(pe, unit, start)

        def weight_high(e, g):
            w = 256 if g >= GR_IN else GROUPS[g // 2][3]
            e.wait_ge(raw_full[g % 3], 16 * (g // 3 + 1))
            if g >= 2:
                n = (g - 2) // 2
                if g % 2 == 0:
                    e.wait_ge(half_used, n + 1)
                else:
                    wait_full(e, ("y", n, (T if n >= NIN or GROUPS[n][0] == "n" else 2) - 1))
            e.activation(whi[g % 2][:, :, 0:w], raw[g % 3][:, :, 0:w], ACT.Copy).then_inc(whi_done, 1)

        @block.scalar
        def _(act):
            cnt = [0]

            def link(ins):
                cnt[0] += 1
                ins.then_inc(act_self, 1)
                act.wait_ge(act_self, cnt[0])

            act.dma_start(PW48[:, :], convw[0].rearrange("k (b p) -> (k b) p", p=P)).then_inc(s_cw, 16)
            act.wait_ge(one_set, 1)
            act.activation(rs[0:1, 0:1], rs[0:1, 0:1], ACT.Sqrt)
            for t in range(T):
                act.wait_ge(s_x[t], 16)
                link(act.activation(junk[:, :], X0[:, t, :], ACT.Square, accum_out=ssx[:, t:t + 1]))
                if t == 0:
                    act.wait_ge(s_const, 16)
                act.activation(ssx[:, t:t + 1], ssx[:, t:t + 1], ACT.Sqrt, scale=1.0 / D, bias=eps).then_inc(ssx_done, 1)
            weight_high(act, 0)
            weight_high(act, 1)
            wait_full(act, ("par",))
            release(act.activation(PCW[:, :, :].rearrange("p k b -> p (k b)"), pb[BANK[("par",)][0]][:, 0:48], ACT.Copy), ("par",))
            for t in range(T):
                for i in range(2):
                    name = ("xT", t, i)
                    wait_full(act, name)
                    act.activation(hHi[:, 4 * i:4 * i + 4, t * P:(t + 1) * P],
                                   psum(name)[:, :].rearrange("p (c n) -> p c n", n=P), ACT.Copy).then_inc(hhi_done, 1)

            def evac(n):
                kind, what, _, w = GROUPS[n]
                if kind == "n":
                    for t in range(T):
                        name = ("y", n, t)
                        wait_full(act, name)
                        ps = psum(name)
                        cp = lambda dst, src: act.activation(dst, src, ACT.Copy)
                        if what == "fv":
                            cp(fv[:, t, :], ps[:, 0:256])
                            i = cp(FFT[:, t, :], ps[:, 256:260])
                        elif what == "zb":
                            cp(mix[:, t, GW + 260:D], ps[:, 0:252])
                            i = cp(GAB[:, t, :], ps[:, 252:260])
                        elif what == "za":
                            i = cp(mix[:, t, GW:GW + 260], ps[:, 0:260])
                        elif what == "rg":
                            i = cp(mix[:, t, 256:GW], ps[:, 0:256])
                        else:
                            i = cp({"rq": rq, "rk": rk, "rv": rv}[what][:, t, :], ps[:, 0:256])
                        release(i, name)
                    act.wait_ge(free[BANK[name][0]], BANK[name][1] + 1)
                    act.sem_inc(y_copied, 1) if what not in ("zb", "za", "rg") else act.sem_inc(z_in, 1)
                elif what in ("fq", "fk"):
                    for b in range(2):
                        name = ("y", n, b)
                        wait_full(act, name)
                        release(act.activation((fqT if what == "fq" else fkT)[:, b, :], psum(name)[:, :], ACT.Copy), name)
                    act.wait_ge(free[BANK[name][0]], BANK[name][1] + 1)
                    act.sem_inc(y_copied, 1)
                else:
                    for b in range(2):
                        name = ("y", n, b)
                        blk = tcol[what] + b
                        i = CONVN[what] + b
                        wait_full(act, name)
                        if i >= 2:
                            act.wait_ge(silu_done, i - 1)
                        act.activation(cacc[i % 2][:, :], psum(name)[:, :], ACT.Copy,
                                       scale=PCW[:, 3, blk:blk + 1]).then_inc(tap0_done, 1)
                    for b in range(2):
                        i = CONVN[what] + b
                        wait_read(act, ("y", n, b))
                        h = i % 4
                        if what[0] == "v":
                            dst = vS[h % 2][:, :]
                            if h >= 2:
                                act.wait_ge(vb_done, h - 1)
                        else:
                            dst = (kT if what[0] == "k" else qT)[:, h, :]
                        act.activation(dst, cacc[i % 2][:, :], ACT.Silu).then_inc(silu_done, 1)
                        if b == 0:
                            weight_high(act, 2 * n + 4)

            def task(k):
                if k[0] == "evac":
                    evac(k[1])
                elif k[0] == "gates":
                    act.wait_ge(gexp_in, 1)
                    act.activation(e8, az, ACT.Exp, scale=-1.0)
                    act.activation(eb.rearrange("p (t n) -> p t n", t=T), GAB[:, :, 4:8], ACT.Exp, scale=-1.0)
                    act.activation(ea, PAL[:, :], ACT.Exp).then_inc(gexp_done, 1)
                elif k[0] == "gcum":
                    act.wait_ge(cum_done, 3)
                    act.activation(egc, cum[:, 0:16], ACT.Exp)
                    act.activation(egl, cum[:, 16:32], ACT.Exp)
                    act.activation(etl, tl, ACT.Exp).then_inc(cexp_done, 1)
                elif k[0] == "cB":
                    for h in range(NH):
                        name = ("cB", h)
                        wait_full(act, name)
                        release(act.activation(cB8[:, h, :], psum(name)[:, :], ACT.Copy), name)
                    act.wait_ge(free[BANK[name][0]], BANK[name][1] + 1)
                    act.sem_inc(cB_done, 1)
                elif k[0] == "ss" and k[1] == 1:
                    act.wait_ge(ss_read, 2)
                    act.activation(rks, ssk, ACT.Sqrt, bias=eps)
                    act.activation(rqs[:, :], ssq, ACT.Sqrt, scale=float(P), bias=const("eps128")).then_inc(root_done, 1)
                elif k[0] == "prep":
                    t = k[1]
                    i = t % 2
                    act.wait_ge(d_raw, t + 1)
                    name = ("gcB", t)
                    if t >= 2:
                        wait_read(act, ("Up", t - 2, LEVELS - 1))
                    j = act.activation(Xm[i][:, :, :], psum(name)[:, :].rearrange("p (h n) -> p h n", h=NH), ACT.Exp)
                    release(j, name)
                    act.activation(Dm[i][:, :, :], Dm[i][:, :, :], ACT.Exp).then_inc(d_exp, 1)
                elif k[0] == "xt":
                    for t in (2 * k[1], 2 * k[1] + 1):
                        name = ("XT", t)
                        wait_full(act, name)
                        j = act.activation(Xm[t % 2][:, :, :], psum(name)[:, :].rearrange("p (h n) -> p h n", h=NH), ACT.Copy)
                        release(j, name)
                elif k[0] == "silu":
                    act.wait_ge(z_in, 3)
                    act.activation(mix[:, :, 256:D], mix[:, :, 256:D], ACT.Silu).then_inc(silu2_done, 1)
                    act.activation(PDT[0:1, 0:1], eps[0:1, :], ACT.Exp)
                elif k[0] == "lv" and k[2]:
                    for i in range(2):
                        name = ("UT", 2 * k[1] + i, k[2])
                        wait_full(act, name)
                        release(act.activation(Um[i][:, :, :], psum(name)[:, :].rearrange("p (h n) -> p h n", h=NH), ACT.Copy), name)
                elif k[0] == "fin":
                    for t in (2 * k[1], 2 * k[1] + 1):
                        for name, dst, sc in ((("wT", t), kbg, -1.0), (("u0", t), vb, 1.0)):
                            wait_full(act, name)
                            j = act.activation(dst[:, t, :, :], psum(name)[:, :].rearrange("p (h n) -> p h n", h=NH),
                                               ACT.Copy, scale=sc)
                            release(j, name)

            for g in range(GR_IN):
                if g % 2 or g < 2 or GROUPS[g // 2 - 1][1] not in CONVN:
                    weight_high(act, g + 2)
                for k in AFTER[g]:
                    task(k)
            for i in range(4):
                name = ("rT", i)
                wait_full(act, name)
                release(act.activation((rqT if i < 2 else rkT)[:, i % 2, :], psum(name)[:, :], ACT.Copy), name)
            for k in range(KSTEPS):
                if k < 16:
                    h, t = FOX[k]
                    w = (t + 1) * P
                    act.wait_ge(sx_ready, k + 1)
                    if k >= 2:
                        wait_full(act, ("fT", k - 2))
                    act.activation(Pf[k % 2][:, 0:w], Sx[k % 2][:, 0:w], ACT.Exp, scale=HD ** -0.5,
                                   bias=nmx[:, k:k + 1], accum_out=rs[:, k:k + 1]).then_inc(pf_ready, 1)
                if 1 <= k <= 16:
                    h, t = FOX[k - 1]
                    name = ("fT", k - 1)
                    wait_full(act, name)
                    if k >= 3:
                        wait_full(act, ("fO", k - 3))
                    j = act.activation(PT[(k - 1) % 2][:, 0:t + 1, :],
                                       psum(name)[:, 0:(t + 1) * P].rearrange("p (j n) -> p j n", n=P), ACT.Copy)
                    release(j, name)
                if k in OO:
                    n = OO[k]
                    name = ("o", n)
                    wait_full(act, name)
                    j = act.activation(kbg[:, n, :, :], psum(name)[:, :].rearrange("p (h n) -> p h n", h=NH), ACT.Copy)
                    release(j, name)
                if k in RO:
                    n = RO[k]
                    name = ("rO", n)
                    wait_full(act, name)
                    j = act.activation(oret[:, :, n * HD:(n + 1) * HD],
                                       psum(name)[:, 0:T * HD].rearrange("p (t n) -> p t n", t=T), ACT.Copy)
                    release(j, name)
                if k == 16:
                    act.wait_ge(ssr_done, 2)
                    act.activation(ssx4, ssx4, ACT.Sqrt, scale=1.0 / HD, bias=eps).then_inc(rtr_done, 1)
                    act.activation(ssn, ssn, ACT.Sqrt, scale=1.0 / P, bias=eps).then_inc(rtr_done, 1)
            for c in MT:
                name = ("mT", c)
                wait_full(act, name)
                act.activation(hHi[:, c, :], psum(name)[:, :], ACT.Copy).then_inc(hhi_done, 1)

            def squares_and_columns(n):
                for t in range(T):
                    wait_read(act, ("y", NIN + n, t))
                    link(act.activation(sqj[:, :], x2[:, t, n * 256:(n + 1) * 256], ACT.Square,
                                        accum_out=ssp[:, 4 * t + n:4 * t + n + 1]))
                if n == NOUT - 1:
                    act.sem_inc(ssp_done, 1)
                for c in (2 * n, 2 * n + 1):
                    name = ("hT", c)
                    wait_full(act, name)
                    release(act.activation(x2T[:, c, :], psum(name)[:, :], ACT.Copy), name)

            for j in range(2 * NOUT):
                if j + 2 < 2 * NOUT:
                    weight_high(act, GR_IN + j + 2)
                if j and j % 2 == 0:
                    squares_and_columns(j // 2 - 1)
            squares_and_columns(NOUT - 1)
            act.wait_ge(ssp_sum, 1)
            act.activation(ss2, ss2, ACT.Sqrt, scale=1.0 / D, bias=eps).then_inc(ss2_done, 1)
            name = ("lgT",)
            wait_full(act, name)
            release(act.activation(lgs[0:NG + NE, :], psum(name)[0:NG + NE, :], ACT.Copy), name)
            act.wait_ge(r2_done, 1)
            for t in range(T // 2, T):
                act.activation(turned_view(h2[:, t, :]), plain_view(x2[:, t, :]), ACT.Copy,
                               scale=r2[:, t:t + 1]).then_inc(h2s_done, 1)
            act.wait_ge(rexp_in, 1)
            act.activation(gd, gd, ACT.Exp).then_inc(rexp_done, 1)
            act.wait_ge(rexp_in, 2)
            act.activation(e2, mm1, ACT.Exp).then_inc(rexp_done, 1)
            act.activation(PDT[0:1, 0:1], eps[0:1, :], ACT.Silu)

            def turned(U):
                act.wait_ge(xt_full, U + 2)
                act.wait_ge(up_full, U + 1)
                act.activation(xT[:, 0:4, :], pb[1][:, :].rearrange("p (c n) -> p c n", n=P), ACT.Copy)
                act.activation(xT[:, 4:8, :], pb[2][:, :].rearrange("p (c n) -> p c n", n=P), ACT.Copy).then_inc(xt_ready, 1)

            def unit(U, q, s, use, nuse, ahead, more):
                act.wait_ge(gate_full, U + 2)
                act.activation(sa[:, :], pb[3][:, 0:FF], ACT.Silu).then_inc(sa_ready, 1)
                act.wait_ge(ht_full, U + 2)
                act.activation(hidT[:, :, :], pb[4][:, 0:2 * P].rearrange("p (c n) -> p c n", n=P), ACT.Copy).then_inc(ht_ready, 1)
                act.wait_ge(slots_freed, U + 4)
                act.wait_ge(scattered[s], use * 16 + 16)
                act.activation(oy[s][:, 512:D], pb[6][:, :], ACT.Copy).then_inc(oyB, 1)
                if more:
                    turned(U + 1)

            passes(act, unit, lambda p: turned(p * PAIRS))
            act.activation(PDT[0:1, 0:1], eps[0:1, :], ACT.Sqrt)
            for t in range(T):
                act.wait_ge(acc_done, t + 1)
                act.activation(jk[:, :], yt[t][:, 0, :], ACT.Square, accum_out=ssf[:, t:t + 1]).then_inc(ssf_done, 1)
                act.wait_ge(ssf_done, 2 * t + 1)
                act.activation(ssf[:, t:t + 1], ssf[:, t:t + 1], ACT.Sqrt, scale=1.0 / D, bias=eps).then_inc(ssf_done, 1)
                if t < T - 1:
                    act.wait_ge(rf_done, t + 1)
                    act.activation(x2[:, t, :], yt[t][:, 0, :], ACT.Copy, scale=rf[:, t:t + 1]).then_inc(fins_done, 1)

        @block.gpsimd
        def _(pool):
            cnt = [0]

            def link(ins):
                cnt[0] += 1
                ins.then_inc(pool_self, 1)
                pool.wait_ge(pool_self, cnt[0])

            def weight_low(g):
                w = 256 if g >= GR_IN else GROUPS[g // 2][3]
                pool.wait_ge(whi_done, g + 1)
                pool.tensor_tensor(wlo[g % 2][:, :, 0:w], raw[g % 3][:, :, 0:w], whi[g % 2][:, :, 0:w].bitcast(F32),
                                   ALU.subtract).then_inc(wlo_done, 1)

            def bc(m):
                return m.unsqueeze(1).broadcast_to([P, NH, P])

            weight_low(0)
            weight_low(1)

            def task(k):
                if k[0] == "prep":
                    t = k[1]
                    i = t % 2
                    tk = slice(t * P, (t + 1) * P)
                    pool.wait_ge(d_exp, t + 1)
                    pool.tensor_tensor(Ym[i][:, :, :], Dm[i][:, :, :], bc(strict), ALU.mult).then_inc(ds_ready, 1)
                    pool.tensor_tensor(Dm[i][:, :, :], Dm[i][:, :, :], bc(tri), ALU.mult).then_inc(di_ready, 1)
                    wait_full(pool, ("QK", t))
                    pool.tensor_tensor(qT[:, :, tk], qT[:, :, tk], Xm[i][:, :, :], ALU.mult).then_inc(qg_ready, 1)
                    wait_read(pool, ("bB", t))
                    link(pool.tensor_tensor(Ym[i][:, :, :], Nm[i][:, :, :], bc(const("nM1")), ALU.mult))
                    pool.tensor_tensor(Um[i][:, :, :], Ym[i][:, :, :], bc(ident), ALU.add).then_inc(uinit, 1)
                elif k == ("evac", GIDX["rv"]):
                    rotary(rq, 1)
                elif k == ("evac", GIDX["za"]):
                    rotary(rk, 2)

            def rotary(r, n):
                pool.wait_ge(y_copied, n + 1)
                v = r[:, :, :].rearrange("p t (h s n) -> p t h s n", h=NH, s=2)
                t1, t2 = v[:, :, :, 0, :], v[:, :, :, 1, :]
                co = cosT.unsqueeze(2).broadcast_to([P, T, NH, 32])
                si = sinT.unsqueeze(2).broadcast_to([P, T, NH, 32])
                if n == 2:
                    pool.wait_ge(rot_done, 1)
                pool.tensor_tensor(rtmp[0][:, :, :, :], t1, co, ALU.mult)
                pool.tensor_tensor(rtmp[1][:, :, :, :], t2, si, ALU.mult)
                pool.tensor_tensor(rtmp[2][:, :, :, :], t1, si, ALU.mult)
                link(pool.tensor_tensor(rtmp[3][:, :, :, :], t2, co, ALU.mult))
                pool.tensor_tensor(t1, rtmp[0][:, :, :, :], rtmp[1][:, :, :, :], ALU.subtract)
                pool.tensor_tensor(t2, rtmp[2][:, :, :, :], rtmp[3][:, :, :, :], ALU.add).then_inc(rot_done, 1)

            for g in range(GR_IN):
                weight_low(g + 2)
                for k in AFTER[g]:
                    task(k)
            pool.wait_ge(silu2_done, 1)
            for t in range(T):
                m4 = mix[:, t, GW:D].rearrange("p (h n) -> p h n", h=NH)
                j = pool.tensor_tensor(m4, m4, bc(PGN[:, :]), ALU.mult)
            j.then_inc(zg_done, 1)
            for t in range(T):
                wait_read(pool, ("o", t))
                pool.tensor_tensor(gsq[t][:, :, :], kbg[:, t, :, :], kbg[:, t, :, :], ALU.mult).then_inc(sqr_done, 1)
            for n in range(NH):
                wait_read(pool, ("rO", n))
            pool.tensor_tensor(osq[:, :, :], oret[:, :, :], oret[:, :, :], ALU.mult).then_inc(sqr_done, 1)
            pool.wait_ge(rx4_done, 1)
            o4 = oret[:, :, :].rearrange("p t (h n) -> p (t h) n", h=NH)
            link(pool.tensor_tensor(o4, o4, ssx4.unsqueeze(2).broadcast_to([P, 16, HD]), ALU.mult))
            pool.tensor_tensor(mix[:, :, 256:GW], oret[:, :, :], mix[:, :, 256:GW], ALU.mult).then_inc(mixr_done, 1)
            for g in range(GR_IN, GR - 2):
                weight_low(g + 2)
                if g == GR_IN + 2:
                    pool.wait_ge(s_rw, 48)
                    pool.tensor_tensor(rw[:, :, :], rw[:, :, :], n2p[:, :].unsqueeze(2).broadcast_to([P, KC, NG + NE]),
                                       ALU.mult).then_inc(rw_ready, 1)
            for k in range(3):
                pool.dma_start(oy[k][:, 0:KC], fnw.rearrange("(p c) -> p c", c=KC)).then_inc(scattered[k], 16)
            pool.wait_ge(s_n2, 16)
            for t in range(T // 2, T):
                pool.wait_ge(h2s_done, t - T // 2 + 1)
                pool.tensor_tensor(turned_view(h2[:, t, :]), turned_view(h2[:, t, :]), plain_view(n2b[:, :]),
                                   ALU.mult).then_inc(h2p_done, 1)

            pool.wait_ge(s_h2d, 16 * T)

            def gather(U, s, turned):
                pool.wait_ge(idx_ready, U + 2)
                pool.wait_ge(xt_full, turned + 1)
                pool.sem_inc(pool_step, 1)
                pool.indirect_dma_start(xg[s][:, :], None, h2d.ap()[:, :],
                                        bass.IndirectOffsetOnAxis(ap=tok_i[s][:, 0:1].bitcast(U32), axis=0),
                                        bounds_check=S - 1, oob_is_err=False).then_inc(gathered[s], 16)

            def unit(U, q, s, use, nuse, ahead, more):
                if ahead:
                    gather(U + 3, s, U + 1)
                pool.wait_ge(oyA, U + 2)
                pool.wait_ge(oyB, U + 2)
                pool.sem_inc(pool_step, 1)
                pool.indirect_dma_start(yd.ap()[:, :],
                                        bass.IndirectOffsetOnAxis(ap=dst_i[s][:, 0:1].bitcast(U32), axis=0),
                                        oy[s][:, :], None, bounds_check=2 * S - 1, oob_is_err=False).then_inc(scattered[s], 16)


            def start(p):
                for k in range(3):
                    gather(p * PAIRS + k, k, p * PAIRS)

            passes(pool, unit, start)
            pool.wait_ge(s_fn, 16)
            for t in range(T - 1):
                pool.wait_ge(fins_done, t + 1)
                pool.tensor_tensor(x2[:, t, :], x2[:, t, :], fnb[:, :], ALU.mult).then_inc(finp_done, 1)

        @block.vector
        def _(dve):
            cnt = [0]

            def link(ins):
                cnt[0] += 1
                ins.then_inc(dve_self, 1)
                dve.wait_ge(dve_self, cnt[0])

            def v4(name):
                return psum(name)[:, :].rearrange("p (h n) -> p h n", h=NH)

            dve.memset(rs[0:1, 0:1], 1.0).then_inc(one_set, 1)
            dve.wait_ge(s_n1, 16)
            for t in range(T):
                dve.wait_ge(ssx_done, t + 1)
                link(dve.reciprocal(rx[:, t:t + 1], ssx[:, t:t + 1]))
                dve.scalar_tensor_tensor(out=X0[:, t, :], in0=X0[:, t, :], scalar=rx[:, t:t + 1], in1=n1b[:, :],
                                         op0=ALU.mult, op1=ALU.mult).then_inc(xn_done, 1)
            for t in range(T):
                for i in range(2):
                    name = ("xT", t, i)
                    dve.wait_ge(hhi_done, 2 * t + i + 1)
                    tk = slice(t * P, (t + 1) * P)
                    cs = slice(4 * i, 4 * i + 4)
                    j = dve.tensor_tensor(hLo[:, cs, tk], psum(name)[:, :].rearrange("p (c n) -> p c n", n=P),
                                          hHi[:, cs, tk].bitcast(F32), ALU.subtract)
                    release(j, name)

            def evac(n):
                kind, what, _, _ = GROUPS[n]
                if what not in CONVN:
                    return
                for b in range(2):
                    name = ("y", n, b)
                    i = CONVN[what] + b
                    blk = tcol[what] + b
                    dve.wait_ge(tap0_done, i + 1)
                    a = cacc[i % 2]
                    for s in (1, 2, 3):
                        j = dve.scalar_tensor_tensor(out=a[:, s:S], in0=psum(name)[:, 0:S - s],
                                                     scalar=PCW[:, 3 - s, blk:blk + 1], in1=a[:, s:S],
                                                     op0=ALU.mult, op1=ALU.add)
                        if s < 3:
                            link(j)
                    release(j, name)

            def gates():
                dve.wait_ge(y_copied, 1)
                dve.wait_ge(z_in, 1)
                dve.wait_ge(s_par, 16 * 6)
                dtv = PDT[:, :].unsqueeze(1).broadcast_to([P, T, 4])
                fbv = PFB[:, :].unsqueeze(1).broadcast_to([P, T, 4])
                dve.tensor_tensor(z8[:, :, 0:4], GAB[:, :, 0:4], dtv, ALU.add)
                link(dve.tensor_tensor(hv[:, :, 4:8], FFT, fbv, ALU.add))
                link(dve.tensor_scalar(z8[:, :, 4:8], hv[:, :, 4:8], -1.0, None, ALU.mult))
                dve.scalar_tensor_tensor(out=az, in0=z8, scalar=-1.0, in1=z8, op0=ALU.mult, op1=ALU.max).then_inc(gexp_in, 1)
                dve.wait_ge(gexp_done, 1)
                link(dve.tensor_scalar(dd, e8, 2.0, None, ALU.add))
                link(dve.reciprocal(sv, dd))
                link(dve.tensor_tensor(sv, sv, e8, ALU.mult))
                link(dve.tensor_tensor(qv, sv, sv, ALU.mult))
                link(dve.tensor_scalar(hv, qv, 1.0 / 17, None, ALU.mult))
                for c in (15, 13, 11, 9, 7, 5, 3):
                    link(dve.scalar_tensor_tensor(out=hv, in0=hv, scalar=1.0 / c, in1=qv, op0=ALU.add, op1=ALU.mult))
                link(dve.scalar_tensor_tensor(out=hv, in0=hv, scalar=1.0, in1=sv, op0=ALU.add, op1=ALU.mult))
                link(dve.tensor_scalar(sp8, z8, 0.0, None, ALU.max))
                link(dve.scalar_tensor_tensor(out=sp8, in0=hv, scalar=2.0, in1=sp8, op0=ALU.mult, op1=ALU.add))
                link(dve.tensor_scalar(eb, eb, 1.0, None, ALU.add))
                dve.reciprocal(beta, eb)
                t3 = lambda a: a.rearrange("p (t n) -> p t n", t=T)
                link(dve.tensor_tensor(t3(gg), sp8[:, :, 0:4], ea.unsqueeze(1).broadcast_to([P, T, 4]), ALU.mult))
                dve.tensor_scalar(t3(lf), sp8[:, :, 4:8], -1.0, None, ALU.mult)
                link(dve.tensor_scalar(gg, gg, -1.0, None, ALU.mult))
                dve.memset(lfc[:, 0:4], 0.0)
                link(dve.tensor_copy(lfc[:, 4:8], lf[:, 0:4]))
                link(dve.tensor_tensor(lfc[:, 8:12], lfc[:, 4:8], lf[:, 4:8], ALU.add))
                dve.tensor_tensor(lfc[:, 12:16], lfc[:, 8:12], lf[:, 8:12], ALU.add).then_inc(gates_done, 1)

            def task(k):
                if k[0] == "evac":
                    evac(k[1])
                elif k[0] == "sq":
                    for h in (2 * k[2], 2 * k[2] + 1):
                        dve.wait_ge(silu_done, NH * (k[1] + 1) + h + 1)
                        src = (kT if k[1] == 0 else qT)[:, h, :]
                        dve.tensor_tensor(nrm[h][:, :], src, src, ALU.mult).then_inc(sq_done, 1)
                elif k[0] == "gates":
                    gates()
                elif k[0] == "gcum":
                    wait_full(dve, k)
                    dve.tensor_copy(cum, psum(k)[:, 0:48]).then_inc(cum_done, 1)
                    dve.wait_ge(cum_done, 1)
                    dve.tensor_scalar(c8, cum[:, 32:48], -float(HD ** 0.5), None, ALU.mult).then_inc(cum_done, 1)
                    release(dve.tensor_tensor(tl, cum[:, 16:32], cum[:, 0:16], ALU.subtract), k)
                    dve.wait_ge(free[BANK[k][0]], BANK[k][1] + 1)
                    dve.sem_inc(cum_done, 1)
                    dve.wait_ge(cexp_done, 1)
                    link(dve.tensor_tensor(bgc, beta, egc, ALU.mult))
                elif k[0] == "vt":
                    h = k[1]
                    wait_full(dve, k)
                    dve.wait_ge(gates_done, 1)
                    bv = beta.rearrange("p (t n) -> p t n", t=T)[:, :, h:h + 1].broadcast_to([P, T, P])
                    release(dve.tensor_tensor(vb[:, :, h, :], v4(k), bv, ALU.mult), k)
                    dve.wait_ge(free[BANK[k][0]], BANK[k][1] + 1)
                    dve.sem_inc(vb_done, 1)
                elif k[0] == "ss":
                    wait_full(dve, k)
                    release(dve.tensor_copy(ssk if k[1] == 0 else ssq, psum(k)[:, 0:16]), k)
                    dve.wait_ge(free[BANK[k][0]], BANK[k][1] + 1)
                    dve.sem_inc(ss_read, 1)
                    if k[1]:
                        dve.wait_ge(root_done, 1)
                        link(dve.reciprocal(rks, rks))
                        dve.reciprocal(rqs[:, :], rqs[:, :])
                        dve.tensor_tensor(br, beta, rks, ALU.mult)
                        dve.tensor_tensor(bgr, bgc, rks, ALU.mult)
                        link(dve.tensor_tensor(etr, etl, rks, ALU.mult))
                        dve.sem_inc(rk_done, 1)
                elif k[0] == "kt":
                    for h in range(NH):
                        name = ("kt", h)
                        wait_full(dve, name)
                        f = lambda a: a.rearrange("p (t n) -> p t n", t=T)[:, :, h:h + 1].broadcast_to([P, T, P])
                        dve.tensor_tensor(kbg[:, :, h, :], v4(name), f(bgr), ALU.mult)
                        release(dve.tensor_tensor(ktail[:, :, h, :], v4(name), f(etr), ALU.mult), name)
                        dve.wait_ge(free[BANK[name][0]], BANK[name][1] + 1)
                        dve.sem_inc(kt_done, 1)
                elif k[0] == "prep":
                    t = k[1]
                    i = t % 2
                    name = ("gcB", t)
                    wait_full(dve, name)
                    for h in range(NH):
                        j = dve.tensor_scalar(Dm[i][:, h, :], psum(name)[:, h * P:(h + 1) * P],
                                              cum[:, 4 * t + h:4 * t + h + 1], 0.0, ALU.subtract, ALU.min)
                    j.then_inc(d_raw, 1)
                    dve.wait_ge(ds_ready, t + 1)
                    wait_full(dve, ("KK", t))
                    for h in range(NH):
                        j = dve.scalar_tensor_tensor(out=Nm[i][:, h, :], in0=psum(("KK", t))[:, h * P:(h + 1) * P],
                                                     scalar=rks[:, 4 * t + h:4 * t + h + 1], in1=Ym[i][:, h, :],
                                                     op0=ALU.mult, op1=ALU.mult)
                    release(j, ("KK", t))
                    b, n = BANK[("KK", t)]
                    dve.wait_ge(free[b], n + 1)
                    wait_full(dve, ("bB", t))
                    release(dve.tensor_tensor(Nm[i][:, :, :], Nm[i][:, :, :], v4(("bB", t)), ALU.mult), ("bB", t))
                    dve.wait_ge(di_ready, t + 1)
                    wait_full(dve, ("QK", t))
                    for h in range(NH):
                        j = dve.scalar_tensor_tensor(out=attnT[:, t, h, :], in0=psum(("QK", t))[:, h * P:(h + 1) * P],
                                                     scalar=rks[:, 4 * t + h:4 * t + h + 1], in1=Dm[i][:, h, :],
                                                     op0=ALU.mult, op1=ALU.mult)
                    release(j, ("QK", t))
                elif k[0] == "lv":
                    _, pr, lv = k
                    mask = nM[:, lv, :].unsqueeze(1).broadcast_to([P, NH, P])

                    def update(name, dst, in1, op):
                        wait_full(dve, name)
                        release(dve.tensor_tensor(dst, v4(name), in1, op), name)

                    for i in range(2):
                        update(("Y", 2 * pr + i, lv), Ym[i][:, :, :], mask, ALU.mult)
                    for i in range(2):
                        if lv < LEVELS - 1:
                            update(("Xp", 2 * pr + i, lv), Xm[i][:, :, :], Xm[i][:, :, :], ALU.add)
                        else:
                            update(("Up", 2 * pr + i, lv), Um[i][:, :, :], Um[i][:, :, :], ALU.add)

            for g in range(GR_IN):
                for k in AFTER[g]:
                    task(k)
            for k in range(KSTEPS):
                if k < 16:
                    h, t = FOX[k]
                    w = (t + 1) * P
                    name = ("fS", k)
                    wait_full(dve, name)
                    if k == 0:
                        dve.wait_ge(cB_done, 1)
                        dve.wait_ge(rot_done, 2)
                    if k >= 2:
                        dve.wait_ge(pf_ready, k - 1)
                    j = dve.tensor_tensor_reduce(out=Sx[k % 2][:, 0:w], in0=psum(name)[:, 0:w], in1=cB8[:, h, 0:w],
                                                 scale=1.0, scalar=-3.0e38, op0=ALU.add, op1=ALU.max,
                                                 accum_out=mx[:, k:k + 1])
                    release(j, name)
                    dve.wait_ge(free[BANK[name][0]], BANK[name][1] + 1)
                    dve.tensor_scalar(nmx[:, k:k + 1], mx[:, k:k + 1], -float(HD ** -0.5), None, ALU.mult).then_inc(sx_ready, 1)
                if k in WS:
                    n = WS[k]
                    name = ("wS", n)
                    wait_full(dve, name)
                    wait_read(dve, ("u0", n))
                    release(dve.tensor_tensor(vb[:, n, :, :], v4(name), vb[:, n, :, :], ALU.add), name)
                if k in OO and OO[k] < T - 1:
                    n = OO[k]
                    name = ("Sp", n)
                    wait_full(dve, name)
                    if n == 0:
                        j = dve.tensor_copy(St[:, :, :], v4(name))
                    else:
                        for h in range(NH):
                            j = dve.scalar_tensor_tensor(out=St[:, h, :], in0=St[:, h, :],
                                                         scalar=egl[:, 4 * n + h:4 * n + h + 1],
                                                         in1=psum(name)[:, h * P:(h + 1) * P],
                                                         op0=ALU.mult, op1=ALU.add)
                    release(j, name)
                if k in RS:
                    n = RS[k]
                    for jj in range(T):
                        name = ("rS", n, jj)
                        wait_full(dve, name)
                        if n and jj == 0:
                            wait_full(dve, ("rO", n - 1))
                        release(dve.tensor_tensor(retP[:, POFF[jj]:POFF[jj] + PW[jj]], psum(name)[:, 0:PW[jj]],
                                                  dm[:, n, 0:PW[jj]], ALU.mult), name)
                if k in (3, 6, 9, 12):
                    t = k // 3 - 1
                    dve.wait_ge(sqr_done, t + 1)
                    dve.tensor_reduce(ssn[:, 4 * t:4 * t + 4], gsq[t][:, :, :], AX_X, ALU.add)
                if k == 14:
                    dve.wait_ge(sqr_done, T + 1)
                    link(dve.tensor_reduce(ssx4.rearrange("p (t h) -> p t h", t=T),
                                           osq[:, :, :].rearrange("p t (h n) -> p t h n", h=NH), AX_X, ALU.add))
                    link(dve.tensor_tensor(rn, rqs[:, :], rqs[:, :], ALU.mult))
                    dve.tensor_tensor(ssn, ssn, rn, ALU.mult).then_inc(ssr_done, 2)
                if k >= 2:
                    u = k - 2
                    h, t = FOX[u]
                    name = ("fO", u)
                    wait_full(dve, name)
                    link(dve.reciprocal(ri[:, u:u + 1], rs[:, u:u + 1]))
                    j = dve.tensor_scalar(mix[:, t, h * HD:(h + 1) * HD], psum(name)[:, 0:HD], ri[:, u:u + 1], None, ALU.mult)
                    release(j, name)
            dve.wait_ge(rtr_done, 2)
            dve.reciprocal(ssx4, ssx4).then_inc(rx4_done, 1)
            link(dve.reciprocal(rn, ssn))
            link(dve.tensor_tensor(rn, rn, rqs[:, :], ALU.mult))
            dve.wait_ge(zg_done, 1)
            for h in range(NH):
                for t in range(T):
                    m = mix[:, t, GW + h * P:GW + (h + 1) * P]
                    j = dve.scalar_tensor_tensor(out=m, in0=kbg[:, t, h, :], scalar=rn[:, 4 * t + h:4 * t + h + 1],
                                                 in1=m, op0=ALU.mult, op1=ALU.mult)
                j.then_inc(mixg_done, 1)
            dve.wait_ge(mixg_done, NH)
            dve.sem_inc(slots_freed, 1)
            for ci, c in enumerate(MT):
                name = ("mT", c)
                dve.wait_ge(hhi_done, 2 * T + ci + 1)
                j = dve.tensor_tensor(hLo[:, c, :], psum(name)[:, :], hHi[:, c, :].bitcast(F32), ALU.subtract)
                release(j, name)
            dve.wait_ge(s_x2, 16 * T)
            for n in range(NOUT):
                for t in range(T):
                    name = ("y", NIN + n, t)
                    wait_full(dve, name)
                    xs = x2[:, t, n * 256:(n + 1) * 256]
                    release(dve.tensor_tensor(xs, psum(name)[:, 0:256], xs, ALU.add), name)

            wait_read(dve, ("y", NIN + NOUT - 1, T - 1))
            dve.sem_inc(slots_freed, 2)
            dve.wait_ge(ssp_done, 1)
            dve.tensor_reduce(ss2, ssp.rearrange("p (t n) -> p t n", t=T), AX_X, ALU.add).then_inc(ssp_sum, 1)
            dve.wait_ge(ss2_done, 1)
            dve.reciprocal(r2, ss2).then_inc(r2_done, 1)
            dve.wait_ge(r2_done, 1)
            dve.wait_ge(s_n2, 16)
            dve.wait_ge(lg_used, T // 2)
            for t in range(T // 2):
                dve.scalar_tensor_tensor(out=turned_view(h2[:, t, :]), in0=plain_view(x2[:, t, :]), scalar=r2[:, t:t + 1],
                                         in1=plain_view(n2b[:, :]), op0=ALU.mult, op1=ALU.mult).then_inc(h2_done, 1)
            name = ("lg",)
            wait_full(dve, name)
            for t in range(T):
                j = dve.scalar_tensor_tensor(out=LG[:, t, :], in0=psum(name)[:, t * (NG + NE):(t + 1) * (NG + NE)],
                                             scalar=r2[:, t:t + 1], in1=PRB[:, :], op0=ALU.mult, op1=ALU.add)
            link(j)

            def top(src, desc, mx_, one, scratch, n):
                b = lambda a: a.unsqueeze(2).broadcast_to([P, T, n])
                link(dve.tensor_reduce(mx_, src, AX_X, ALU.max))
                link(dve.tensor_tensor(scratch, src, b(mx_), ALU.is_equal))
                link(dve.tensor_tensor(scratch, scratch, desc.unsqueeze(1).broadcast_to([P, T, n]), ALU.mult))
                link(dve.tensor_reduce(gmx, scratch, AX_X, ALU.max))
                link(dve.tensor_tensor(one, scratch, b(gmx), ALU.is_equal))

            gl, el = LG[:, :, 0:NG], LG[:, :, NG:]
            top(gl, const("gdesc"), gm, goh, ge, NG)
            dve.tensor_tensor(gd, gl, gm.unsqueeze(2).broadcast_to([P, T, NG]), ALU.subtract).then_inc(rexp_in, 1)
            link(dve.tensor_scalar(pen, goh, -1.0, -NEG, ALU.add, ALU.mult))
            e4 = lambda a: a.rearrange("p t (g e) -> p t g e", g=NG)
            for t in range(T):
                j = dve.tensor_tensor(ml[:, t, :].rearrange("p (g e) -> p g e", g=NG),
                                      el[:, t, :].rearrange("p (g e) -> p g e", g=NG),
                                      pen[:, t, :].unsqueeze(2).broadcast_to([P, NG, EG]), ALU.add)
            link(j)
            top(ml, const("desc"), m1, oh1, t32, NE)
            link(dve.scalar_tensor_tensor(out=ml, in0=oh1, scalar=3 * NEG, in1=ml, op0=ALU.mult, op1=ALU.add))
            top(ml, const("desc"), m2, oh2, t32, NE)
            dve.tensor_tensor(mm1, m2, m1, ALU.subtract).then_inc(rexp_in, 1)
            dve.tensor_tensor(M32, oh1, oh2, ALU.add).then_inc(m_done, 1)
            mcv = Mc.rearrange("p (t n) -> p t n", n=NE)
            dve.wait_ge(m_done, 1)
            dve.memset(mcv[:, 0, :], 0.0)
            link(dve.tensor_copy(mcv[:, 1, :], M32[:, 0, :]))
            for t in range(1, T):
                j = dve.tensor_tensor(mcv[:, t + 1, :], mcv[:, t, :], M32[:, t, :], ALU.add)
                if t < T - 1:
                    link(j)
            j.then_inc(m_done, 1)
            link(dve.tensor_tensor(t32, M32, const("tok1").unsqueeze(2).broadcast_to([P, T, NE]), ALU.mult))
            dve.scalar_tensor_tensor(out=Wt, in0=oh2, scalar=float(S), in1=t32, op0=ALU.mult, op1=ALU.add)
            dve.wait_ge(rexp_done, 1)
            link(dve.tensor_reduce(gsum, gd, AX_X, ALU.add))
            link(dve.reciprocal(gp, gsum))
            dve.wait_ge(rexp_done, 2)
            link(dve.tensor_scalar(den, e2, 1.0, None, ALU.add))
            link(dve.reciprocal(den, den))
            link(dve.tensor_tensor(gate0, gp, den, ALU.mult))
            dve.tensor_tensor(gate1, gate0, e2, ALU.mult)
            name = ("rank",)
            wait_full(dve, name)
            dve.tensor_copy(rank, psum(name)[:, 0:T * NE].rearrange("p (t n) -> p t n", t=T))
            link(dve.tensor_reduce(cmax, psum(name)[:, T * NE:(T + 1) * NE], AX_X, ALU.max))
            link(dve.tensor_scalar(t8, const("thr"), cmax, None, ALU.is_lt))
            link(dve.tensor_reduce(npf, t8, AX_X, ALU.add))
            for one_ahead in (idx_full, idx_ready, xt_full, xt_ready, gate_full, sa_ready, up_full, hid_ready, ht_full, ht_ready, oyA, oyB):
                dve.sem_inc(one_ahead, 1)
            dve.tensor_copy(npi[:, :], npf).then_inc(route_done, 1)

            def one_hots(U, q):
                dve.wait_ge(idx_full, U + 1)
                ev = lambda a: a[:, :, bass.ds(q * 2, 2)] if not isinstance(q, int) else a[:, :, 2 * q:2 * q + 2]
                b = lambda a: ev(a).unsqueeze(3).broadcast_to([P, T, 2, CAP])
                it = const("iota").unsqueeze(1).broadcast_to([P, 2 * T, CAP]).rearrange("p (t e) n -> p t e n", t=T)
                link2(dve.tensor_tensor(sel[:, :, :, :], it, b(rank), ALU.is_equal), U * 3 + 1)
                dve.tensor_tensor(selw[:, :, :, :], sel[:, :, :, :], b(Wt), ALU.mult).then_inc(sel_ready, 1)

            def entries(U, q, s, turned):
                dve.wait_ge(idx_full, U + 2)
                link2(dve.tensor_scalar(emp[:, :], pb[0][:, 0:1], 0.0, 4.0 * 2 * S, ALU.is_equal, ALU.mult), U * 3 + 2)
                link2(dve.scalar_tensor_tensor(out=col(dsts, q), in0=pb[0][:, 0:1], scalar=-1.0, in1=emp[:, :],
                                               op0=ALU.add, op1=ALU.add), U * 3 + 3)
                dve.wait_ge(xt_full, turned + 1)
                dve.tensor_scalar(tok_i[s][:, :], col(dsts, q), (S - 1) | (4 * S), None, ALU.bitwise_and).then_inc(idx_ready, 1)

            def link2(ins, n):
                ins.then_inc(loop_self, 1)
                dve.wait_ge(loop_self, n)

            def col(a, q):
                return a[:, bass.ds(q, 1)] if not isinstance(q, int) else a[:, q:q + 1]

            def unit(U, q, s, use, nuse, ahead, more):
                if ahead:
                    entries(U + 3, q + 3, s, U + 1)
                dve.wait_ge(sa_ready, U + 2)
                dve.wait_ge(up_full, U + 2)
                dve.wait_ge(ht_full, U + 1)
                v = lambda a: a.rearrange("q (p c) -> q p c", c=2)
                dve.tensor_tensor(hid[:, :, :].rearrange("q c p -> q p c"), v(sa[:, :]), v(pb[7][:, 0:FF]),
                                  ALU.mult).then_inc(hid_ready, 1)
                if ahead > 1:
                    one_hots(U + 4, q + 4)
                dve.wait_ge(slots_freed, U + 4)
                dve.wait_ge(scattered[s], use * 16 + 16)
                dve.tensor_copy(dst_i[s][:, :], col(dsts, q))
                dve.tensor_copy(oy[s][:, 0:512], pb[5][:, :]).then_inc(oyA, 1)

            def stop(p):
                dve.tensor_scalar(rank, rank, -float(CAP), None, ALU.add).then_inc(next_rank, 1)
                dve.wait_ge(next_rank, p + 1)

            def start(p):
                for k in range(3):
                    one_hots(p * PAIRS + k, k)
                    entries(p * PAIRS + k, k, k, p * PAIRS)
                one_hots(p * PAIRS + 3, 3)

            passes(dve, unit, start, stop)

            def root(t):
                dve.wait_ge(ssf_done, 2 * t + 2)
                dve.reciprocal(rf[:, t:t + 1], ssf[:, t:t + 1]).then_inc(rf_done, 1)

            for t in range(T):
                dve.wait_ge(s_y[t], 16)
                link(dve.scalar_tensor_tensor(out=x2[:, t, :], in0=yt[t][:, 0, :], scalar=gate0[:, t:t + 1],
                                              in1=x2[:, t, :], op0=ALU.mult, op1=ALU.add))
                if t:
                    root(t - 1)
                dve.scalar_tensor_tensor(out=yt[t][:, 0, :], in0=yt[t][:, 1, :], scalar=gate1[:, t:t + 1],
                                         in1=x2[:, t, :], op0=ALU.mult, op1=ALU.add).then_inc(acc_done, 1)
            t = T - 1
            root(t)
            dve.wait_ge(rf_done, T)
            dve.wait_ge(s_fn, 16)
            dve.scalar_tensor_tensor(out=x2[:, t, :], in0=yt[t][:, 0, :], scalar=rf[:, t:t + 1], in1=fnb[:, :],
                                     op0=ALU.mult, op1=ALU.mult).then_inc(fin_done, 1)


_INS = ["x", "norm1_w", "w_in", "fox_forget_bias", "gdn_conv_w", "gdn_a_log", "gdn_dt_bias", "gdn_norm_w", "w_out",
        "norm2_w", "router_group_w", "router_group_b", "router_expert_w", "router_expert_b",
        "expert_w1", "expert_w3", "expert_w2", "final_norm_w"]
_OUTS = [((1, S, D), "float32")]


def kernel(**inputs):
    import numpy as _np
    import concourse.bacc as _bacc
    from concourse import mybir as _mybir
    from concourse.bass_utils import run_bass_kernel_spmd as _run

    nc = _bacc.Bacc("TRN2", target_bir_lowering=False, num_devices=1)
    table = constant_table()
    arrays = {"const_dram": table}
    args = [nc.dram_tensor("const_dram", table.shape, _mybir.dt.from_np(table.dtype), kind="ExternalInput").ap()]
    for name in _INS:
        a = _np.ascontiguousarray(inputs[name])
        arrays[f"in_{name}_dram"] = a
        args.append(nc.dram_tensor(f"in_{name}_dram", a.shape, _mybir.dt.from_np(a.dtype), kind="ExternalInput").ap())
    for i, (shape, dtype) in enumerate(_OUTS):
        dt = _mybir.dt.from_np(_np.dtype(dtype))
        args.append(nc.dram_tensor(f"out_{i}_dram", shape, dt, kind="ExternalOutput").ap())
    build(nc, *args)
    r = _run(nc, [arrays], core_ids=[0])
    return r.results[0]["out_0_dram"]
```
